# Optimizing a Trainium2 kernel written in Bass

```python
import math
import jax
import jax.numpy as jnp
from jax import lax
import numpy as np
import jax, jax.numpy as jnp

D_MODEL = 1024
BATCH = 1
SEQ = 512
DEPTH = 1

GRID_W = 64
CTX_LEN = 256
N_MIXERS = 4
N_MOD = 6
EPS = 1e-6
FFN_HIDDEN = -(-8 * D_MODEL // (3 * 256)) * 256

GLA_HEADS = 4
GLA_QK = D_MODEL // 2
GLA_VD = D_MODEL
GLA_DK = GLA_QK // GLA_HEADS
GLA_DV = GLA_VD // GLA_HEADS
GLA_RANK = 16
GLA_GATE_NORM = 16.0
GLA_CHUNK = 64
GLA_IN = 2 * GLA_QK + GLA_VD + D_MODEL + 2 * GLA_RANK

HY_SHORT = 3
HY_BANDS = 16
HY_EMB = 1 + 2 * HY_BANDS
HY_FILTER_DIM = 64
HY_DECAY_TARGET = 1e-2
HY_FAST_DECAY = 0.3
HY_SLOW_DECAY = 1.5

ML_HEADS = 4
ML_INNER = 2 * D_MODEL
ML_DH = ML_INNER // ML_HEADS
ML_BLOCK = 4
ML_NBLOCKS = ML_INNER // ML_BLOCK
ML_CONV = 3
ML_CHUNK = 64

S5_GROUP = 16
S5_GROUPS = D_MODEL // S5_GROUP
S5_STATE = 64
S5_DT_MIN = 1e-3
S5_DT_MAX = 1e-1

N_GLA = (DEPTH + 3) // N_MIXERS
N_HY = (DEPTH + 2) // N_MIXERS
N_ML = (DEPTH + 1) // N_MIXERS
N_S5 = DEPTH // N_MIXERS


def rms_norm(x, g):
    x = x.astype(jnp.float32)
    return x * lax.rsqrt(jnp.mean(x * x, axis=-1, keepdims=True) + EPS) * g.astype(jnp.float32)

def head_rms_norm(o, g):
    bsz, length, heads, d = o.shape
    o = o * lax.rsqrt(jnp.mean(o * o, axis=-1, keepdims=True) + EPS) * g
    return o.reshape(bsz, length, heads * d)

def multihead_layer_norm(o, g):
    bsz, length, heads, d = o.shape
    o = o - jnp.mean(o, axis=-1, keepdims=True)
    o = o * lax.rsqrt(jnp.mean(o * o, axis=-1, keepdims=True) + EPS)
    return o.reshape(bsz, length, heads * d) * g

def modulate(h, shift, scale):
    return h * (1.0 + scale) + shift

def flip_seq(t):
    return jnp.flip(t, axis=1)

def depthwise_conv_centred(x, w, b):
    k = w.shape[0]
    y = lax.conv_general_dilated(x, w.astype(x.dtype)[:, None, :], window_strides=(1,),
                                 padding=[(k // 2, k // 2)], dimension_numbers=('NWC', 'WIO', 'NWC'),
                                 feature_group_count=x.shape[-1])
    return y + b

def to_col_major(x, rows):
    bsz, length, ch = x.shape
    return x.reshape(bsz, rows, GRID_W, ch).transpose(0, 2, 1, 3).reshape(bsz, length, ch)

def from_col_major(x, rows):
    bsz, length, ch = x.shape
    return x.reshape(bsz, GRID_W, rows, ch).transpose(0, 2, 1, 3).reshape(bsz, length, ch)

def swiglu(h, w_in, w_out):
    gate, up = jnp.split(h @ w_in, 2, axis=-1)
    return (jax.nn.silu(gate) * up) @ w_out

def gla_chunk_scan(q, k, v, g, s0):
    bsz, length, heads, _ = q.shape
    dv = v.shape[-1]
    n_chunks = length // GLA_CHUNK

    def chunked(t):
        return t.reshape(bsz, n_chunks, GLA_CHUNK, heads, t.shape[-1]).swapaxes(0, 1)

    causal = jnp.tril(jnp.ones((GLA_CHUNK, GLA_CHUNK), dtype=bool))

    def step(s, inp):
        qc, kc, vc, gc = inp
        b = jnp.cumsum(gc, axis=1)
        b_end = b[:, -1]
        q_dec = qc * jnp.exp(b)
        scores = jnp.einsum('bihd,bjhd->bhij', q_dec, kc * jnp.exp(-b))
        scores = jnp.where(causal, scores, 0.0)
        o = jnp.einsum('bhij,bjhv->bihv', scores, vc) + jnp.einsum('bihd,bhdv->bihv', q_dec, s)
        k_end = kc * jnp.exp(b_end[:, None] - b)
        s = jnp.exp(b_end)[..., None] * s + jnp.einsum('bjhd,bjhv->bhdv', k_end, vc)
        return s, o

    s_end, o = lax.scan(step, s0, (chunked(q), chunked(k), chunked(v), chunked(g)))
    return o.swapaxes(0, 1).reshape(bsz, length, heads, dv), s_end

def gla_mixer(h_lat, h_ctx, w_in, w_gate, b_gate, norm_g, w_out):
    def project(h):
        bsz, length, _ = h.shape
        z = h.astype(jnp.float32) @ w_in
        q, k, v, r, glr = jnp.split(z, [GLA_QK, 2 * GLA_QK, 2 * GLA_QK + GLA_VD,
                                       2 * GLA_QK + GLA_VD + D_MODEL], axis=-1)
        glr = glr.reshape(bsz, length, 2, GLA_RANK)
        g = jax.nn.log_sigmoid(jnp.einsum('blzr,zrk->blzk', glr, w_gate) + b_gate) / GLA_GATE_NORM
        g = g.reshape(bsz, length, 2, GLA_HEADS, GLA_DK)
        q = q.reshape(bsz, length, GLA_HEADS, GLA_DK) * GLA_DK ** -0.5
        k = k.reshape(bsz, length, GLA_HEADS, GLA_DK)
        v = v.reshape(bsz, length, GLA_HEADS, GLA_DV)
        return q, k, v, r, g[:, :, 0], g[:, :, 1]

    def bidirectional(h, s_f0, s_b0):
        q, k, v, r, g_f, g_b = project(h)
        o_f, s_f = gla_chunk_scan(q, k, v, g_f, s_f0)
        o_b, s_b = gla_chunk_scan(flip_seq(q), flip_seq(k), flip_seq(v), flip_seq(g_b), s_b0)
        o = head_rms_norm(o_f + flip_seq(o_b), norm_g)
        return (o * jax.nn.silu(r)) @ w_out, s_f, s_b

    s0 = jnp.zeros((h_ctx.shape[0], GLA_HEADS, GLA_DK, GLA_DV), jnp.float32)
    y_ctx, s_f, s_b = bidirectional(h_ctx, s0, s0)
    y_lat, _, _ = bidirectional(h_lat, s_f, s_b)
    return y_lat, y_ctx

def hyena_filter(length, w1, b1, w2, b2, w3, freq):
    pos = jnp.arange(length, dtype=jnp.float32)
    t = pos / length
    bands = jnp.linspace(1e-4, HY_BANDS - 1, HY_BANDS, dtype=jnp.float32)
    ang = 2.0 * math.pi * t[:, None] * bands[None]
    feats = jnp.concatenate([t[:, None], jnp.cos(ang), -jnp.sin(ang)], axis=-1)
    z = jnp.sin(freq * (feats @ w1 + b1))
    z = jnp.sin(freq * (z @ w2 + b2))
    h = (z @ w3).reshape(length, 2, D_MODEL)
    log_target = math.log(HY_DECAY_TARGET)
    deltas = jnp.abs(jnp.linspace(log_target / HY_SLOW_DECAY, log_target / HY_FAST_DECAY, D_MODEL,
                                  dtype=jnp.float32))
    decay = jnp.exp(-t[:, None] * deltas)
    h = h * decay[:, None]
    return h[:, 0], h[:, 1]

def fft_long_conv(u, h_f, h_b, bias):
    length = u.shape[1]
    h2 = jnp.concatenate([h_f[:1] + h_b[:1], h_f[1:], jnp.zeros_like(h_f[:1]),
                          jnp.flip(h_b[1:], axis=0)], axis=0)
    u_hat = jnp.fft.rfft(u, n=2 * length, axis=1)
    h_hat = jnp.fft.rfft(h2, axis=0)
    y = jnp.fft.irfft(u_hat * h_hat[None], n=2 * length, axis=1)[:, :length]
    return y + u * bias

def hyena_mixer(h_lat, h_ctx, w_in, conv_w, conv_b, f_w1, f_b1, f_w2, f_b2, f_w3, f_freq, f_bias, w_out):
    def run(h):
        length = h.shape[1]
        u = depthwise_conv_centred(h.astype(jnp.float32) @ w_in, conv_w, conv_b)
        x0, x1, v = jnp.split(u, 3, axis=-1)
        h_f, h_b = hyena_filter(length, f_w1, f_b1, f_w2, f_b2, f_w3, f_freq)
        y = x0 * fft_long_conv(v * x1, h_f, h_b, f_bias)
        return y @ w_out

    return run(h_lat), run(h_ctx)

def mlstm_chunk_scan(q, k, v, i_pre, log_f, state):
    bsz, length, heads, _ = q.shape
    n_chunks = length // ML_CHUNK

    def chunked(t):
        return t.reshape((bsz, n_chunks, ML_CHUNK) + t.shape[2:]).swapaxes(0, 1)

    causal = jnp.tril(jnp.ones((ML_CHUNK, ML_CHUNK), dtype=bool))[None, :, :, None]

    def step(carry, inp):
        c_mat, n_vec, m = carry
        qc, kc, vc, ic, fc = inp
        b = jnp.cumsum(fc, axis=1)
        b_end = b[:, -1]
        d_intra = jnp.where(causal, b[:, :, None] - b[:, None] + ic[:, None], -jnp.inf)
        d_inter = b + m[:, None]
        m_tok = jnp.maximum(jnp.max(d_intra, axis=2), d_inter)
        w_inter = jnp.exp(d_inter - m_tok)
        s = jnp.einsum('bihd,bjhd->bijh', qc, kc) * jnp.exp(d_intra - m_tok[:, :, None])
        num = jnp.einsum('bijh,bjhv->bihv', s, vc) + w_inter[..., None] * jnp.einsum('bihd,bhdv->bihv', qc, c_mat)
        den = jnp.sum(s, axis=2) + w_inter * jnp.einsum('bihd,bhd->bih', qc, n_vec)
        h = num / jnp.maximum(jnp.abs(den), jnp.exp(-m_tok))[..., None]
        d_state = b_end[:, None] - b + ic
        m_new = jnp.maximum(b_end + m, jnp.max(d_state, axis=1))
        w_prev = jnp.exp(b_end + m - m_new)
        w_tok = jnp.exp(d_state - m_new[:, None])
        c_mat = w_prev[..., None, None] * c_mat + jnp.einsum('bjh,bjhd,bjhv->bhdv', w_tok, kc, vc)
        n_vec = w_prev[..., None] * n_vec + jnp.einsum('bjh,bjhd->bhd', w_tok, kc)
        return (c_mat, n_vec, m_new), h

    state, h = lax.scan(step, state, (chunked(q), chunked(k), chunked(v), chunked(i_pre), chunked(log_f)))
    return h.swapaxes(0, 1).reshape(bsz, length, heads, v.shape[-1]), state

def mlstm_mixer(h_lat, h_ctx, w_in, conv_w, conv_b, w_q, w_k, w_v, w_gates, b_gates, norm_g, skip, w_out):
    def project(h):
        bsz, length, _ = h.shape
        x_m, z = jnp.split(h.astype(jnp.float32) @ w_in, 2, axis=-1)
        x_c = jax.nn.silu(depthwise_conv_centred(x_m, conv_w, conv_b))

        def block_diag(t, w):
            t = t.reshape(bsz, length, ML_NBLOCKS, ML_BLOCK)
            return jnp.einsum('blnc,ncd->blnd', t, w).reshape(bsz, length, ML_INNER)

        q, k, v = block_diag(x_c, w_q), block_diag(x_c, w_k), block_diag(x_m, w_v)
        gates = jnp.einsum('blc,zcg->blzg', jnp.concatenate([q, k, v], axis=-1), w_gates) + b_gates
        i_pre = gates[..., :ML_HEADS]
        log_f = jax.nn.log_sigmoid(gates[..., ML_HEADS:])
        heads = lambda t: t.reshape(bsz, length, ML_HEADS, ML_DH)
        return heads(q), heads(k) * ML_DH ** -0.5, heads(v), i_pre, log_f, x_c, z

    def bidirectional(h, state_f, state_b):
        q, k, v, i_pre, log_f, x_c, z = project(h)
        h_f, state_f = mlstm_chunk_scan(q, k, v, i_pre[:, :, 0], log_f[:, :, 0], state_f)
        h_b, state_b = mlstm_chunk_scan(flip_seq(q), flip_seq(k), flip_seq(v), flip_seq(i_pre[:, :, 1]),
                                        flip_seq(log_f[:, :, 1]), state_b)
        h_n = multihead_layer_norm(h_f + flip_seq(h_b), norm_g)
        return ((h_n + skip * x_c) * jax.nn.silu(z)) @ w_out, state_f, state_b

    bsz = h_ctx.shape[0]
    state0 = (jnp.zeros((bsz, ML_HEADS, ML_DH, ML_DH), jnp.float32),
              jnp.zeros((bsz, ML_HEADS, ML_DH), jnp.float32),
              jnp.full((bsz, ML_HEADS), -jnp.inf, jnp.float32))
    y_ctx, st_f, st_b = bidirectional(h_ctx, state0, state0)
    y_lat, _, _ = bidirectional(h_lat, st_f, st_b)
    return y_lat, y_ctx

def _linear_recurrence_combine(left, right):
    a_l, b_l = left
    a_r, b_r = right
    return a_l * a_r, a_r * b_l + b_r

def s5_mixer(h_lat, h_ctx, lam_re, lam_im, log_dt, b_re, b_im, c_re, c_im, d_skip, w_glu):
    f32 = jnp.float32
    b_mat = lax.complex(b_re.astype(f32), b_im.astype(f32))
    c_mat = lax.complex(c_re.astype(f32), c_im.astype(f32))

    def discretise(direction):
        lam = lax.complex(lam_re[direction].astype(f32), lam_im[direction].astype(f32))
        lam_bar = jnp.exp(lam * jnp.exp(log_dt[direction].astype(f32))[:, None])
        return lam_bar, ((lam_bar - 1.0) / lam)[..., None] * b_mat

    disc = (discretise(0), discretise(1))

    def scan_readout(u_seq, lam_bar, b_bar, x0):
        bu = jnp.einsum('gpc,lbgc->lbgp', b_bar, u_seq)
        a = jnp.broadcast_to(lam_bar, (u_seq.shape[0], 1) + lam_bar.shape)
        a_cum, xs = lax.associative_scan(_linear_recurrence_combine, (a, bu), axis=0)
        xs = xs + a_cum * x0
        return jnp.real(jnp.einsum('gcp,lbgp->lbgc', c_mat, xs)), xs[-1]

    def bidirectional(h, x0_f, x0_b):
        bsz, length, _ = h.shape
        u = h.astype(f32)
        u_seq = u.swapaxes(0, 1).reshape(length, bsz, S5_GROUPS, S5_GROUP).astype(jnp.complex64)
        y_f, x_f = scan_readout(u_seq, disc[0][0], disc[0][1], x0_f)
        y_b, x_b = scan_readout(jnp.flip(u_seq, axis=0), disc[1][0], disc[1][1], x0_b)
        y = (y_f + jnp.flip(y_b, axis=0)).reshape(length, bsz, D_MODEL).swapaxes(0, 1) + d_skip * u
        val, gate = jnp.split(jax.nn.gelu(y) @ w_glu, 2, axis=-1)
        return val * jax.nn.sigmoid(gate), x_f, x_b

    x0 = jnp.zeros((h_ctx.shape[0], S5_GROUPS, S5_STATE), jnp.complex64)
    y_ctx, x_f, x_b = bidirectional(h_ctx, x0, x0)
    y_lat, _, _ = bidirectional(h_lat, x_f, x_b)
    return y_lat, y_ctx

def first_inputs(seed: int = 0) -> dict:
    key = jax.random.key(seed)
    keys = iter(jax.random.split(key, 96))
    f32 = jnp.float32

    def normal(shape, scale=1.0):
        return scale * jax.random.normal(next(keys), shape, f32)

    def gain(shape):
        return 1.0 + normal(shape, 0.02)

    D, F = D_MODEL, FFN_HIDDEN
    ml_b_i = normal((N_ML, 2, ML_HEADS), 0.1)
    ml_b_f = jnp.linspace(3.0, 6.0, ML_HEADS, dtype=f32) + normal((N_ML, 2, ML_HEADS), 0.1)
    lam_im_init = math.pi * jnp.arange(S5_STATE, dtype=f32)
    return {
        'x': normal((BATCH, SEQ, D)),
        'c': normal((BATCH, D)),
        'ctx': normal((BATCH, CTX_LEN, D)),
        'c_ctx': normal((D,)),
        'mod_w': normal((DEPTH, D, N_MOD * D), D ** -0.5),
        'mod_b': normal((DEPTH, N_MOD * D), 0.01),
        'norm_g': gain((DEPTH, 4, D)),
        'ffn_w_in': normal((DEPTH, D, 2 * F), D ** -0.5),
        'ffn_w_out': normal((DEPTH, F, D), F ** -0.5),
        'gla_w_in': normal((N_GLA, D, GLA_IN), D ** -0.5),
        'gla_w_gate': normal((N_GLA, 2, GLA_RANK, GLA_QK), GLA_RANK ** -0.5),
        'gla_b_gate': normal((N_GLA, 2, GLA_QK), 0.1),
        'gla_norm_g': gain((N_GLA, GLA_DV)),
        'gla_w_out': normal((N_GLA, GLA_VD, D), GLA_VD ** -0.5),
        'hy_w_in': normal((N_HY, D, 3 * D), D ** -0.5),
        'hy_conv_w': normal((N_HY, HY_SHORT, 3 * D), HY_SHORT ** -0.5),
        'hy_conv_b': normal((N_HY, 3 * D), 0.01),
        'hy_f_w1': normal((N_HY, HY_EMB, HY_FILTER_DIM), HY_EMB ** -0.5),
        'hy_f_b1': normal((N_HY, HY_FILTER_DIM), 0.1),
        'hy_f_w2': normal((N_HY, HY_FILTER_DIM, HY_FILTER_DIM), HY_FILTER_DIM ** -0.5),
        'hy_f_b2': normal((N_HY, HY_FILTER_DIM), 0.1),
        'hy_f_w3': normal((N_HY, HY_FILTER_DIM, 2 * D), HY_FILTER_DIM ** -0.5),
        'hy_f_freq': gain((N_HY, HY_FILTER_DIM)),
        'hy_f_bias': normal((N_HY, D), 0.1),
        'hy_w_out': normal((N_HY, D, D), D ** -0.5),
        'ml_w_in': normal((N_ML, D, 2 * ML_INNER), D ** -0.5),
        'ml_conv_w': normal((N_ML, ML_CONV, ML_INNER), ML_CONV ** -0.5),
        'ml_conv_b': normal((N_ML, ML_INNER), 0.01),
        'ml_w_q': normal((N_ML, ML_NBLOCKS, ML_BLOCK, ML_BLOCK), ML_BLOCK ** -0.5),
        'ml_w_k': normal((N_ML, ML_NBLOCKS, ML_BLOCK, ML_BLOCK), ML_BLOCK ** -0.5),
        'ml_w_v': normal((N_ML, ML_NBLOCKS, ML_BLOCK, ML_BLOCK), ML_BLOCK ** -0.5),
        'ml_w_gates': normal((N_ML, 2, 3 * ML_INNER, 2 * ML_HEADS), (3 * ML_INNER) ** -0.5),
        'ml_b_gates': jnp.concatenate([ml_b_i, ml_b_f], axis=-1),
        'ml_norm_g': gain((N_ML, ML_INNER)),
        'ml_skip': gain((N_ML, ML_INNER)),
        'ml_w_out': normal((N_ML, ML_INNER, D), ML_INNER ** -0.5),
        's5_lam_re': -0.5 + normal((N_S5, 2, S5_GROUPS, S5_STATE), 0.01),
        's5_lam_im': lam_im_init + normal((N_S5, 2, S5_GROUPS, S5_STATE), 0.01),
        's5_log_dt': jax.random.uniform(next(keys), (N_S5, 2, S5_GROUPS), f32,
                                        minval=math.log(S5_DT_MIN), maxval=math.log(S5_DT_MAX)),
        's5_b_re': normal((N_S5, S5_GROUPS, S5_STATE, S5_GROUP), (2 * S5_GROUP) ** -0.5),
        's5_b_im': normal((N_S5, S5_GROUPS, S5_STATE, S5_GROUP), (2 * S5_GROUP) ** -0.5),
        's5_c_re': normal((N_S5, S5_GROUPS, S5_GROUP, S5_STATE), (2 * S5_STATE) ** -0.5),
        's5_c_im': normal((N_S5, S5_GROUPS, S5_GROUP, S5_STATE), (2 * S5_STATE) ** -0.5),
        's5_d': normal((N_S5, D)),
        's5_w_glu': normal((N_S5, D, 2 * D), D ** -0.5),
    }

def first_block(x, c, ctx, c_ctx, mod_w, mod_b, norm_g, ffn_w_in, ffn_w_out,
              gla_w_in, gla_w_gate, gla_b_gate, gla_norm_g, gla_w_out,
              hy_w_in, hy_conv_w, hy_conv_b, hy_f_w1, hy_f_b1, hy_f_w2, hy_f_b2, hy_f_w3, hy_f_freq, hy_f_bias,
              hy_w_out,
              ml_w_in, ml_conv_w, ml_conv_b, ml_w_q, ml_w_k, ml_w_v, ml_w_gates, ml_b_gates, ml_norm_g, ml_skip,
              ml_w_out,
              s5_lam_re, s5_lam_im, s5_log_dt, s5_b_re, s5_b_im, s5_c_re, s5_c_im, s5_d, s5_w_glu):
    bsz = x.shape[0]
    rows = x.shape[1] // GRID_W
    lat, cx = x, ctx
    silu_c = jax.nn.silu(c.astype(jnp.float32))
    silu_cc = jax.nn.silu(c_ctx.astype(jnp.float32))
    for i in range(DEPTH):
        kind, j = i % N_MIXERS, i // N_MIXERS
        last = i == DEPTH - 1
        mod_l = (silu_c @ mod_w[i] + mod_b[i]).reshape(bsz, N_MOD, 1, D_MODEL)
        mod_c = (silu_cc @ mod_w[i] + mod_b[i]).reshape(N_MOD, 1, D_MODEL)
        h_lat = modulate(rms_norm(lat, norm_g[i, 0]), mod_l[:, 0], mod_l[:, 1])
        h_ctx = modulate(rms_norm(cx, norm_g[i, 0]), mod_c[0], mod_c[1])
        if kind == 0:
            y_lat, y_ctx = gla_mixer(h_lat, h_ctx, gla_w_in[j], gla_w_gate[j], gla_b_gate[j], gla_norm_g[j],
                                     gla_w_out[j])
        elif kind == 1:
            y_lat, y_ctx = hyena_mixer(h_lat, h_ctx, hy_w_in[j], hy_conv_w[j], hy_conv_b[j], hy_f_w1[j],
                                       hy_f_b1[j], hy_f_w2[j], hy_f_b2[j], hy_f_w3[j], hy_f_freq[j],
                                       hy_f_bias[j], hy_w_out[j])
        elif kind == 2:
            y_lat, y_ctx = mlstm_mixer(to_col_major(h_lat, rows), h_ctx, ml_w_in[j], ml_conv_w[j], ml_conv_b[j],
                                       ml_w_q[j], ml_w_k[j], ml_w_v[j], ml_w_gates[j], ml_b_gates[j],
                                       ml_norm_g[j], ml_skip[j], ml_w_out[j])
            y_lat = from_col_major(y_lat, rows)
        else:
            y_lat, y_ctx = s5_mixer(to_col_major(h_lat, rows), h_ctx, s5_lam_re[j], s5_lam_im[j], s5_log_dt[j],
                                    s5_b_re[j], s5_b_im[j], s5_c_re[j], s5_c_im[j], s5_d[j], s5_w_glu[j])
            y_lat = from_col_major(y_lat, rows)
        lat = lat + (mod_l[:, 2] * rms_norm(y_lat, norm_g[i, 1])).astype(lat.dtype)
        h = modulate(rms_norm(lat, norm_g[i, 2]), mod_l[:, 3], mod_l[:, 4])
        lat = lat + (mod_l[:, 5] * rms_norm(swiglu(h, ffn_w_in[i], ffn_w_out[i]), norm_g[i, 3])).astype(lat.dtype)
        if not last:
            cx = cx + (mod_c[2] * rms_norm(y_ctx, norm_g[i, 1])).astype(cx.dtype)
            hc = modulate(rms_norm(cx, norm_g[i, 2]), mod_c[3], mod_c[4])
            cx = cx + (mod_c[5] * rms_norm(swiglu(hc, ffn_w_in[i], ffn_w_out[i]), norm_g[i, 3])).astype(cx.dtype)
    return lat


MIX_WIDTH = D_MODEL
POOL_WIDTH = MIX_WIDTH // 2
POOL_WINDOWS = (2, 4, 8, 16)
N_POOL_GROUPS = len(POOL_WINDOWS)
POOL_GROUP_DIM = POOL_WIDTH // N_POOL_GROUPS
RET_WIDTH = MIX_WIDTH - POOL_WIDTH
RET_HEADS = 4
RET_HEAD_DIM = RET_WIDTH // RET_HEADS
RET_CHUNK = 128
ROPE_BASE = 10000.0
IN_WIDTH = POOL_WIDTH + 4 * RET_WIDTH
D_FF = 2816


def rmsnorm(x, gain):
    xf = x.astype(jnp.float32)
    y = xf * lax.rsqrt(jnp.mean(xf * xf, axis=-1, keepdims=True) + EPS)
    return (y * gain.astype(jnp.float32)).astype(x.dtype)

def swiglu_2(x, w1, w3, w2):
    return (jax.nn.silu(x @ w1) * (x @ w3)) @ w2

def pool_mixer(u, pool_w, pool_scale):
    B, S, _ = u.shape
    ug = u.reshape(B, S, N_POOL_GROUPS, POOL_GROUP_DIM)
    t = jnp.arange(1, S + 1, dtype=jnp.float32)
    outs = []
    for gi, w in enumerate(POOL_WINDOWS):
        xg = ug[:, :, gi, :]
        cs = lax.cumsum(xg.astype(jnp.float32), axis=1)
        csp = jnp.pad(cs, ((0, 0), (w, 0), (0, 0)))
        window_sum = csp[:, w:, :] - csp[:, :S, :]
        count = jnp.minimum(t, float(w))[None, :, None]
        pooled = (window_sum / count).astype(u.dtype) - xg
        outs.append(pooled @ pool_w[gi])
    return jnp.concatenate(outs, axis=-1) * pool_scale

def rope_tables(S, D):
    inv_freq = 1.0 / (ROPE_BASE ** (jnp.arange(0, D, 2, dtype=jnp.float32) / D))
    ang = jnp.arange(S, dtype=jnp.float32)[:, None] * inv_freq[None, :]
    return jnp.cos(ang), jnp.sin(ang)

def apply_rope(t, cos, sin):
    t1, t2 = jnp.split(t, 2, axis=-1)
    c = cos[None, :, None, :]
    s = sin[None, :, None, :]
    return jnp.concatenate([t1 * c - t2 * s, t1 * s + t2 * c], axis=-1)

def retention(q, k, v, g, gain):
    B, S, _ = q.shape
    H, D, C = RET_HEADS, RET_HEAD_DIM, RET_CHUNK
    NC = S // C
    dt = q.dtype

    def heads(t):
        return t.astype(jnp.float32).reshape(B, S, H, D)

    cos, sin = rope_tables(S, D)
    qh = apply_rope(heads(q), cos, sin)
    kh = apply_rope(heads(k), cos, sin) * (D ** -0.5)
    vh = heads(v)

    def chunks(t):
        return t.reshape(B, NC, C, H, D).transpose(0, 3, 1, 2, 4)

    qc, kc, vc = chunks(qh), chunks(kh), chunks(vh)

    log_gamma = jnp.log1p(-jnp.exp2(-5.0 - jnp.arange(H, dtype=jnp.float32)))
    pos = jnp.arange(C, dtype=jnp.float32)
    rel = pos[:, None] - pos[None, :]
    intra_decay = jnp.where(rel[None] >= 0,
                            jnp.exp(log_gamma[:, None, None] * jnp.maximum(rel, 0.0)[None]),
                            0.0)

    scores = jnp.einsum('bhncd,bhnsd->bhncs', qc, kc) * intra_decay[None, :, None]
    o_intra = jnp.einsum('bhncs,bhnse->bhnce', scores, vc)

    k_tail = jnp.exp(log_gamma[:, None] * (C - 1 - pos)[None, :])
    kv = jnp.einsum('bhnsd,bhnse->nbhde', kc * k_tail[None, :, None, :, None], vc)
    chunk_decay = jnp.exp(log_gamma * C)[None, :, None, None]

    def step(R, kv_n):
        return chunk_decay * R + kv_n, R

    _, R_prev = lax.scan(step, jnp.zeros((B, H, D, D), jnp.float32), kv)

    q_head = jnp.exp(log_gamma[:, None] * (pos + 1.0)[None, :])
    o_cross = jnp.einsum('bhncd,nbhde->bhnce', qc * q_head[None, :, None, :, None], R_prev)

    o = (o_intra + o_cross).transpose(0, 2, 3, 1, 4).reshape(B, S, H, D)
    o = o * lax.rsqrt(jnp.mean(o * o, axis=-1, keepdims=True) + EPS)
    o = o.reshape(B, S, H * D) * gain.astype(jnp.float32)
    return (jax.nn.silu(g.astype(jnp.float32)) * o).astype(dt)

def second_inputs(seed: int = 0) -> dict:
    key = jax.random.key(seed)
    ks = jax.random.split(key, 20)
    f32 = jnp.float32

    def nrm(k, shape, fan_in):
        return jax.random.normal(k, shape, f32) * (fan_in ** -0.5)

    def gain(k, shape):
        return 1.0 + 0.05 * jax.random.normal(k, shape, f32)

    L = DEPTH
    return {
        "x": jax.random.normal(ks[0], (BATCH, SEQ, D_MODEL), f32),
        "ffn1_norm": gain(ks[1], (L, D_MODEL)),
        "ffn1_w1": nrm(ks[2], (L, D_MODEL, D_FF), D_MODEL),
        "ffn1_w3": nrm(ks[3], (L, D_MODEL, D_FF), D_MODEL),
        "ffn1_w2": nrm(ks[4], (L, D_FF, D_MODEL), D_FF),
        "mix_norm": gain(ks[5], (L, D_MODEL)),
        "w_in": nrm(ks[6], (L, D_MODEL, IN_WIDTH), D_MODEL),
        "pool_w": nrm(ks[7], (L, N_POOL_GROUPS, POOL_GROUP_DIM, POOL_GROUP_DIM), POOL_GROUP_DIM),
        "pool_scale": gain(ks[8], (L, POOL_WIDTH)),
        "ret_norm": gain(ks[9], (L, RET_WIDTH)),
        "w_out": nrm(ks[10], (L, MIX_WIDTH, D_MODEL), MIX_WIDTH),
        "ffn2_norm": gain(ks[11], (L, D_MODEL)),
        "ffn2_w1": nrm(ks[12], (L, D_MODEL, D_FF), D_MODEL),
        "ffn2_w3": nrm(ks[13], (L, D_MODEL, D_FF), D_MODEL),
        "ffn2_w2": nrm(ks[14], (L, D_FF, D_MODEL), D_FF),
        "final_norm": gain(ks[15], (D_MODEL,)),
    }

def second_block(x, ffn1_norm, ffn1_w1, ffn1_w3, ffn1_w2, mix_norm, w_in, pool_w, pool_scale,
              ret_norm, w_out, ffn2_norm, ffn2_w1, ffn2_w3, ffn2_w2, final_norm):
    h = x
    for l in range(DEPTH):
        h = h + 0.5 * swiglu_2(rmsnorm(h, ffn1_norm[l]), ffn1_w1[l], ffn1_w3[l], ffn1_w2[l])

        u = rmsnorm(h, mix_norm[l])
        proj = u @ w_in[l]
        u_pool, q, k, v, g = jnp.split(
            proj, [POOL_WIDTH, POOL_WIDTH + RET_WIDTH, POOL_WIDTH + 2 * RET_WIDTH,
                   POOL_WIDTH + 3 * RET_WIDTH], axis=-1)
        a = pool_mixer(u_pool, pool_w[l], pool_scale[l])
        b = retention(q, k, v, g, ret_norm[l])
        h = h + jnp.concatenate([a, b], axis=-1) @ w_out[l]

        h = h + 0.5 * swiglu_2(rmsnorm(h, ffn2_norm[l]), ffn2_w1[l], ffn2_w3[l], ffn2_w2[l])
    return rmsnorm(h, final_norm)


def setup_inputs(seed=0):
    out = dict(first_inputs(seed))
    for name, value in second_inputs(seed + 1).items():
        if name != "x":
            out[name + "_2"] = value
    return out


def reference(
    x, c, ctx, c_ctx, mod_w, mod_b, norm_g, ffn_w_in, ffn_w_out, gla_w_in, gla_w_gate,
    gla_b_gate, gla_norm_g, gla_w_out, hy_w_in, hy_conv_w, hy_conv_b, hy_f_w1, hy_f_b1, hy_f_w2,
    hy_f_b2, hy_f_w3, hy_f_freq, hy_f_bias, hy_w_out, ml_w_in, ml_conv_w, ml_conv_b, ml_w_q,
    ml_w_k, ml_w_v, ml_w_gates, ml_b_gates, ml_norm_g, ml_skip, ml_w_out, s5_lam_re, s5_lam_im,
    s5_log_dt, s5_b_re, s5_b_im, s5_c_re, s5_c_im, s5_d, s5_w_glu, ffn1_norm_2, ffn1_w1_2,
    ffn1_w3_2, ffn1_w2_2, mix_norm_2, w_in_2, pool_w_2, pool_scale_2, ret_norm_2, w_out_2,
    ffn2_norm_2, ffn2_w1_2, ffn2_w3_2, ffn2_w2_2, final_norm_2,
):
    x = first_block(
        x, c, ctx, c_ctx, mod_w, mod_b, norm_g, ffn_w_in, ffn_w_out, gla_w_in, gla_w_gate,
        gla_b_gate, gla_norm_g, gla_w_out, hy_w_in, hy_conv_w, hy_conv_b, hy_f_w1, hy_f_b1,
        hy_f_w2, hy_f_b2, hy_f_w3, hy_f_freq, hy_f_bias, hy_w_out, ml_w_in, ml_conv_w,
        ml_conv_b, ml_w_q, ml_w_k, ml_w_v, ml_w_gates, ml_b_gates, ml_norm_g, ml_skip, ml_w_out,
        s5_lam_re, s5_lam_im, s5_log_dt, s5_b_re, s5_b_im, s5_c_re, s5_c_im, s5_d, s5_w_glu,
    )
    return second_block(
        x, ffn1_norm_2, ffn1_w1_2, ffn1_w3_2, ffn1_w2_2, mix_norm_2, w_in_2, pool_w_2,
        pool_scale_2, ret_norm_2, w_out_2, ffn2_norm_2, ffn2_w1_2, ffn2_w3_2, ffn2_w2_2,
        final_norm_2,
    )


_drawn_inputs = setup_inputs


def setup_inputs(seed=0):
    import zlib

    import numpy as np

    out = dict(_drawn_inputs(seed))
    spreads = {}
    factors = {'gla_norm_g': 5.065,
     'ffn1_norm_2': 3.046,
     'pool_scale_2': 2.761,
     'ret_norm_2': 4.333,
     'ffn2_norm_2': 3.824}
    for name, (base, spread) in spreads.items():
        noise = np.random.default_rng([zlib.crc32(name.encode()), seed]).standard_normal(out[name].shape)
        drawn = base * np.exp(spread * noise) if base else spread * noise
        out[name] = jnp.asarray(drawn.astype(out[name].dtype))
    for name, factor in factors.items():
        out[name] = (out[name] * factor).astype(out[name].dtype)
    return out
```

```python
from contextlib import ExitStack, contextmanager

import numpy as np

import concourse.bass as bass
from concourse import mybir

ALU = mybir.AluOpType
ACT = mybir.ActivationFunctionType
F32 = mybir.dt.float32
F32R = mybir.dt.float32r
U32 = mybir.dt.uint32

P = 128
D = 1024
T = 512
TC = 256
KD = D // P
F = 2816
KF = F // P
UC = 256
CPU = UC // P
UNIT = KD * UC
EPS = 1e-6

HG = 4
DK, DV = 128, 256
RANK = 16
CHUNK = 64
NCH = T // CHUNK
GATE_NORM = 16.0
PAIRS = T // P

HR = 4
RCH = T // P
WINDOWS = (2, 4, 8, 16)

OUT_PARTS = ((0, 6), (6, 12), (12, 17), (17, 22))

COLS = {}
_n = 0
for _name, _w in (("c", 2 * KD), ("mod_b", 6 * KD), ("norm_g", 4 * KD), ("b_gate", 2 * HG), ("gla_g", 2),
                  ("ffn1_g", KD), ("mix_g", KD), ("pool_scale", 4), ("ret_g", 4), ("ffn2_g", KD),
                  ("final_g", KD)):
    COLS[_name] = _n
    _n += _w
NCOLS = _n


GATE_ORDER = [d * HG + h for h in range(HG) for d in range(2)]


class Counts:

    def __init__(self, eng):
        self.eng, self.n, self.i, self.per = eng, {}, None, {}

    def expect(self, sem, more=1):
        self.n[sem] = self.n.get(sem, 0) + more

    def has(self, sem):
        return self.n.get(sem, 0) > 0

    def now(self, sem, back=0):
        value = self.n.get(sem, 0) - back
        assert value > 0, str(sem)
        if self.i is not None and self.per.get(sem, 0):
            value = self.i * self.per[sem] + value
        return value

    def next(self, sem, more=1):
        self.expect(sem, more)
        return self.now(sem)

    def upto(self, sem, value):
        self.n[sem] = max(value, self.n.get(sem, 0))
        return self.now(sem)

    @contextmanager
    def loop(self, turns, per):
        start = dict(self.n)
        with self.eng.Fori(0, turns) as i:
            self.i, self.per = i, per
            yield i
            self.i = None
        for sem, n in self.n.items():
            grown = n - start.get(sem, 0)
            assert grown == per.get(sem, 0), (str(sem), grown, per.get(sem, 0))
            self.n[sem] = start.get(sem, 0) + turns * grown
        self.per = {}


def build(nc, a):
    with ExitStack() as ctx:
        sems = {}

        def sem(name):
            if name not in sems:
                sems[name] = ctx.enter_context(nc.semaphore(name))
            return sems[name]

        top = [256]

        def place(name, shape, dtype=F32, at=None):
            size = int(np.prod(shape[1:])) * 4
            if at is None:
                at = top[0]
                top[0] += (size + 31) // 32 * 32
            assert at + size <= nc.sbuf_usable_end, (name, at, size)
            return nc.alloc_sbuf_tensor_at(name, shape, dtype, offset=at)

        def here(size):
            at = top[0]
            top[0] += size
            return at

        KB = 1024
        base = nc.sbuf_base
        top[0] = (base + 31) // 32 * 32
        w_raw = [place(f"w_raw{s}", [P, KD, UC]) for s in range(2)]
        w_hi = [place(f"w_hi{s}", [P, KD, UC], F32R) for s in range(2)]
        w_lo = [place(f"w_lo{s}", [P, KD, UC], F32R) for s in range(2)]
        mod_raw = place("mod_raw", [P, KD, P])
        xT = place("xT", [P, KD, T])
        act_at = here(32 * KB)
        a_hi = place("a_hi", [P, KD, T], F32R, act_at)
        a_lo = place("a_lo", [P, KD, T], F32R, act_at + 16 * KB)
        y_ffn = place("y_ffn", [P, KD, T], F32, act_at)
        big = here(88 * KB)
        g_hi = place("g_hi", [P, KF, T], F32R, big)
        g_lo = place("g_lo", [P, KF, T], F32R, big + 44 * KB)
        kT = place("kT", [P, HG, T], F32, big)
        cT = place("cT", [P, KD, TC], F32, big)
        kcT = place("kcT", [P, HG, TC], F32, big + 8 * KB)
        vc = [place(f"vc{s}", [P, 2, DV], F32, big + (12 + 2 * s) * KB) for s in range(2)]
        qT = place("qT", [P, HG, T], F32, big + 16 * KB)
        v = place("v", [P, PAIRS, D], F32, big + 24 * KB)
        y_gla = place("y_gla", [P, KD, T], F32, big + 24 * KB)
        wr_hi = place("wr_hi", [P, KD, P], F32R, big + 24 * KB)
        wr_lo = place("wr_lo", [P, KD, P], F32R, big + 28 * KB)
        wg_hi = place("wg_hi", [P, D], F32R, big + 32 * KB)
        small_raw = place("small_raw", [P, 2, D], F32, big + 48 * KB)
        wg = place("wg", [P, D], F32R, big + 36 * KB)
        G = place("G", [P, 2 * HG, T], F32, big + 40 * KB)
        ke_tok = [place(f"ke_tok{n}", [P, PAIRS, DK], F32, big + (40 + 2 * n) * KB) for n in range(8)]
        o_sq = [place(f"o_sq{n}", [P, T], F32, big + (40 + 2 * n) * KB) for n in range(8)]
        Gc = place("Gc", [P, 2 * HG, TC], F32, big + 56 * KB)
        st = [place(f"st{d}", [P, PAIRS, P], F32, big + (56 + 2 * d) * KB) for d in range(2)]
        state = [place(f"state{s}", [P, DV], F32, big + (60 + s) * KB) for s in range(4)]
        hc_hi = place("hc_hi", [P, KD, TC], F32R, big + 64 * KB)
        hc_lo = place("hc_lo", [P, KD, TC], F32R, big + 72 * KB)
        sr = place("sr", [P, KD, T], F32, big + 64 * KB)
        cst = place("cst", [P, 2 * HG, DV], F32, big + 80 * KB)
        glr = place("glr", [P, T + TC], F32R, big + 82 * KB)
        m_hi = place("m_hi", [P, KD, T], F32R, big)
        m_lo = place("m_lo", [P, KD, T], F32R, big + 16 * KB)
        qr = place("qr", [P, HR, T], F32, big + 32 * KB)
        kr = place("kr", [P, HR, T], F32, big + 40 * KB)
        vr = place("vr", [P, RCH, HR * P], F32, big + 48 * KB)
        gr = place("gr", [P, HR, T], F32, big + 56 * KB)
        trig = place("trig", [P, 2, T], F32, big + 64 * KB)
        decay = place("decay", [P, 3, HR, P], F32, big + 68 * KB)
        pool_w = place("pool_w", [P, 4, P], F32, big + 74 * KB)
        pool_n = place("pool_n", [P, 4, 16], F32, big + 76 * KB)
        pool_u = [place(f"pool_u{s}", [P, T], F32, big + (77 + 2 * s) * KB) for s in range(4)]
        rstate = place("rstate", [P, 2, 3, P], F32, big + 85 * KB)
        ret_kt = [place(f"ret_kt{s}", [P, T], F32, big + (77 + 2 * s) * KB) for s in range(2)]
        ret_diag = place("ret_diag", [P, T], F32, big + 81 * KB)
        ret_sq_t = place("ret_sq_t", [P, T], F32, big + 83 * KB)
        tmp = [place(f"tmp{s}", [P, T]) for s in range(4)]
        col4 = place("col4", [P, 16])
        root4 = place("root4", [P, 16])
        power = place("power", [P, 16])
        dec_k = [[place(f"{x}0", [P, T]) for x in ("qd", "kd", "ke")],
                 [place(f"{x}1", [P, T], F32, big + (8 + 2 * j) * KB) for j, x in enumerate(("qd", "kd", "ke"))]]
        ret_q, ret_k, ret_p = ([tmp[j], dec_k[0][i]] for i, j in enumerate((0, 1, 3)))
        ends = [place(f"ends{s}", [P, NCH]) for s in range(2)]
        cols = place("cols", [P, NCOLS])
        mod = place("mod", [P, 6 * KD, 2])
        gain = place("gain", [P, 5, KD])
        end16 = place("end16", [P, HG])
        sc = place("sc", [P, KD, 2])
        ident = place("ident", [P, P])
        ones = place("ones", [P, P])
        masks = place("masks", [P, 2, P])
        reset = place("reset", [P, T])
        one = place("one", [P, 1])

        bank = [ctx.enter_context(nc.psum_tensor(f"bank{b}", [P, T], F32)) for b in range(8)]

        ready = [sem(f"bank_ready{b}") for b in range(8)]
        free = [sem(f"bank_free{b}") for b in range(8)]
        raw_loaded = [sem(f"raw_loaded{s}") for s in range(2)]
        hi_done = [sem(f"weight_hi_done{s}") for s in range(2)]
        lo_done = [sem(f"weight_lo_done{s}") for s in range(2)]
        unit_used = [sem(f"unit_used{s}") for s in range(2)]
        mod_loaded, mod_used = sem("mod_tile_loaded"), sem("mod_tile_used")
        cols_loaded, x_loaded, c_loaded = sem("cols_loaded"), sem("x_loaded"), sem("context_loaded")
        rank_loaded, consts_loaded = sem("rank_weights_loaded"), sem("constants_loaded")
        mix_loaded, stored = sem("mix_constants_loaded"), sem("out_stored")
        const_set, silu_c_done, mods_done = sem("constants_set"), sem("silu_c_done"), sem("modulation_done")
        sq_streamed, sq_stream_used = sem("square_streamed"), sem("square_stream_used")
        var_done, root_done, diag_done = sem("mean_square_done"), sem("inverse_root_done"), sem("diagonal_done")
        y_squared, sum_step = sem("y_squared"), sem("square_sum_step")
        y_scaled, x_added = sem("y_scaled"), sem("x_added")
        scaled, norm_hi, norm_lo = sem("norm_scaled"), sem("norm_hi_done"), sem("norm_lo_done")
        silu_done, prod_done, gate_hi, gated = sem("silu_done"), sem("product_done"), sem("gated_hi_done"), sem("gated_done")
        chunk_done, sq_done = sem("chunk_done"), sem("chunk_squared")
        pair_done = [sem(f"column_pair_done{j}") for j in range(2)]
        rank_hi, rank_lo, glr_hi = sem("rank_hi_done"), sem("rank_lo_done"), sem("glr_hi_done")
        act_step, dve_step = sem("act_step"), sem("dve_step")
        abs_done, ln_done, log_gate, scanned = sem("abs_done"), sem("ln_done"), sem("log_gate_done"), sem("scan_done")
        ctx_exp, ctx_key, ctx_tok = sem("context_exp_done"), sem("context_key_done"), sem("context_key_turned")
        rest_done, exp_done, dec_done, ke_done = sem("rest_decay_done"), sem("exp_done"), sem("decayed_done"), sem("end_key_turned")
        silu_r, r_copied = sem("silu_r_done"), sem("r_copied")
        st_done, state_done = sem("masked_scores_done"), sem("state_done")
        state_used, forward_used = sem("state_used"), sem("forward_scan_used")
        o_squared, o_summed = sem("o_squared"), sem("o_squares_summed")
        u_copied, pooled, mixed_hi, mixed_lo = sem("pool_input_copied"), sem("pooled_done"), sem("mixed_hi_done"), sem("mixed_lo_done")
        roped, ret_in, ret_scores = sem("rotated"), sem("retention_operand_done"), sem("retention_scores_done")
        ktok_done, r_state, v_copied = sem("key_turned"), sem("retention_state_done"), sem("v_copied")
        gate_silu, ret_sq = sem("gate_silu_done"), sem("retention_squared")
        sums_ready, roots_ready = sem("square_sums_ready"), sem("roots_spread")
        glr_ready, gates_ready = sem("low_rank_ready"), sem("gates_ready")
        ctx_keys_ready, ctx_state_ready = sem("context_keys_ready"), sem("context_state_ready")
        scan_keys, scan_scores, kv_ready = sem("scan_keys_ready"), sem("scan_scores_ready"), sem("kv_ready")
        o_ready = sem("o_ready")
        silu_in, up_ready, out_ready = sem("ffn_gate_ready"), sem("ffn_up_ready"), sem("ffn_out_ready")
        rope_ready, pool_mapped, mix_out = sem("rotation_input_ready"), sem("pool_mapped"), sem("mix_out_ready")
        ret_keys, ret_scored, ret_kv, ret_o_ready = (sem("retention_keys_ready"), sem("retention_scores_ready"),
                                                     sem("retention_kv_ready"), sem("retention_out_ready"))
        log_min, ctx_end, ret_o = sem("log_gate_min_done"), sem("context_end_done"), sem("retention_out_gated")
        half_summed, out_done = sem("half_pair_summed"), sem("out_chunk_done")

        def col(name, j=0, n=1):
            return cols[:, COLS[name] + j:COLS[name] + j + n]

        def flat(t):
            return t[:].rearrange("p a b -> p (a b)")

        def spread(ap, axis, shape):
            return ap.unsqueeze(axis).to_broadcast(shape)

        def head_of(n):
            return n // 2, n % 2, (n % 2) * HG + n // 2

        def ends_at(d):
            return CHUNK - 1 if d == 0 else 0

        block = ctx.enter_context(nc.Block())

        @block.sync
        def _(sp):
            cnt = Counts(sp)
            sp.dma_start(cols[:], a["cols"]).then_inc(cols_loaded, 16)
            sp.dma_start(xT[:], a["x_fm"]).then_inc(x_loaded, 16)
            sp.dma_start(cT[:], a["ctx_fm"]).then_inc(c_loaded, 16)
            sp.dma_start(ident[:], a["ident"]).then_inc(consts_loaded, 16)

            def load(s, src, width=UNIT):
                sp.wait_ge(hi_done[s], cnt.next(hi_done[s]))
                sp.wait_ge(lo_done[s], cnt.next(lo_done[s]))
                sp.dma_start(flat(w_raw[s])[:, 0:width], src).then_inc(raw_loaded[s], 16)

            def load_tile(j):
                if j:
                    sp.wait_ge(mod_used, cnt.next(mod_used))
                sp.dma_start(flat(mod_raw), a["mod25"][j]).then_inc(mod_loaded, 16)

            for n in range(10):
                s = n % 2
                if n >= 2:
                    sp.wait_ge(unit_used[s], cnt.next(unit_used[s]))
                src = a["mod01"][n] if n < 8 else a["gla_in"][n - 8]
                sp.dma_start(flat(w_raw[s]), src).then_inc(raw_loaded[s], 16)
                if n == 3:
                    sp.dma_start(small_raw[:], a["rank_w"]).then_inc(rank_loaded, 16)
                if n == 5:
                    sp.dma_start(masks[:], a["masks"]).then_inc(consts_loaded, 16)
                    sp.dma_start(reset[:], a["reset"]).then_inc(consts_loaded, 16)
            load_tile(0)
            for n in range(16):
                if n + 2 < 16:
                    m = n + 2
                    load(m % 2, a["gla_in"][m] if m < 12 else a["gla_out"][m - 12])
                load_tile(2 * n + 1)
                if n < 15:
                    load_tile(2 * n + 2)

            def ffn(w_in, w_out):
                both = {x[s]: 1 for x in (hi_done, lo_done) for s in range(2)}
                with cnt.loop(F // UC, both) as i:
                    for s in range(2):
                        load(s, w_in[bass.ds(i * 2 + s, 1)].rearrange("u p w -> p (u w)"))
                with cnt.loop(D // UC, {x: 2 for x in both}) as i:
                    for j, (k0, k1) in enumerate(OUT_PARTS):
                        src = w_out[bass.ds(i, 1), :, k0 * UC:k1 * UC].rearrange("u p w -> p (u w)")
                        load(j % 2, src, (k1 - k0) * UC)

            ffn(a["ffn0_in"], a["ffn0_out"])
            ffn(a["ffn1_in"], a["ffn1_out"])
            for n in range(10):
                load(n % 2, a["mix_in"][n])
                if n == 1:
                    sp.wait_ge(chunk_done, 2 * KD)
                    for dst, name in ((trig, "trig"), (decay, "decay"), (pool_w, "pool_w"), (pool_n, "pool_n")):
                        sp.dma_start(dst[:], a[name]).then_inc(mix_loaded, 16)
            for n in range(4):
                load(n % 2, a["mix_out"][n])
            ffn(a["ffn2_in"], a["ffn2_out"])
            for m in range(KD):
                sp.wait_ge(out_done, m + 1)
                sp.dma_start(a["out"][:, m], y_ffn[:, m]).then_inc(stored, 16)
            sp.wait_ge(stored, 16 * KD)

        @block.gpsimd
        def _(pool):
            cnt = Counts(pool)
            pool.wait_ge(const_set, 3)

            def inverse_root(n):
                pool.wait_ge(var_done, cnt.next(var_done))
                nc.gpsimd.tensor_tensor(root4[:, 0:n], col4[:, 0:n], power[:, 0:n], ALU.pow).then_inc(root_done, 1)

            for n in (4, 2, 16, 4, 4, 4, 4, 4, 4, 4, 4, 4, 4, 4):
                inverse_root(n)

        @block.tensor
        def _(pe):
            cnt = Counts(pe)
            filled = [False] * 8

            def take(b):
                if filled[b]:
                    pe.wait_ge(free[b], cnt.next(free[b]))
                filled[b] = True

            def mm(out, lhs, rhs, first, last):
                return pe.matmul(out, lhs, rhs, start=first, stop=last, skip_group_check=True)

            def mm3(out, lhs, rhs, first, last):
                mm(out, lhs[0], rhs[0], first, False)
                mm(out, lhs[0], rhs[1], False, False)
                return mm(out, lhs[1], rhs[0], False, last)

            def weights(s, k, c):
                return w_hi[s][:, k, c * P:(c + 1) * P], w_lo[s][:, k, c * P:(c + 1) * P]

            def unit(s, banks, acts, by_chunk=None, says=None):
                pe.wait_ge(lo_done[s], cnt.next(lo_done[s]))
                for b in banks:
                    take(b)
                order = [(k, c) for k in range(KD) for c in range(CPU)] if by_chunk else \
                        [(k, c) for c in range(CPU) for k in range(KD)]
                for k, c in order:
                    if by_chunk is norm_lo and c == 0:
                        pe.wait_ge(norm_lo, cnt.next(norm_lo))
                    if by_chunk is mixed_lo and c == 0 and k >= KD - HR:
                        pe.wait_ge(mixed_lo, cnt.upto(mixed_lo, k + 1))
                    m = mm3(bank[banks[c]][:], weights(s, k, c), (acts[0][:, k], acts[1][:, k]), k == 0, k == KD - 1)
                    if k == KD - 1:
                        m.then_inc(says or ready[banks[c]], 1)

            def token_sums(b, col0, src, n, first, last):
                for j in range(n // P):
                    m = mm(bank[b][:, col0 + j:col0 + j + 1], src[:, j * P:(j + 1) * P], ones[:, 0:1], first and j == 0, last)
                return m

            def broadcast(b, n, diag):
                pe.wait_ge(diag_done, cnt.next(diag_done))
                mm(bank[b][:, 0:n], ones[:], diag[:, 0:n], True, True).then_inc(roots_ready, 1)

            def stats_streamed(b, n):
                for m in range(KD):
                    pe.wait_ge(sq_streamed, cnt.next(sq_streamed))
                    ins = token_sums(b, 0, tmp[m % 2], n, m == 0, m == KD - 1)
                    ins.then_inc(sq_stream_used if m < KD - 1 else sums_ready, 1)

            def stats_summed(b):
                token_sums(b, 0, tmp[2], T, True, True).then_inc(sums_ready, 1)
                broadcast(b, T, tmp[3])

            def mod_tile(j):
                pe.wait_ge(mod_loaded, cnt.next(mod_loaded, 16))
                for k in range(KD):
                    m = mm(bank[7][:, j:j + 1], mod_raw[:, k], sc[:, k, 0:1], k == 0, k == KD - 1)
                m.then_inc(mod_used, 1)

            pe.wait_ge(const_set, 3)
            stats_streamed(6, T)
            stats_streamed(5, TC)
            broadcast(6, T, tmp[3])
            broadcast(5, TC, dec_k[0][2])
            pe.wait_ge(silu_c_done, 1)
            for n in range(8):
                s = n % 2
                pe.wait_ge(raw_loaded[s], cnt.next(raw_loaded[s], 16))
                for c in range(CPU):
                    j = CPU * n + c
                    for k in range(KD):
                        m = mm(bank[7][:, 2 * j:2 * j + 2], w_raw[s][:, k, c * P:(c + 1) * P], sc[:, k], k == 0, k == KD - 1)
                m.then_inc(unit_used[s], 1)
            pe.wait_ge(rank_lo, 1)
            for b, n, parts in ((3, T, (a_hi, a_lo)), (4, TC, (hc_hi, hc_lo))):
                for k in range(KD):
                    pe.wait_ge(norm_lo, cnt.next(norm_lo))
                    m = mm3(bank[b][:, 0:n], (wr_hi[:, k], wr_lo[:, k]), (parts[0][:, k], parts[1][:, k]), k == 0, k == KD - 1)
                m.then_inc(glr_ready, 1)
            filled[3] = filled[4] = True

            def gla_unit(n, banks, cx):
                s = n % 2
                unit(s, banks, (a_hi, a_lo))
                if cx is not None:
                    take(cx)
                    for c in range(CPU):
                        for k in range(KD):
                            m = mm3(bank[cx][:, c * TC:(c + 1) * TC], weights(s, k, c), (hc_hi[:, k], hc_lo[:, k]),
                                    k == 0, k == KD - 1)
                    m.then_inc(ready[cx], 1)
                mod_tile(2 * n)
                mod_tile(2 * n + 1)

            gla_unit(0, (0, 1), 2)
            pe.wait_ge(free[3], cnt.next(free[3]))
            pe.wait_ge(free[4], cnt.next(free[4]))
            filled[3] = filled[4] = False
            gla_unit(1, (3, 4), 5)
            pe.wait_ge(rank_lo, 3)

            def gates(i):
                g = GATE_ORDER[i]
                for part, c0, n in ((0, 0, T), (1, T, TC)):
                    x = 3 + 2 * part + i % 2
                    take(x)
                    filled[x] = False
                    if i >= 2:
                        pe.wait_ge(log_gate, cnt.upto(log_gate, 2 * (i - 2) + part + 1))
                    if part and i % 2 == 0 and i >= 4:
                        pe.wait_ge(ctx_tok, cnt.upto(ctx_tok, (i - 2) // 2))
                    mm(bank[x][:, 0:n], wg[:, g * P:(g + 1) * P], glr[:, c0:c0 + n], True, True).then_inc(gates_ready, 1)

            gates(0)
            gates(1)
            gla_unit(2, (0, 1), None)
            gates(2)
            gates(3)
            gla_unit(3, (0, 1), None)

            def context_keys(h):
                pe.wait_ge(ctx_key, cnt.next(ctx_key))
                pe.wait_ge(log_gate, cnt.upto(log_gate, 2 * (2 * h + 3) if h < 2 else 16))
                for j in range(4):
                    m = pe.transpose(bank[5][:, j * P:(j + 1) * P], dec_k[0][0][:, j * P:(j + 1) * P], ident[:])
                m.then_inc(ctx_keys_ready, 1)

            def v_unit(h):
                s = h % 2
                context_keys(h)
                if h < 2:
                    gates(4 + 2 * h)
                    gates(5 + 2 * h)
                pe.wait_ge(lo_done[s], cnt.next(lo_done[s]))
                for b, tiles, parts in ((0, (0, 1), (a_hi, a_lo)), (1, (2, 3), (a_hi, a_lo)), (2, (0, 1), (hc_hi, hc_lo))):
                    take(b)
                    for j, t in enumerate(tiles):
                        for k in range(KD):
                            m = mm3(bank[b][:, j * DV:(j + 1) * DV],
                                    (parts[0][:, k, t * P:(t + 1) * P], parts[1][:, k, t * P:(t + 1) * P]),
                                    (w_hi[s][:, k], w_lo[s][:, k]), k == 0, k == KD - 1)
                    m.then_inc(ready[b], 1)
                mod_tile(8 + 2 * h)
                mod_tile(9 + 2 * h)
                pe.wait_ge(ctx_tok, cnt.upto(ctx_tok, h + 1))
                take(2)
                filled[2] = False
                pe.wait_ge(log_gate, cnt.upto(log_gate, 12 if h == 0 else 16))
                take(6)
                for d in range(2):
                    for t in range(2):
                        m = mm(bank[6][:, d * DV:(d + 1) * DV], dec_k[0][1][:, (2 * d + t) * P:(2 * d + t + 1) * P],
                               vc[h % 2][:, t], t == 0, t == 1)
                m.then_inc(ctx_state_ready, 1)

            for h in range(HG):
                v_unit(h)
            for n in range(4):
                unit(n % 2, ((0, 1), (3, 4))[n % 2], (a_hi, a_lo))
                mod_tile(16 + 2 * n)
                mod_tile(17 + 2 * n)
            filled[7] = True
            filled[3] = filled[4] = False

            def scores(n):
                qd, kd, ke = dec_k[n % 2]
                pe.wait_ge(dec_done, cnt.next(dec_done, 3))
                if n == 0:
                    pe.wait_ge(r_copied, cnt.next(r_copied))
                    cnt.expect(free[3])
                for t in range(PAIRS):
                    m = pe.transpose(bank[5][:, t * P:(t + 1) * P], ke[:, t * P:(t + 1) * P], ident[:])
                m.then_inc(scan_keys, 1)
                for t in range(PAIRS):
                    m = mm(bank[4][:, t * P:(t + 1) * P], kd[:, t * P:(t + 1) * P], qd[:, t * P:(t + 1) * P], True, True)
                m.then_inc(scan_scores, 1)

            def scan(n):
                h, d, g = head_of(n)
                order = range(NCH) if d == 0 else range(NCH)[::-1]
                ob = (2 * (h % 2), 2 * (h % 2) + 1)
                qd = dec_k[n % 2][0]

                def kv(j):
                    t, r = order[j] // 2, (order[j] % 2) * CHUNK
                    b = 6 + j % 2
                    mm(bank[b][:, 0:DV], ke_tok[g][r:r + CHUNK, t], v[r:r + CHUNK, t, h * DV:(h + 1) * DV],
                       True, True).then_inc(kv_ready, 1)

                def inter(j):
                    c = order[j]
                    for e in range(2):
                        w = state[(7 * n + j - 1) % 4][:, e * P:(e + 1) * P] if j else cst[:, 2 * h + d, e * P:(e + 1) * P]
                        m = mm(bank[ob[e]][:, c * CHUNK:(c + 1) * CHUNK], w, qd[:, c * CHUNK:(c + 1) * CHUNK],
                               False, d == 1 and j == NCH - 1)
                        if j == NCH - 1 and d == 1:
                            m.then_inc(o_ready, 1)
                    if j == NCH - 1 and d == 0:
                        m.then_inc(forward_used, 1)
                    elif 0 < j < NCH - 1:
                        m.then_inc(state_used, 1)

                pe.wait_ge(ke_done, cnt.next(ke_done))
                if n == 0:
                    take(6)
                    take(7)
                    filled[6] = filled[7] = False
                kv(0)
                kv(1)
                if d == 0:
                    for b in ob:
                        take(b)
                pe.wait_ge(st_done, cnt.next(st_done))
                for e in range(2):
                    for t in range(PAIRS):
                        mm(bank[ob[e]][:, t * P:(t + 1) * P], v[:, t, h * DV + e * P:h * DV + (e + 1) * P],
                           st[d][:, t], d == 0 and t == 0, False)
                inter(0)
                for j in range(2, NCH - 1):
                    pe.wait_ge(state_done, cnt.next(state_done))
                    kv(j)
                    inter(j - 1)
                pe.wait_ge(state_done, cnt.next(state_done))
                inter(NCH - 2)
                if n + 1 < 2 * HG:
                    scores(n + 1)
                pe.wait_ge(state_done, cnt.next(state_done))
                inter(NCH - 1)

            scores(0)
            for n in range(2 * HG):
                scan(n)
            pe.wait_ge(o_summed, cnt.next(o_summed, HG))
            for h in range(HG):
                m = token_sums(4, PAIRS * h, tmp[h], T, True, True)
            m.then_inc(sums_ready, 1)
            for h in range(HG):
                broadcast(4 + h, T, tmp[h])
            for n in range(4):
                unit(n % 2, ((0, 1), (2, 3))[n % 2], (a_hi, a_lo), norm_lo if n == 0 else None)
                mod_tile(24 + 2 * n)
                mod_tile(25 + 2 * n)

            def double_norm():
                stats_summed(6)
                stats_streamed(5, T)
                broadcast(5, T, tmp[3])

            pe.wait_ge(sum_step, cnt.next(sum_step, KD))
            for b in range(4):
                take(b)
                filled[b] = False
            double_norm()

            def ffn(final=False):
                def group(by_chunk=None):
                    if cnt.has(silu_done):
                        pe.wait_ge(silu_done, cnt.now(silu_done))
                    unit(0, (0, 1), (a_hi, a_lo), by_chunk, silu_in)
                    cnt.expect(silu_done, CPU)
                    if cnt.has(gated):
                        pe.wait_ge(gated, cnt.now(gated))
                    unit(1, (2, 3), (a_hi, a_lo), None, up_ready)
                    cnt.expect(gated, CPU)
                    filled[0] = filled[1] = filled[2] = filled[3] = False

                def out_body():
                    for j in range(2):
                        pe.wait_ge(pair_done[j], cnt.now(pair_done[j]))
                        for q, (k0, k1) in enumerate(OUT_PARTS):
                            s = q % 2
                            pe.wait_ge(lo_done[s], cnt.next(lo_done[s]))
                            for c in range(CPU):
                                b = 4 + 2 * j + c
                                for k in range(k0, k1):
                                    m = mm3(bank[b][:], weights(s, k - k0, c), (g_hi[:, k], g_lo[:, k]), k == 0, k == KF - 1)
                                if k1 == KF:
                                    m.then_inc(out_ready, 1)
                            if k1 < KF:
                                m.then_inc(unit_used[s], 1)
                        cnt.expect(pair_done[j])

                group(norm_lo)
                with cnt.loop(F // UC - 1, {lo_done[0]: 1, lo_done[1]: 1, silu_done: CPU, gated: CPU}):
                    group()
                pe.wait_ge(gated, cnt.now(gated))
                for j in range(2):
                    cnt.expect(pair_done[j])
                if final:
                    out_body()
                    out_body()
                else:
                    with cnt.loop(2, {lo_done[0]: 4, lo_done[1]: 4, pair_done[0]: 1, pair_done[1]: 1}):
                        out_body()
                pe.wait_ge(pair_done[1], cnt.now(pair_done[1]))

            ffn()
            double_norm()
            ffn()
            stats_summed(6)

            for n in range(6):
                banks = ((0, 1), (2, 3))[n % 2]
                if n >= 2:
                    if n < 4:
                        pe.wait_ge(u_copied, cnt.upto(u_copied, CPU * (n - 1)))
                    else:
                        pe.wait_ge(roped, cnt.upto(roped, CPU * (n - 3)))
                unit(n % 2, banks, (a_hi, a_lo), norm_lo if n == 0 else None, rope_ready if n >= 2 else None)
                for b in banks:
                    filled[b] = False
            for n in range(2):
                pe.wait_ge(lo_done[n], cnt.next(lo_done[n]))
                pe.wait_ge(roped, cnt.upto(roped, CPU * (n + 3)))
                for b in (2 * n, 2 * n + 1):
                    for j in range(2):
                        t = 2 * (b % 2) + j
                        for k in range(KD):
                            m = mm3(bank[b][:, j * UC:(j + 1) * UC],
                                    (a_hi[:, k, t * P:(t + 1) * P], a_lo[:, k, t * P:(t + 1) * P]),
                                    (w_hi[n][:, k], w_lo[n][:, k]), k == 0, k == KD - 1)
                    m.then_inc(ready[b], 1)
            pe.wait_ge(mix_loaded, 64)
            for g in range(4):
                pe.wait_ge(pooled, cnt.next(pooled))
                if g:
                    pe.wait_ge(mixed_lo, cnt.upto(mixed_lo, g))
                mm(bank[6][:], pool_w[:, g], pool_u[g][:], True, True).then_inc(pool_mapped, 1)

            def ret_scores_of(h):
                pe.wait_ge(ret_in, cnt.next(ret_in, 2))
                if h:
                    pe.wait_ge(ret_scores, cnt.upto(ret_scores, h))
                for t in range(RCH):
                    s = slice(t * P, (t + 1) * P)
                    m = mm(bank[4][:, s], kr[:, h, s], qr[:, h, s], True, True)
                m.then_inc(ret_scored, 1)
                if h:
                    pe.wait_ge(ktok_done, cnt.upto(ktok_done, h))
                for t in range(RCH):
                    m = pe.transpose(bank[5][:, t * P:(t + 1) * P], ret_k[h % 2][:, t * P:(t + 1) * P], ident[:])
                m.then_inc(ret_keys, 1)

            def ret_states_of(h):
                pe.wait_ge(ktok_done, cnt.upto(ktok_done, h + 1))
                if h:
                    pe.wait_ge(r_state, cnt.upto(r_state, 3 * h))
                for t in range(RCH - 1):
                    m = mm(bank[7][:, t * P:(t + 1) * P], ret_kt[h % 2][:, t * P:(t + 1) * P], vr[:, t, h * P:(h + 1) * P], True, True)
                m.then_inc(ret_kv, 1)

            def ret_out_of(h):
                b = h % 2
                if h >= 2:
                    pe.wait_ge(ret_o, cnt.upto(ret_o, h - 1))
                pe.wait_ge(ret_scores, cnt.upto(ret_scores, h + 1))
                for t in range(RCH):
                    s = slice(t * P, (t + 1) * P)
                    mm(bank[b][:, s], vr[:, t, h * P:(h + 1) * P], ret_p[h % 2][:, s], t == 0, False)
                for t in range(1, RCH):
                    s = slice(t * P, (t + 1) * P)
                    pe.wait_ge(r_state, cnt.upto(r_state, 3 * h + t))
                    m = mm(bank[b][:, s], rstate[:, h % 2, t - 1], ret_q[h % 2][:, s], False, t == RCH - 1)
                m.then_inc(ret_o_ready, 1)

            def ret_stats_of(h):
                pe.wait_ge(ret_sq, cnt.next(ret_sq))
                pe.wait_ge(mixed_lo, cnt.upto(mixed_lo, 4 + h))
                token_sums(6, 0, ret_sq_t, T, True, True).then_inc(sums_ready, 1)
                broadcast(6, T, ret_diag)

            pe.wait_ge(v_copied, cnt.next(v_copied, 4))
            filled[2] = filled[3] = False
            ret_scores_of(0)
            unit(0, (2, 3), (a_hi, a_lo))
            ret_states_of(0)
            ret_scores_of(1)
            ret_out_of(0)
            pe.wait_ge(gate_silu, cnt.next(gate_silu, CPU))
            filled[2] = filled[3] = False
            unit(1, (2, 3), (a_hi, a_lo))
            ret_states_of(1)
            for h in range(1, HR):
                if h + 1 < HR:
                    ret_scores_of(h + 1)
                ret_stats_of(h - 1)
                ret_out_of(h)
                if h + 1 < HR:
                    ret_states_of(h + 1)
            ret_stats_of(HR - 1)
            pe.wait_ge(ret_o, cnt.upto(ret_o, HR))
            pe.wait_ge(gate_silu, cnt.next(gate_silu, CPU))

            base = [cnt.n.get(pair_done[j], 0) for j in range(2)]
            for n in range(4):
                for b in range(4):
                    filled[b] = False
                if n >= 2:
                    pe.wait_ge(pair_done[n % 2], cnt.upto(pair_done[n % 2], base[n % 2] + 1))
                unit(n % 2, ((0, 1), (2, 3))[n % 2], (m_hi, m_lo), mixed_lo if n == 0 else None, mix_out)
            for j in range(2):
                pe.wait_ge(pair_done[j], cnt.upto(pair_done[j], base[j] + 2))
            for b in range(4):
                filled[b] = False
            stats_summed(6)
            ffn(final=True)
            stats_summed(6)

        @block.scalar
        def _(act):
            cnt = Counts(act)

            def split_hi(s):
                act.wait_ge(raw_loaded[s], cnt.next(raw_loaded[s], 16))
                nc.scalar.activation(flat(w_hi[s]), flat(w_raw[s]), ACT.Copy).then_inc(hi_done[s], 1)

            def stream_squares(src, n, summed=False):
                for m in range(KD):
                    if summed:
                        act.wait_ge(x_added, cnt.next(x_added))
                    if m >= 2:
                        act.wait_ge(sq_stream_used, cnt.next(sq_stream_used))
                    nc.scalar.activation(tmp[m % 2][:, 0:n], src[:, m], ACT.Square).then_inc(sq_streamed, 1)
                cnt.expect(sq_stream_used)

            def norm_his(dst, n, shift=None):
                for m in range(KD):
                    act.wait_ge(scaled, cnt.next(scaled))
                    if shift is None:
                        ins = nc.scalar.activation(dst[:, m], tmp[m % 2][:, 0:n], ACT.Copy)
                    else:
                        ins = nc.scalar.activation(dst[:, m], tmp[m % 2][:, 0:n], ACT.Identity, bias=shift(m))
                    ins.then_inc(norm_hi, 1)

            def copy_out(b, dst, s=None):
                act.wait_ge(ready[b], cnt.next(ready[b]))
                nc.scalar.activation(dst, bank[b][:], ACT.Copy).then_inc(s or free[b], 1)

            act.wait_ge(x_loaded, 16)
            stream_squares(xT, T)
            act.wait_ge(c_loaded, 16)
            act.wait_ge(var_done, cnt.next(var_done))
            stream_squares(cT, TC)
            act.wait_ge(cols_loaded, 16)
            nc.scalar.activation(flat(sc), col("c", 0, 2 * KD), ACT.Silu).then_inc(silu_c_done, 1)
            act.wait_ge(rank_loaded, 16)
            nc.scalar.activation(flat(wr_hi), small_raw[:, 0], ACT.Copy).then_inc(rank_hi, 1)
            nc.scalar.activation(wg_hi[:], small_raw[:, 1], ACT.Copy).then_inc(rank_hi, 1)
            for s in range(2):
                cnt.expect(raw_loaded[s], 4 * 16)
            act.wait_ge(mods_done, cnt.next(mods_done))
            norm_his(a_hi, T, lambda m: mod[:, m, 0:1])
            split_hi(0)
            norm_his(hc_hi, TC, lambda m: mod[:, m, 1:2])
            split_hi(1)
            for b, c0, n in ((3, 0, T), (4, T, TC)):
                act.wait_ge(glr_ready, cnt.next(glr_ready))
                nc.scalar.activation(glr[:, c0:c0 + n], bank[b][:, 0:n], ACT.Copy).then_inc(glr_hi, 1)

            def gate_logs(i):
                g = GATE_ORDER[i]
                parts = [(part, tmp[2 * part + i % 2][:, 0:n]) for part, n in ((0, T), (1, TC))]
                for part, t in parts:
                    b = 3 + 2 * part + i % 2
                    act.wait_ge(gates_ready, cnt.next(gates_ready))
                    if i >= 2:
                        act.wait_ge(log_gate, cnt.upto(log_gate, 2 * (i - 2) + part + 1))
                    nc.scalar.activation(t, bank[b][:, 0:t.shape[-1]], ACT.Abs, bias=col("b_gate", g)).then_inc(abs_done, 1)
                    cnt.expect(abs_done)
                for part, t in parts:
                    act.wait_ge(abs_done, cnt.now(abs_done, 1 - part))
                    nc.scalar.activation(t, t, ACT.Exp, scale=-1.0).then_inc(act_step, 1)
                    cnt.expect(act_step)
                for part, t in parts:
                    act.wait_ge(act_step, cnt.now(act_step, 1 - part))
                    nc.scalar.activation(t, t, ACT.Ln, bias=one[:, 0:1]).then_inc(ln_done, 1)

            copy_out(0, kT[:, 0])
            copy_out(1, kT[:, 1])
            act.wait_ge(ready[2], cnt.next(ready[2]))
            split_hi(0)
            copy_out(3, kT[:, 2])
            copy_out(4, kT[:, 3])
            act.wait_ge(ready[5], cnt.next(ready[5]))
            split_hi(1)
            gate_logs(0)
            gate_logs(1)
            copy_out(0, qT[:, 0])
            copy_out(1, qT[:, 1])
            split_hi(0)
            gate_logs(2)
            gate_logs(3)
            copy_out(0, qT[:, 2])
            copy_out(1, qT[:, 3])
            split_hi(1)
            for h in range(HG):
                act.wait_ge(ctx_end, cnt.upto(ctx_end, h + 1))
                act.wait_ge(scanned, cnt.upto(scanned, 2 * (2 * h + 2)))
                nc.scalar.activation(dec_k[0][0][:, 0:TC], Gc[:, h], ACT.Exp, scale=-1.0 / GATE_NORM,
                                     bias=end16[:, h:h + 1]).then_inc(ctx_exp, 1)
                nc.scalar.activation(dec_k[0][0][:, TC + 1:2 * TC], Gc[:, HG + h, 0:TC - 1], ACT.Exp,
                                     scale=1.0 / GATE_NORM).then_inc(ctx_exp, 1)
                act.wait_ge(ctx_keys_ready, cnt.next(ctx_keys_ready))
                if h:
                    act.wait_ge(ctx_state_ready, cnt.upto(ctx_state_ready, h))
                nc.scalar.activation(dec_k[0][1][:], bank[5][:], ACT.Copy).then_inc(ctx_tok, 1)
                if h < 2:
                    gate_logs(4 + 2 * h)
                    gate_logs(5 + 2 * h)
                for b in range(2):
                    act.wait_ge(ready[b], cnt.next(ready[b]))
                    nc.scalar.activation(v[:, 2 * b:2 * b + 2, h * DV:(h + 1) * DV],
                                         bank[b][:].rearrange("p (t e) -> p t e", t=2), ACT.Copy).then_inc(free[b], 1)
                act.wait_ge(ready[2], cnt.next(ready[2]))
                split_hi(h % 2)

            def decays(n):
                h, d, g = head_of(n)
                qd, kd, ke = dec_k[n % 2]
                if n >= 2 and n % 2 == 0:
                    act.wait_ge(forward_used, cnt.next(forward_used))
                gate = G[:, g]
                act.wait_ge(rest_done, cnt.next(rest_done))
                nc.scalar.activation(ke[:], ke[:], ACT.Exp, scale=1.0 / GATE_NORM).then_inc(exp_done, 1)
                nc.scalar.activation(qd[:], gate, ACT.Exp, scale=1.0 / GATE_NORM).then_inc(exp_done, 1)
                nc.scalar.activation(kd[:], gate, ACT.Exp, scale=-1.0 / GATE_NORM).then_inc(exp_done, 1)
                nc.scalar.activation(ends[n % 2][:], gate.rearrange("p (c t) -> p c t", t=CHUNK)[:, :, ends_at(d)], ACT.Exp,
                                     scale=1.0 / GATE_NORM).then_inc(exp_done, 1)

            decays(0)
            for n in range(4):
                b = ((0, 1), (3, 4))[n % 2]
                for c in range(CPU):
                    copy_out(b[c], sr[:, CPU * n + c], r_copied if (n, c) == (3, 1) else None)
                split_hi(n % 2)
            act.wait_ge(r_copied, cnt.next(r_copied))
            nc.scalar.activation(flat(sr), flat(sr), ACT.Silu).then_inc(silu_r, 1)

            def turned_keys(n):
                act.wait_ge(scan_keys, cnt.next(scan_keys))
                nc.scalar.activation(flat(ke_tok[head_of(n)[2]]), bank[5][:], ACT.Copy).then_inc(ke_done, 1)

            def o_squares(h):
                for e in range(2):
                    b = 2 * (h % 2) + e
                    act.wait_ge(o_ready, cnt.next(o_ready))
                    nc.scalar.activation(o_sq[h + HG * e][:], bank[b][:], ACT.Square).then_inc(o_squared, 1)

            turned_keys(0)
            decays(1)
            for n in range(1, 2 * HG):
                turned_keys(n)
                if n >= 2 and n % 2 == 0:
                    o_squares(n // 2 - 1)
                if n + 1 < 2 * HG:
                    decays(n + 1)
            o_squares(HG - 1)
            for m in range(KD):
                act.wait_ge(scaled, cnt.next(scaled))
                nc.scalar.activation(a_hi[:, m], sr[:, m], ACT.Copy).then_inc(norm_hi, 1)
            for n in range(4):
                for c in range(CPU):
                    m = CPU * n + c
                    b = (0, 1, 2, 3)[m % 4]
                    act.wait_ge(ready[b], cnt.next(ready[b]))
                    if m >= 2:
                        act.wait_ge(sum_step, cnt.next(sum_step))
                    nc.scalar.activation(tmp[m % 2][:], bank[b][:], ACT.Square).then_inc(y_squared, 1)
                    nc.scalar.activation(y_gla[:, m], bank[b][:], ACT.Copy).then_inc(free[b], 1)
                if n < 3:
                    split_hi(n % 2)
            cnt.expect(sum_step, 2)

            def double_norm_act(shift):
                stream_squares(xT, T, True)
                norm_his(a_hi, T, shift)

            def ffn(final=False):
                def group():
                    split_hi(1)
                    if cnt.has(gated):
                        act.wait_ge(gated, cnt.now(gated))
                    for c in range(CPU):
                        act.wait_ge(silu_in, cnt.next(silu_in))
                        nc.scalar.activation(tmp[c][:], bank[c][:], ACT.Silu).then_inc(silu_done, 1)
                    split_hi(0)
                    act.wait_ge(up_ready, cnt.next(up_ready, CPU))
                    cnt.expect(gated, CPU)

                def out_body(final=False):
                    for j in range(2):
                        split_hi(1)
                        act.wait_ge(unit_used[0], cnt.next(unit_used[0]))
                        split_hi(0)
                        act.wait_ge(unit_used[1], cnt.next(unit_used[1]))
                        split_hi(1)
                        if not (final and j == 1):
                            act.wait_ge(unit_used[0], cnt.next(unit_used[0]))
                            split_hi(0)
                            act.wait_ge(out_ready, cnt.next(out_ready, CPU))

                group()
                with cnt.loop(F // UC - 1, {raw_loaded[0]: 16, raw_loaded[1]: 16, gated: CPU,
                                            silu_in: CPU, up_ready: CPU}):
                    group()
                if final:
                    out_body()
                    out_body(True)
                else:
                    with cnt.loop(2, {raw_loaded[0]: 64, raw_loaded[1]: 64, unit_used[0]: 4, unit_used[1]: 2,
                                      out_ready: 2 * CPU}):
                        out_body()

            cnt.expect(unit_used[0], 4)
            cnt.expect(unit_used[1], 4)
            double_norm_act(lambda m: mod[:, 3 * KD + m, 0:1])
            ffn()
            double_norm_act(None)
            ffn()
            norm_his(a_hi, T)
            split_hi(1)
            for n in range(2):
                for c in range(CPU):
                    copy_out(2 * n + c, pool_u[CPU * n + c][:], u_copied)
                split_hi(n)
            for n in range(2, 6):
                act.wait_ge(rope_ready, cnt.next(rope_ready, CPU))
                split_hi(n % 2)
            for n in range(2):
                for b in (2 * n, 2 * n + 1):
                    t = 2 * (b % 2)
                    act.wait_ge(ready[b], cnt.next(ready[b]))
                    nc.scalar.activation(vr[:, t:t + 2, n * UC:(n + 1) * UC],
                                         bank[b][:].rearrange("p (t e) -> p t e", t=2), ACT.Copy).then_inc(v_copied, 1)
                split_hi(n)
            for g in range(4):
                act.wait_ge(pool_mapped, cnt.next(pool_mapped))
                nc.scalar.activation(m_hi[:, g], bank[6][:], ACT.Copy, scale=col("pool_scale", g)).then_inc(mixed_hi, 1)

            def turned(h):
                act.wait_ge(ret_keys, cnt.next(ret_keys))
                nc.scalar.activation(ret_kt[h % 2][:], bank[5][:], ACT.Copy).then_inc(ktok_done, 1)

            def gate_unit(n):
                for c in range(CPU):
                    act.wait_ge(ready[2 + c], cnt.next(ready[2 + c]))
                    nc.scalar.activation(gr[:, CPU * n + c], bank[2 + c][:], ACT.Silu).then_inc(gate_silu, 1)
                    cnt.expect(gate_silu)
                split_hi(n)

            def ret_square(h):
                act.wait_ge(ret_o_ready, cnt.next(ret_o_ready))
                nc.scalar.activation(ret_sq_t[:], bank[h % 2][:], ACT.Square).then_inc(ret_sq, 1)

            def mixed_upper(h):
                act.wait_ge(scaled, cnt.next(scaled))
                nc.scalar.activation(m_hi[:, 4 + h], gr[:, h], ACT.Copy).then_inc(mixed_hi, 1)

            turned(0)
            gate_unit(0)
            turned(1)
            ret_square(0)
            gate_unit(1)
            for h in range(1, HR):
                if h + 1 < HR:
                    turned(h + 1)
                mixed_upper(h - 1)
                ret_square(h)
            mixed_upper(HR - 1)
            for n in range(4):
                act.wait_ge(mix_out, cnt.next(mix_out, CPU))
                if n < 3:
                    split_hi(n % 2)
            norm_his(a_hi, T)
            ffn(final=True)

        @block.vector
        def _(dve):
            cnt = Counts(dve)
            V = nc.vector

            def split_lo(s):
                dve.wait_ge(hi_done[s], cnt.next(hi_done[s]))
                V.tensor_tensor(flat(w_lo[s]), flat(w_raw[s]), flat(w_hi[s]).bitcast(F32), ALU.subtract).then_inc(lo_done[s], 1)

            def mean_square(b, n, width):
                dve.wait_ge(sums_ready, cnt.next(sums_ready))
                V.tensor_scalar(col4[:, 0:n], bank[b][:, 0:n], 1.0 / width, EPS, ALU.mult, ALU.add).then_inc(var_done, 1)

            def diagonal(dst, n, c0=0):
                V.tensor_tensor(dst[:, 0:n * P].rearrange("p (t q) -> p t q", q=P), spread(ident[:], 1, [P, n, P]),
                                spread(root4[:, c0:c0 + n], 2, [P, n, P]), ALU.mult).then_inc(diag_done, 1)

            def stats(b, diag, n=PAIRS):
                mean_square(b, n, D)
                dve.wait_ge(root_done, cnt.next(root_done))
                diagonal(diag, n)
                dve.wait_ge(roots_ready, cnt.next(roots_ready))

            def norm_parts(src, b, gains, n, hi, lo, shift=None):
                def lower(m):
                    dve.wait_ge(norm_hi, cnt.next(norm_hi))
                    t = tmp[m % 2][:, 0:n]
                    up = hi[:, m].bitcast(F32)
                    if shift is None:
                        V.tensor_tensor(lo[:, m], t, up, ALU.subtract).then_inc(norm_lo, 1)
                        cnt.expect(norm_lo)
                    else:
                        V.scalar_tensor_tensor(lo[:, m], t, shift(m), up, ALU.add, ALU.subtract).then_inc(norm_lo, 1)
                        cnt.expect(norm_lo)

                for m in range(KD):
                    if m >= 2:
                        dve.wait_ge(norm_lo, cnt.now(norm_lo))
                    V.scalar_tensor_tensor(tmp[m % 2][:, 0:n], src[:, m], gains(m), bank[b][:, 0:n], ALU.mult, ALU.mult).then_inc(scaled, 1)
                    cnt.expect(scaled)
                    if m:
                        lower(m - 1)
                lower(KD - 1)

            V.memset(power[:], -0.5).then_inc(const_set, 1)
            V.memset(one[:], 1.0).then_inc(const_set, 1)
            V.memset(ones[:], 1.0).then_inc(const_set, 1)
            dve.wait_ge(consts_loaded, 16)
            mean_square(6, PAIRS, D)
            dve.wait_ge(root_done, cnt.next(root_done))
            diagonal(tmp[3], PAIRS)
            mean_square(5, 2, D)
            dve.wait_ge(root_done, cnt.next(root_done))
            diagonal(dec_k[0][2], 2)
            dve.wait_ge(roots_ready, cnt.next(roots_ready, 2))
            dve.wait_ge(rank_hi, cnt.next(rank_hi))
            V.tensor_tensor(flat(wr_lo), small_raw[:, 0], flat(wr_hi).bitcast(F32), ALU.subtract).then_inc(rank_lo, 1)
            dve.wait_ge(rank_hi, cnt.next(rank_hi))
            V.tensor_copy(wg[0:64, :], wg_hi[0:64, :].bitcast(F32)).then_inc(rank_lo, 1)
            V.tensor_tensor(wg[64:128, :], small_raw[64:128, 1], wg_hi[64:128, :].bitcast(F32), ALU.subtract).then_inc(rank_lo, 1)
            dve.wait_ge(cols_loaded, 16)
            dve.wait_ge(unit_used[0], cnt.next(unit_used[0], 4))
            dve.wait_ge(unit_used[1], cnt.next(unit_used[1], 4))
            V.tensor_tensor(mod[:, 0:2 * KD], bank[7][:, 0:4 * KD].rearrange("p (j v) -> p j v", v=2),
                            spread(col("mod_b", 0, 2 * KD), 2, [P, 2 * KD, 2]), ALU.add).then_inc(dve_step, 1)
            dve.wait_ge(dve_step, cnt.next(dve_step))
            for u in range(2):
                V.scalar_tensor_tensor(gain[:, u], mod[:, KD:2 * KD, u], 1.0, col("norm_g", 0, KD), ALU.add, ALU.mult).then_inc(mods_done, 1)
                cnt.expect(mods_done)
            dve.wait_ge(mods_done, cnt.now(mods_done))
            norm_parts(xT, 6, lambda m: gain[:, 0, m:m + 1], T, a_hi, a_lo, lambda m: mod[:, m, 0:1])
            dve.wait_ge(norm_lo, cnt.now(norm_lo))
            split_lo(0)
            norm_parts(cT, 5, lambda m: gain[:, 1, m:m + 1], TC, hc_hi, hc_lo, lambda m: mod[:, m, 1:2])
            split_lo(1)
            for b, c0, n in ((3, 0, T), (4, T, TC)):
                dve.wait_ge(glr_hi, cnt.next(glr_hi))
                for r in (32, 96):
                    g = glr[r:r + 32, c0:c0 + n]
                    ins = V.tensor_tensor(g, bank[b][r:r + 32, 0:n], g.bitcast(F32), ALU.subtract)
                ins.then_inc(free[b], 1)
            dve.wait_ge(ready[2], cnt.next(ready[2]))
            V.tensor_copy(kcT[:, 0:2].rearrange("p a b -> p (a b)"), bank[2][:]).then_inc(free[2], 1)
            split_lo(0)
            dve.wait_ge(ready[5], cnt.next(ready[5]))
            V.tensor_copy(kcT[:, 2:4].rearrange("p a b -> p (a b)"), bank[5][:]).then_inc(free[5], 1)
            split_lo(1)
            dve.wait_ge(consts_loaded, 48)

            def log_gates(i):
                g = GATE_ORDER[i]
                parts = ((G, 0, T), (Gc, 1, TC))
                for dst, part, n in parts:
                    dve.wait_ge(abs_done, cnt.next(abs_done))
                    V.tensor_scalar(dst[:, g], bank[3 + 2 * part + i % 2][:, 0:n], col("b_gate", g), 0.0, ALU.add, ALU.min).then_inc(log_min, 1)
                    cnt.expect(log_min)
                for dst, part, n in parts:
                    dve.wait_ge(ln_done, cnt.next(ln_done))
                    dve.wait_ge(log_min, cnt.now(log_min, 1 - part))
                    V.tensor_tensor(dst[:, g], dst[:, g], tmp[2 * part + i % 2][:, 0:n], ALU.subtract).then_inc(log_gate, 1)
                    cnt.expect(log_gate)
                for dst, part, n in parts:
                    dve.wait_ge(log_gate, cnt.now(log_gate, 1 - part))
                    x = dst[:, g, ::-1] if part == 0 and g >= HG else dst[:, g]
                    keep = reset[:] if part == 0 else one[:, 0:1].to_broadcast([P, n])
                    V.tensor_tensor_scan(x, keep, x, 0.0, ALU.mult, ALU.add).then_inc(scanned, 1)
                    cnt.expect(scanned)
                if g < HG:
                    dve.wait_ge(scanned, cnt.now(scanned))
                    V.tensor_scalar(end16[:, g:g + 1], Gc[:, g, TC - 1:TC], 1.0 / GATE_NORM, None, ALU.mult).then_inc(ctx_end, 1)

            log_gates(0)
            log_gates(1)
            split_lo(0)
            log_gates(2)
            log_gates(3)
            split_lo(1)
            for h in range(HG):
                dve.wait_ge(ctx_exp, cnt.next(ctx_exp, 2))
                V.memset(dec_k[0][0][:, TC:TC + 1], 1.0).then_inc(dve_step, 1)
                dve.wait_ge(dve_step, cnt.next(dve_step))
                e = dec_k[0][0][:].rearrange("p (d t) -> p d t", d=2)
                V.tensor_tensor(e, e, spread(kcT[:, h], 1, [P, 2, TC]), ALU.mult).then_inc(ctx_key, 1)
                if h < 2:
                    log_gates(4 + 2 * h)
                    log_gates(5 + 2 * h)
                dve.wait_ge(ready[2], cnt.next(ready[2]))
                V.tensor_copy(flat(vc[h % 2]), bank[2][:]).then_inc(free[2], 1)
                split_lo(h % 2)
                dve.wait_ge(ctx_state_ready, cnt.next(ctx_state_ready))
                V.tensor_copy(cst[:, 2 * h:2 * h + 2].rearrange("p a b -> p (a b)"), bank[6][:]).then_inc(free[6], 1)

            def rest(n):
                h, d, g = head_of(n)
                gate = G[:, g].rearrange("p (c t) -> p c t", t=CHUNK)
                j = ends_at(d)
                V.tensor_tensor(dec_k[n % 2][2][:].rearrange("p (c t) -> p c t", t=CHUNK),
                                gate[:, :, j:j + 1].to_broadcast([P, NCH, CHUNK]), gate, ALU.subtract).then_inc(rest_done, 1)

            def decayed(n, j):
                h = n // 2
                qd, kd, ke = dec_k[n % 2]
                dve.wait_ge(exp_done, cnt.next(exp_done))
                if j == 0:
                    V.tensor_tensor(ke[:], ke[:], kT[:, h], ALU.mult).then_inc(dec_done, 1)
                elif j == 1:
                    V.scalar_tensor_tensor(qd[:], qd[:], DK ** -0.5, qT[:, h], ALU.mult, ALU.mult).then_inc(dec_done, 1)
                else:
                    V.tensor_tensor(kd[:], kd[:], kT[:, h], ALU.mult).then_inc(dec_done, 1)
                    dve.wait_ge(exp_done, cnt.next(exp_done))

            def gate_o(h):
                for e in range(2):
                    dve.wait_ge(o_squared, cnt.next(o_squared))
                    m = 2 * h + e
                    V.scalar_tensor_tensor(sr[:, m], bank[2 * (h % 2) + e][:], col("gla_g", e), sr[:, m],
                                           ALU.mult, ALU.mult).then_inc(free[2 * (h % 2) + e], 1)
                V.tensor_tensor(tmp[h][:], o_sq[h][:], o_sq[HG + h][:], ALU.add).then_inc(o_summed, 1)

            for d in range(2):
                V.memset(flat(st[d]), 0.0).then_inc(dve_step, 1)
                dve.wait_ge(dve_step, cnt.next(dve_step))
            rest(0)
            rest(1)
            for j in range(3):
                decayed(0, j)
            for n in range(4):
                split_lo(n % 2)
            dve.wait_ge(mod_used, cnt.next(mod_used, 3 * KD))
            V.tensor_tensor(mod[:, 2 * KD:5 * KD, 0], bank[7][:, 0:3 * KD], col("mod_b", 2 * KD, 3 * KD), ALU.add).then_inc(free[7], 1)
            cnt.expect(free[7])
            dve.wait_ge(free[7], cnt.now(free[7]))
            V.tensor_tensor(gain[:, 2], mod[:, 2 * KD:3 * KD, 0], col("norm_g", KD, KD), ALU.mult)
            V.scalar_tensor_tensor(gain[:, 3], mod[:, 4 * KD:5 * KD, 0], 1.0, col("norm_g", 2 * KD, KD), ALU.add, ALU.mult).then_inc(dve_step, 1)
            dve.wait_ge(dve_step, cnt.next(dve_step))
            dve.wait_ge(silu_r, cnt.next(silu_r))

            def scan(n):
                h, d, g = head_of(n)
                order = range(NCH) if d == 0 else range(NCH)[::-1]
                dve.wait_ge(scan_scores, cnt.next(scan_scores))
                V.copy_predicated(st[d][:], spread(masks[:, d].bitcast(U32), 1, [P, PAIRS, P]),
                                  bank[4][:].rearrange("p (t q) -> p t q", q=P)).then_inc(st_done, 1)
                for j in range(NCH - 1):
                    w = 7 * n + j
                    dve.wait_ge(kv_ready, cnt.next(kv_ready))
                    if j:
                        dve.wait_ge(state_done, cnt.now(state_done))
                    if w >= 4:
                        q, r = divmod(w - 4, 7)
                        dve.wait_ge(state_used, cnt.upto(state_used, 6 * q + r + 1))
                    prev = state[(w - 1) % 4][:] if j else cst[:, n]
                    c = order[j]
                    V.scalar_tensor_tensor(state[w % 4][:], prev, ends[n % 2][:, c:c + 1], bank[6 + j % 2][:, 0:DV],
                                           ALU.mult, ALU.add).then_inc(state_done, 1)
                    cnt.expect(state_done)
                    if j == 0 and n >= 2 and n % 2 == 0:
                        gate_o(n // 2 - 1)
                    elif 2 <= j < 5 and n + 1 < 2 * HG:
                        decayed(n + 1, j - 2)
                    elif j == 5 and n + 2 < 2 * HG:
                        rest(n + 2)

            for n in range(2 * HG):
                scan(n)
            gate_o(HG - 1)
            mean_square(4, HG * PAIRS, DV)
            dve.wait_ge(root_done, cnt.next(root_done))
            for h in range(HG):
                diagonal(tmp[h], PAIRS, PAIRS * h)

            def lower_o(m):
                dve.wait_ge(norm_hi, cnt.next(norm_hi))
                V.tensor_tensor(a_lo[:, m], sr[:, m], a_hi[:, m].bitcast(F32), ALU.subtract).then_inc(norm_lo, 1)
                cnt.expect(norm_lo)

            for m in range(KD):
                if m % 2 == 0:
                    dve.wait_ge(roots_ready, cnt.next(roots_ready))
                V.tensor_tensor(sr[:, m], sr[:, m], bank[4 + m // 2][:], ALU.mult).then_inc(scaled, 1)
                cnt.expect(scaled)
                if m:
                    lower_o(m - 1)
            lower_o(KD - 1)
            V.memset(tmp[2][:], 0.0).then_inc(dve_step, 1)
            dve.wait_ge(dve_step, cnt.next(dve_step))
            for n in range(4):
                for c in range(CPU):
                    dve.wait_ge(y_squared, cnt.next(y_squared))
                    if cnt.has(sum_step):
                        dve.wait_ge(sum_step, cnt.now(sum_step))
                    V.tensor_tensor(tmp[2][:], tmp[2][:], tmp[c][:], ALU.add).then_inc(sum_step, 1)
                    cnt.expect(sum_step)
                if n < 3:
                    split_lo(n % 2)
            dve.wait_ge(mod_used, cnt.next(mod_used, KD))
            V.tensor_tensor(mod[:, 5 * KD:, 0], bank[7][:, 3 * KD:4 * KD], col("mod_b", 5 * KD, KD), ALU.add).then_inc(dve_step, 1)
            dve.wait_ge(dve_step, cnt.next(dve_step))
            V.tensor_tensor(gain[:, 4], mod[:, 5 * KD:, 0], col("norm_g", 3 * KD, KD), ALU.mult).then_inc(dve_step, 1)
            dve.wait_ge(dve_step, cnt.next(dve_step))

            def double_norm(y, c, gains, shift=None):
                stats(6, tmp[3])
                for m in range(KD + 1):
                    if m < KD:
                        V.scalar_tensor_tensor(y[:, m], y[:, m], gain[:, c, m:m + 1], bank[6][:], ALU.mult, ALU.mult).then_inc(y_scaled, 1)
                        cnt.expect(y_scaled)
                    if m:
                        dve.wait_ge(y_scaled, cnt.now(y_scaled, 1 if m < KD else 0))
                        V.tensor_tensor(xT[:, m - 1], xT[:, m - 1], y[:, m - 1], ALU.add).then_inc(x_added, 1)
                stats(5, tmp[3])
                norm_parts(xT, 5, gains, T, a_hi, a_lo, shift)

            def sum_pair(banks, chunks, half, to_x, j):
                dst = xT if to_x else y_ffn
                for c in range(CPU):
                    if half:
                        dve.wait_ge(out_ready, cnt.next(out_ready))
                    else:
                        dve.wait_ge(mix_out, cnt.next(mix_out))
                    at = dst[:, chunks[c]]
                    if len(at.shape) == 3:
                        at = at.rearrange("p o t -> p (o t)")
                    b = bank[banks[c]][:]
                    if not to_x:
                        ins = V.tensor_scalar(at, b, 1.0, None, ALU.mult)
                    else:
                        ins = V.scalar_tensor_tensor(at, b, 0.5 if half else 1.0, at, ALU.mult, ALU.add)
                    ins.then_inc(chunk_done, 1)
                    cnt.expect(chunk_done)
                dve.wait_ge(pair_done[1 - j], cnt.now(pair_done[1 - j]))
                for c in range(CPU):
                    at = dst[:, chunks[c]]
                    if len(at.shape) == 3:
                        at = at.rearrange("p o t -> p (o t)")
                    dve.wait_ge(chunk_done, cnt.now(chunk_done, 1 - c))
                    V.tensor_tensor(tmp[c][:], at, at, ALU.mult).then_inc(sq_done, 1)
                    cnt.expect(sq_done)
                for c in range(CPU):
                    dve.wait_ge(sq_done, cnt.now(sq_done, 1 - c))
                    if c:
                        dve.wait_ge(half_summed, cnt.now(half_summed))
                    V.tensor_tensor(tmp[2][:], tmp[2][:], tmp[c][:], ALU.add).then_inc(pair_done[j] if c else half_summed, 1)
                    cnt.expect(pair_done[j] if c else half_summed)

            def ffn(to_x, final=False):
                def group(m0):
                    split_lo(1)
                    split_lo(0)
                    for c in range(CPU):
                        dve.wait_ge(silu_done, cnt.next(silu_done))
                        dve.wait_ge(up_ready, cnt.next(up_ready))
                        if cnt.has(gated):
                            dve.wait_ge(gated, cnt.now(gated, 1 - c))
                        V.tensor_tensor(tmp[2 + c][:], tmp[c][:], bank[2 + c][:], ALU.mult).then_inc(prod_done, 1)
                        cnt.expect(prod_done)
                        V.tensor_tensor(hidden(g_hi, m0, c), tmp[c][:], bank[2 + c][:], ALU.mult).then_inc(gate_hi, 1)
                        cnt.expect(gate_hi)
                    for c in range(CPU):
                        dve.wait_ge(prod_done, cnt.now(prod_done, 1 - c))
                        dve.wait_ge(gate_hi, cnt.now(gate_hi, 1 - c))
                        V.tensor_tensor(hidden(g_lo, m0, c), tmp[2 + c][:], hidden(g_hi, m0, c).bitcast(F32), ALU.subtract).then_inc(gated, 1)
                        cnt.expect(gated)

                def out_body(i, final=False):
                    for j in range(2):
                        split_lo(1)
                        split_lo(0)
                        split_lo(1)
                        if not (final and j == 1):
                            split_lo(0)
                        chunks = [bass.ds(i * 4 + (2 * j + c), 1) if not isinstance(i, int) else 4 * i + 2 * j + c for c in range(CPU)]
                        sum_pair((4 + 2 * j, 5 + 2 * j), chunks, True, to_x, j)

                def hidden(t, m0, c):
                    if isinstance(m0, int):
                        return t[:, m0 + c]
                    return t[:, bass.ds(m0 * CPU + (CPU + c), 1)].rearrange("p o t -> p (o t)")

                group(0)
                with cnt.loop(F // UC - 1, {hi_done[0]: 1, hi_done[1]: 1, up_ready: CPU, silu_done: CPU,
                                            prod_done: CPU, gate_hi: CPU, gated: CPU}) as i:
                    group(i)
                dve.wait_ge(gated, cnt.now(gated))
                for j in range(2):
                    V.memset(tmp[2][:, j * (T // 2):(j + 1) * (T // 2)], 0.0).then_inc(pair_done[j], 1)
                    cnt.expect(pair_done[j])
                if final:
                    out_body(0)
                    out_body(1, True)
                else:
                    with cnt.loop(2, {hi_done[0]: 4, hi_done[1]: 4, out_ready: 2 * CPU, chunk_done: 2 * CPU,
                                      sq_done: 2 * CPU, half_summed: 2, pair_done[0]: 1, pair_done[1]: 1}) as i:
                        out_body(i)

            double_norm(y_gla, 2, lambda m: gain[:, 3, m:m + 1], lambda m: mod[:, 3 * KD + m, 0:1])
            ffn(False)
            double_norm(y_ffn, 4, lambda m: col("ffn1_g", m))
            ffn(True)
            stats(6, tmp[3])
            norm_parts(xT, 6, lambda m: col("mix_g", m), T, a_hi, a_lo)
            split_lo(1)
            dve.wait_ge(mix_loaded, 64)

            def pooling(g):
                w = WINDOWS[g]
                dve.wait_ge(u_copied, cnt.next(u_copied))
                u = cur = pool_u[g]
                s, turn = 1, 0
                while s < w:
                    nxt = tmp[2 + turn]
                    V.tensor_copy(nxt[:, 0:s], cur[:, 0:s])
                    V.tensor_tensor(nxt[:, s:T], cur[:, s:T], cur[:, 0:T - s], ALU.add).then_inc(dve_step, 1)
                    dve.wait_ge(dve_step, cnt.next(dve_step))
                    cur, s, turn = nxt, 2 * s, 1 - turn
                V.tensor_tensor(cur[:, 0:16], cur[:, 0:16], pool_n[:, g], ALU.mult).then_inc(dve_step, 1)
                dve.wait_ge(dve_step, cnt.next(dve_step))
                V.scalar_tensor_tensor(u[:], cur[:], 1.0 / w, u[:], ALU.mult, ALU.subtract).then_inc(pooled, 1)
                cnt.expect(pooled)
                dve.wait_ge(pooled, cnt.now(pooled))

            def rotate(n):
                dst = kr if n < 4 else qr
                for c in range(CPU):
                    b = bank[2 * (n % 2) + c]
                    t = tmp[c]
                    h = CPU * (n % 2) + c
                    dve.wait_ge(rope_ready, cnt.next(rope_ready))
                    if cnt.has(roped):
                        dve.wait_ge(roped, cnt.now(roped, 1 if c == 0 else 0))
                    V.tensor_tensor(t[0:64, :], b[64:128, :], trig[64:128, 1], ALU.mult)
                    V.tensor_tensor(t[64:128, :], b[0:64, :], trig[0:64, 1], ALU.mult)
                    V.tensor_tensor(dst[:, h], b[:], trig[:, 0], ALU.mult).then_inc(dve_step, 1)
                    dve.wait_ge(dve_step, cnt.next(dve_step))
                    V.tensor_tensor(dst[:, h], dst[:, h], t[:], ALU.add).then_inc(roped, 1)
                    cnt.expect(roped)

            split_lo(0)
            pooling(0)
            split_lo(1)
            pooling(1)
            split_lo(0)
            rotate(2)
            pooling(2)
            split_lo(1)
            rotate(3)
            pooling(3)
            split_lo(0)
            rotate(4)
            split_lo(1)
            rotate(5)
            split_lo(0)
            dve.wait_ge(roped, cnt.now(roped))

            def ret_inputs(h):
                for out, x, r in ((ret_q[h % 2], qr, 0), (ret_k[h % 2], kr, 1)):
                    V.tensor_tensor(out[:].rearrange("p (t q) -> p t q", q=P), x[:, h].rearrange("p (t q) -> p t q", q=P),
                                    spread(decay[:, r, h], 1, [P, RCH, P]), ALU.mult).then_inc(ret_in, 1)

            def ret_decayed_scores(h):
                dve.wait_ge(ret_scored, cnt.next(ret_scored))
                V.tensor_tensor(ret_p[h % 2][:].rearrange("p (t q) -> p t q", q=P), bank[4][:].rearrange("p (t q) -> p t q", q=P),
                                spread(decay[:, 2, h], 1, [P, RCH, P]), ALU.mult).then_inc(ret_scores, 1)

            def ret_state(h):
                whole = float((1.0 - 2.0 ** (-5.0 - h)) ** P)
                dve.wait_ge(ret_kv, cnt.next(ret_kv))
                r = rstate[:, h % 2]
                V.tensor_scalar(r[:, 0], bank[7][:, 0:P], 1.0, None, ALU.mult).then_inc(r_state, 1)
                cnt.expect(r_state)
                for t in (1, 2):
                    dve.wait_ge(r_state, cnt.now(r_state))
                    V.scalar_tensor_tensor(r[:, t], r[:, t - 1], whole, bank[7][:, t * P:(t + 1) * P], ALU.mult, ALU.add).then_inc(r_state, 1)
                    cnt.expect(r_state)

            def ret_gated(h):
                dve.wait_ge(ret_sq, cnt.next(ret_sq))
                if h == 0:
                    dve.wait_ge(gate_silu, cnt.upto(gate_silu, 1))
                dve.wait_ge(gate_silu, cnt.upto(gate_silu, h + 1))
                V.scalar_tensor_tensor(gr[:, h], bank[h % 2][:], col("ret_g", h), gr[:, h], ALU.mult, ALU.mult).then_inc(ret_o, 1)
                cnt.expect(ret_o)

            def ret_norm(h):
                mean_square(6, RCH, P)
                dve.wait_ge(root_done, cnt.next(root_done))
                diagonal(ret_diag, RCH)
                dve.wait_ge(roots_ready, cnt.next(roots_ready))
                dve.wait_ge(ret_o, cnt.now(ret_o))
                V.tensor_tensor(gr[:, h], gr[:, h], bank[6][:], ALU.mult).then_inc(scaled, 1)
                cnt.expect(scaled)
                dve.wait_ge(mixed_hi, cnt.next(mixed_hi))
                V.tensor_tensor(m_lo[:, 4 + h], gr[:, h], m_hi[:, 4 + h].bitcast(F32), ALU.subtract).then_inc(mixed_lo, 1)

            for g in range(4):
                dve.wait_ge(mixed_hi, cnt.next(mixed_hi))
                V.scalar_tensor_tensor(m_lo[:, g], bank[6][:], col("pool_scale", g), m_hi[:, g].bitcast(F32),
                                       ALU.mult, ALU.subtract).then_inc(mixed_lo, 1)
                if g == 0:
                    ret_inputs(0)
                if g == 1:
                    ret_inputs(1)
                if g == 2:
                    split_lo(1)
            ret_decayed_scores(0)
            ret_state(0)
            split_lo(0)
            ret_decayed_scores(1)
            ret_gated(0)
            ret_state(1)
            split_lo(1)
            for h in range(1, HR):
                if h + 1 < HR:
                    ret_inputs(h + 1)
                    ret_decayed_scores(h + 1)
                ret_norm(h - 1)
                ret_gated(h)
                if h + 1 < HR:
                    ret_state(h + 1)
            ret_norm(HR - 1)
            V.memset(tmp[2][:], 0.0).then_inc(dve_step, 1)
            dve.wait_ge(dve_step, cnt.next(dve_step))
            for n in range(4):
                sum_pair((2 * (n % 2), 2 * (n % 2) + 1), (CPU * n, CPU * n + 1), False, True, n % 2)
                if n < 3:
                    split_lo(n % 2)
            stats(6, tmp[3])
            norm_parts(xT, 6, lambda m: col("ffn2_g", m), T, a_hi, a_lo)
            ffn(True, final=True)
            stats(6, tmp[3])
            for m in range(KD):
                V.scalar_tensor_tensor(y_ffn[:, m], xT[:, m], col("final_g", m), bank[6][:], ALU.mult, ALU.mult).then_inc(out_done, 1)


def _units(w):
    n = w.shape[1] // UC
    return w.reshape(KD, P, n, UC).transpose(2, 1, 0, 3).reshape(n, P, UNIT)


def _tiles(w):
    n = w.shape[1] // P
    return w.reshape(KD, P, n, P).transpose(2, 1, 0, 3).reshape(n, P, KD * P)


def _out_units(w):
    return w.reshape(KF, P, D // UC, UC).transpose(2, 1, 0, 3).reshape(D // UC, P, KF * UC)


def _fm(x):
    return x.T.reshape(KD, P, x.shape[0]).transpose(1, 0, 2)


def _cols(v):
    return v.reshape(-1, P).T


def _constants():
    f = np.float32
    j, i = np.arange(P)[:, None], np.arange(P)[None, :]
    same = j // CHUNK == i // CHUNK
    masks = np.stack([same & (j <= i), same & (j >= i)], 1).astype(f)
    reset = np.ones((P, T), f)
    reset[:, ::CHUNK] = 0
    inv_freq = (f(1) / (f(10000.0) ** (np.arange(0, P, 2, dtype=f) / f(P)))).astype(f)
    ang = (np.arange(T, dtype=f)[:, None] * inv_freq[None, :]).astype(f).T
    cos, sin = np.cos(ang), np.sin(ang)
    trig = np.stack([np.concatenate([cos, cos]), np.concatenate([sin, -sin])], 1).astype(f)
    lg = np.log1p(-np.exp2(-5.0 - np.arange(HR)))
    pos = np.arange(P)
    decay = np.zeros((P, 3, HR, P))
    for h in range(HR):
        decay[:, 0, h] = np.exp(lg[h] * (pos + 1))[None]
        decay[:, 1, h] = np.exp(lg[h] * (P - 1 - pos))[None] * P ** -0.5
        rel = pos[None, :] - pos[:, None]
        decay[:, 2, h] = np.where(rel >= 0, np.exp(lg[h] * np.maximum(rel, 0)), 0) * P ** -0.5
    pool_n = np.zeros((P, 4, 16))
    for g, w in enumerate(WINDOWS):
        pool_n[:, g] = w / np.minimum(np.arange(1, 17), w)
    return {"masks": masks, "reset": reset, "trig": trig, "decay": decay.astype(f), "pool_n": pool_n.astype(f),
            "ident": np.eye(P, dtype=f)}


def kernel(x, c, ctx, c_ctx, mod_w, mod_b, norm_g, ffn_w_in, ffn_w_out, gla_w_in, gla_w_gate, gla_b_gate,
           gla_norm_g, gla_w_out, ffn1_norm_2, ffn1_w1_2, ffn1_w3_2, ffn1_w2_2, mix_norm_2, w_in_2, pool_w_2,
           pool_scale_2, ret_norm_2, w_out_2, ffn2_norm_2, ffn2_w1_2, ffn2_w3_2, ffn2_w2_2, final_norm_2, **_unused):
    import concourse.bacc as bacc
    from concourse.bass_utils import run_bass_kernel_spmd

    f = np.float32
    w = np.asarray(gla_w_in)[0]
    q, k, v, r, lr = np.split(w, [512, 1024, 2048, 3072], axis=1)
    gate = np.zeros((2 * RANK, 2, HG * DK), f)
    for z in range(2):
        gate[z * RANK:(z + 1) * RANK, z] = np.asarray(gla_w_gate)[0, z]
    gate = np.tile(gate.reshape(2 * RANK, D), (4, 1))
    rank = np.tile(lr, (1, 4)).reshape(KD, P, P).transpose(1, 0, 2).reshape(P, D)
    mod = np.asarray(mod_w)[0]
    c2 = np.stack([_cols(np.asarray(c)[0]), _cols(np.asarray(c_ctx))], 2).reshape(P, 2 * KD)

    def pairs(w1, w3):
        u = np.stack([_units(w1), _units(w3)], 1)
        return u.reshape(-1, P, UNIT)

    ffn_in = np.asarray(ffn_w_in)[0]
    wi = np.asarray(w_in_2)[0]
    u2, q2, k2, v2, g2 = np.split(wi, 5, axis=1)
    arrays = {
        "cols": np.concatenate([c2, _cols(np.asarray(mod_b)[0]), _cols(np.asarray(norm_g)[0]),
                                _cols(np.asarray(gla_b_gate)[0]), _cols(np.asarray(gla_norm_g)[0]),
                                _cols(np.asarray(ffn1_norm_2)[0]), _cols(np.asarray(mix_norm_2)[0]),
                                _cols(np.asarray(pool_scale_2)[0]), _cols(np.asarray(ret_norm_2)[0]),
                                _cols(np.asarray(ffn2_norm_2)[0]), _cols(np.asarray(final_norm_2))], 1),
        "x_fm": _fm(np.asarray(x)[0]), "ctx_fm": _fm(np.asarray(ctx)[0]),
        "mod01": _units(mod[:, :2 * D]), "mod25": _tiles(mod[:, 2 * D:]),
        "gla_in": np.concatenate([_units(k), _units(q), _units(v), _units(r)]),
        "rank_w": np.stack([rank, gate], 1),
        "gla_out": _units(np.asarray(gla_w_out)[0]),
        "ffn0_in": pairs(ffn_in[:, :F], ffn_in[:, F:]), "ffn0_out": _out_units(np.asarray(ffn_w_out)[0]),
        "ffn1_in": pairs(np.asarray(ffn1_w1_2)[0], np.asarray(ffn1_w3_2)[0]),
        "ffn1_out": _out_units(np.asarray(ffn1_w2_2)[0]),
        "mix_in": np.concatenate([_units(u2), _units(k2), _units(q2), _units(v2), _units(g2)]),
        "pool_w": np.asarray(pool_w_2)[0].transpose(1, 0, 2),
        "mix_out": _units(np.asarray(w_out_2)[0]),
        "ffn2_in": pairs(np.asarray(ffn2_w1_2)[0], np.asarray(ffn2_w3_2)[0]),
        "ffn2_out": _out_units(np.asarray(ffn2_w2_2)[0]),
        **_constants(),
    }
    nc = bacc.Bacc("TRN2", target_bir_lowering=False, num_devices=1)
    aps, inputs = {}, {}
    for name, value in arrays.items():
        value = np.ascontiguousarray(value)
        inputs[f"in_{name}"] = value
        aps[name] = nc.dram_tensor(f"in_{name}", value.shape, mybir.dt.from_np(value.dtype), kind="ExternalInput").ap()
    aps["out"] = nc.dram_tensor("out_fm", (P, KD, T), F32, kind="ExternalOutput").ap()
    build(nc, aps)
    got = run_bass_kernel_spmd(nc, [inputs], core_ids=[0]).results[0]["out_fm"]
    return np.ascontiguousarray(got.transpose(2, 1, 0).reshape(1, T, D))
```

```python
from contextlib import ExitStack, contextmanager

import numpy as np

import concourse.bass as bass
from concourse import mybir

ALU = mybir.AluOpType
ACT = mybir.ActivationFunctionType
F32 = mybir.dt.float32
F32R = mybir.dt.float32r
U32 = mybir.dt.uint32

P = 128
D = 1024
T = 512
TC = 256
KD = D // P
F = 2816
KF = F // P
UC = 256
CPU = UC // P
UNIT = KD * UC
EPS = 1e-6

HG = 4
DK, DV = 128, 256
RANK = 16
CHUNK = 64
NCH = T // CHUNK
GATE_NORM = 16.0
PAIRS = T // P

HR = 4
RCH = T // P
WINDOWS = (2, 4, 8, 16)

OUT_PARTS = ((0, 6), (6, 12), (12, 17), (17, 22))

COLS = {}
_n = 0
for _name, _w in (("c", 2 * KD), ("mod_b", 6 * KD), ("norm_g", 4 * KD), ("b_gate", 2 * HG), ("gla_g", 2),
                  ("ffn1_g", KD), ("mix_g", KD), ("pool_scale", 4), ("ret_g", 4), ("ffn2_g", KD),
                  ("final_g", KD)):
    COLS[_name] = _n
    _n += _w
NCOLS = _n


GATE_ORDER = [d * HG + h for h in range(HG) for d in range(2)]

ROOT_BANKS = (4, 5, 6, 3)

FIRST_MODS = 4
LAG = 2


class Counts:

    def __init__(self, eng):
        self.eng, self.n, self.i, self.per = eng, {}, None, {}

    def expect(self, sem, more=1):
        self.n[sem] = self.n.get(sem, 0) + more

    def has(self, sem):
        return self.n.get(sem, 0) > 0

    def now(self, sem, back=0):
        value = self.n.get(sem, 0) - back
        assert value > 0, str(sem)
        if self.i is not None and self.per.get(sem, 0):
            value = self.i * self.per[sem] + value
        return value

    def next(self, sem, more=1):
        self.expect(sem, more)
        return self.now(sem)

    def upto(self, sem, value):
        self.n[sem] = max(value, self.n.get(sem, 0))
        return self.now(sem)

    @contextmanager
    def loop(self, turns, per):
        start = dict(self.n)
        with self.eng.Fori(0, turns) as i:
            self.i, self.per = i, per
            yield i
            self.i = None
        for sem, n in self.n.items():
            grown = n - start.get(sem, 0)
            assert grown == per.get(sem, 0), (str(sem), grown, per.get(sem, 0))
            self.n[sem] = start.get(sem, 0) + turns * grown
        self.per = {}


def build(nc, a):
    with ExitStack() as ctx:
        sems = {}

        def sem(name):
            if name not in sems:
                sems[name] = ctx.enter_context(nc.semaphore(name))
            return sems[name]

        top = [256]

        def place(name, shape, dtype=F32, at=None):
            size = int(np.prod(shape[1:])) * 4
            if at is None:
                at = top[0]
                top[0] += (size + 31) // 32 * 32
            assert at + size <= nc.sbuf_usable_end, (name, at, size)
            return nc.alloc_sbuf_tensor_at(name, shape, dtype, offset=at)

        def here(size):
            at = top[0]
            top[0] += size
            return at

        KB = 1024
        base = nc.sbuf_base
        top[0] = (base + 31) // 32 * 32
        w_raw = [place(f"w_raw{s}", [P, KD, UC]) for s in range(2)]
        w_hi = [place(f"w_hi{s}", [P, KD, UC], F32R) for s in range(2)]
        w_lo = [place(f"w_lo{s}", [P, KD, UC], F32R) for s in range(2)]
        mod_at = top[0]
        mod_raw = place("mod_raw", [P, KD, P])
        xT = place("xT", [P, KD, T])
        act_at = here(32 * KB)
        a_hi = place("a_hi", [P, KD, T], F32R, act_at)
        a_lo = place("a_lo", [P, KD, T], F32R, act_at + 16 * KB)
        y_ffn = place("y_ffn", [P, KD, T], F32, act_at)
        big = here(88 * KB)
        g_hi = place("g_hi", [P, KF, T], F32R, big)
        g_lo = place("g_lo", [P, KF, T], F32R, big + 44 * KB)
        mod_w = [place(f"mod_w{n}", [P, KD, UC], F32, at) for n, at in
                 enumerate([act_at + 8 * KB * n for n in range(4)] + [big + n * KB for n in (8, 16, 40, 56)])]
        mod_rows = place("mod_rows", [P, 4, T], F32, big + 80 * KB)
        kT = place("kT", [P, HG, T], F32, big)
        cT = place("cT", [P, KD, TC], F32, big)
        kcT = place("kcT", [P, HG, TC], F32, big + 8 * KB)
        vc = [place(f"vc{s}", [P, 2, DV], F32, big + (12 + 2 * s) * KB) for s in range(2)]
        qT = place("qT", [P, HG, T], F32, big + 16 * KB)
        v = place("v", [P, PAIRS, D], F32, big + 24 * KB)
        y_gla = place("y_gla", [P, KD, T], F32, big + 24 * KB)
        wr_hi = place("wr_hi", [P, KD, P], F32R, big + 24 * KB)
        wr_lo = place("wr_lo", [P, KD, P], F32R, big + 28 * KB)
        wg_hi = place("wg_hi", [P, D], F32R, big + 32 * KB)
        small_raw = place("small_raw", [P, 2, D], F32, big + 48 * KB)
        wg = place("wg", [P, D], F32R, big + 36 * KB)
        G = place("G", [P, 2 * HG, T], F32, big + 40 * KB)
        ke_tok = [place(f"ke_tok{n}", [P, PAIRS, DK], F32, big + (40 + 2 * n) * KB) for n in range(8)]
        o_sq = [place(f"o_sq{n}", [P, T], F32, big + (40 + 2 * n) * KB) for n in range(8)]
        Gc = place("Gc", [P, 2 * HG, TC], F32, big + 56 * KB)
        st = [place(f"st{d}", [P, PAIRS, P], F32, big + (56 + 2 * d) * KB) for d in range(2)]
        state = [place(f"state{s}", [P, DV], F32, big + (60 + s) * KB) for s in range(4)]
        hc_hi = place("hc_hi", [P, KD, TC], F32R, big + 64 * KB)
        hc_lo = place("hc_lo", [P, KD, TC], F32R, big + 72 * KB)
        sr = place("sr", [P, KD, T], F32, big + 64 * KB)
        cst = place("cst", [P, 2 * HG, DV], F32, big + 80 * KB)
        glr = place("glr", [P, T + TC], F32R, big + 82 * KB)
        m_hi = place("m_hi", [P, KD, T], F32R, big)
        m_lo = place("m_lo", [P, KD, T], F32R, big + 16 * KB)
        qr = place("qr", [P, HR, T], F32, big + 32 * KB)
        kr = place("kr", [P, HR, T], F32, big + 40 * KB)
        vr = place("vr", [P, RCH, HR * P], F32, big + 48 * KB)
        gr = place("gr", [P, HR, T], F32, big + 56 * KB)
        trig = place("trig", [P, 2, T], F32, big + 64 * KB)
        decay = place("decay", [P, 3, HR, P], F32, big + 68 * KB)
        pool_w = place("pool_w", [P, 4, P], F32, big + 74 * KB)
        pool_n = place("pool_n", [P, 4, 17], F32, big + 76 * KB)
        pool_u = [place(f"pool_u{s}", [P, T], F32, big + (77 + 2 * s) * KB) for s in range(4)]
        rstate = place("rstate", [P, 2, 3, P], F32, big + 85 * KB)
        ret_kt = [place(f"ret_kt{s}", [P, T], F32, mod_at + 2 * s * KB) for s in range(2)]
        ret_sq_t = [place(f"ret_sq_t{s}", [P, T], F32, big + (64 + 2 * s) * KB) for s in range(2)]
        tmp = [place(f"tmp{s}", [P, T]) for s in range(4)]
        col4 = place("col4", [P, 16])
        root4 = place("root4", [P, 16])
        power = place("power", [P, 16])
        dec_k = [[place(f"{x}0", [P, T]) for x in ("qd", "kd", "ke")],
                 [place(f"{x}1", [P, T], F32, big + (8 + 2 * j) * KB) for j, x in enumerate(("qd", "kd", "ke"))]]
        sq_sum, sq_pool = dec_k[0][0], dec_k[0][2]
        ret_q, ret_k, ret_p = ([tmp[j], dec_k[0][i]] for i, j in enumerate((0, 1, 3)))
        ends = [place(f"ends{s}", [P, NCH]) for s in range(2)]
        cols = place("cols", [P, NCOLS])
        mod = place("mod", [P, 6 * KD, 2])
        gain = place("gain", [P, 5, KD])
        end16 = place("end16", [P, HG])
        sc = place("sc", [P, KD, 2])
        ident = place("ident", [P, P])
        ones = place("ones", [P, P])
        masks = place("masks", [P, 2, P])
        reset_at = top[0]
        reset = place("reset", [P, T])
        one = place("one", [P, 1])
        roots = place("roots", [P, T], F32, reset_at)

        bank = [ctx.enter_context(nc.psum_tensor(f"bank{b}", [P, T], F32)) for b in range(8)]

        ready = [sem(f"bank_ready{b}") for b in range(8)]
        free = [sem(f"bank_free{b}") for b in range(8)]
        raw_loaded = [sem(f"raw_loaded{s}") for s in range(2)]
        hi_done = [sem(f"weight_hi_done{s}") for s in range(2)]
        lo_done = [sem(f"weight_lo_done{s}") for s in range(2)]
        unit_used = [sem(f"unit_used{s}") for s in range(2)]
        mod_w_loaded = [sem(f"mod_weights_loaded{n}") for n in range(8)]
        masks_loaded = sem("masks_loaded")
        rows_ready, rows_copied = sem("modulation_rows_ready"), sem("modulation_rows_copied")
        cols_ready = sem("modulation_columns_ready")
        mod_loaded, mod_used = sem("mod_tile_loaded"), sem("mod_tile_used")
        cols_loaded, x_loaded, c_loaded = sem("cols_loaded"), sem("x_loaded"), sem("context_loaded")
        rank_loaded, consts_loaded = sem("rank_weights_loaded"), sem("constants_loaded")
        mix_loaded, stored = sem("mix_constants_loaded"), sem("out_stored")
        const_set, silu_c_done, mods_done = sem("constants_set"), sem("silu_c_done"), sem("modulation_done")
        sq_streamed, sq_stream_used = sem("square_streamed"), sem("square_stream_used")
        streamed_sum = sem("streamed_square_summed")
        var_done, root_done, diag_done = sem("mean_square_done"), sem("inverse_root_done"), sem("diagonal_done")
        y_squared, sum_step = sem("y_squared"), sem("square_sum_step")
        y_scaled, x_added = sem("y_scaled"), sem("x_added")
        scaled, norm_hi, norm_lo = sem("norm_scaled"), sem("norm_hi_done"), sem("norm_lo_done")
        silu_done, prod_done, gate_hi, gated = sem("silu_done"), sem("product_done"), sem("gated_hi_done"), sem("gated_done")
        chunk_done, sq_done = sem("chunk_done"), sem("chunk_squared")
        pair_out = [sem(f"column_pair_out{j}") for j in range(2)]
        gate_scaled, up_scaled = sem("gate_scaled"), sem("up_scaled")
        roots_spread, roots_copied = sem("norm_roots_spread"), sem("norm_roots_copied")
        pool_step, ret_sums_done = sem("pool_step"), sem("retention_sums_done")
        pool_squared, gate_out = sem("pool_squared"), sem("retention_gate_scaled")
        rank_hi, rank_lo, glr_hi = sem("rank_hi_done"), sem("rank_lo_done"), sem("glr_hi_done")
        act_step, dve_step = sem("act_step"), sem("dve_step")
        abs_done, ln_done, log_gate, scanned = sem("abs_done"), sem("ln_done"), sem("log_gate_done"), sem("scan_done")
        ctx_exp, ctx_key, ctx_tok = sem("context_exp_done"), sem("context_key_done"), sem("context_key_turned")
        rest_done, exp_done, dec_done, ke_done = sem("rest_decay_done"), sem("exp_done"), sem("decayed_done"), sem("end_key_turned")
        silu_r, r_copied = sem("silu_r_done"), sem("r_copied")
        st_done, state_done = sem("masked_scores_done"), sem("state_done")
        state_used, forward_used = sem("state_used"), sem("forward_scan_used")
        o_squared, o_summed = sem("o_squared"), sem("o_squares_summed")
        u_copied, pooled, mixed_hi, mixed_lo = sem("pool_input_copied"), sem("pooled_done"), sem("mixed_hi_done"), sem("mixed_lo_done")
        roped, ret_in, ret_scores = sem("rotated"), sem("retention_operand_done"), sem("retention_scores_done")
        ktok_done, r_state, v_copied = sem("key_turned"), sem("retention_state_done"), sem("v_copied")
        gate_silu, ret_sq = sem("gate_silu_done"), sem("retention_squared")
        sums_ready, roots_ready = sem("square_sums_ready"), sem("roots_spread")
        glr_ready, gates_ready = sem("low_rank_ready"), sem("gates_ready")
        ctx_keys_ready, ctx_state_ready = sem("context_keys_ready"), sem("context_state_ready")
        scan_keys, scan_scores, kv_ready = sem("scan_keys_ready"), sem("scan_scores_ready"), sem("kv_ready")
        o_ready = sem("o_ready")
        silu_in, up_ready, out_ready = sem("ffn_gate_ready"), sem("ffn_up_ready"), sem("ffn_out_ready")
        proj_ready, pool_mapped, mix_out = sem("projection_ready"), sem("pool_mapped"), sem("mix_out_ready")
        ret_keys, ret_scored, ret_kv, ret_o_ready = (sem("retention_keys_ready"), sem("retention_scores_ready"),
                                                     sem("retention_kv_ready"), sem("retention_out_ready"))
        log_min, ctx_end, ret_o = sem("log_gate_min_done"), sem("context_end_done"), sem("retention_out_gated")
        out_done = sem("out_chunk_done")

        def col(name, j=0, n=1):
            return cols[:, COLS[name] + j:COLS[name] + j + n]

        def flat(t):
            return t[:].rearrange("p a b -> p (a b)")

        def spread(ap, axis, shape):
            return ap.unsqueeze(axis).to_broadcast(shape)

        def head_of(n):
            return n // 2, n % 2, (n % 2) * HG + n // 2

        def ends_at(d):
            return CHUNK - 1 if d == 0 else 0

        block = ctx.enter_context(nc.Block())

        @block.sync
        def _(sp):
            cnt = Counts(sp)
            sp.dma_start(cols[:], a["cols"]).then_inc(cols_loaded, 16)
            sp.dma_start(ident[:], a["ident"]).then_inc(consts_loaded, 16)

            def load(s, src, width=UNIT):
                sp.wait_ge(hi_done[s], cnt.next(hi_done[s]))
                sp.wait_ge(lo_done[s], cnt.next(lo_done[s]))
                sp.dma_start(flat(w_raw[s])[:, 0:width], src).then_inc(raw_loaded[s], 16)

            def load_tile(j):
                if j:
                    sp.wait_ge(mod_used, cnt.next(mod_used))
                sp.dma_start(flat(mod_raw), a["mod25"][j]).then_inc(mod_loaded, 16)

            for n in range(8):
                sp.dma_start(flat(mod_w[n]), a["mod01"][n]).then_inc(mod_w_loaded[n], 16)
                if n == FIRST_MODS - 1:
                    sp.dma_start(xT[:], a["x_fm"]).then_inc(x_loaded, 16)
                    sp.dma_start(cT[:], a["ctx_fm"]).then_inc(c_loaded, 16)
            sp.dma_start(flat(w_raw[0]), a["gla_in"][0]).then_inc(raw_loaded[0], 16)
            sp.dma_start(small_raw[:], a["rank_w"]).then_inc(rank_loaded, 16)
            sp.dma_start(flat(w_raw[1]), a["gla_in"][1]).then_inc(raw_loaded[1], 16)
            sp.dma_start(masks[:], a["masks"]).then_inc(masks_loaded, 16)
            sp.dma_start(reset[:], a["reset"]).then_inc(masks_loaded, 16)
            load_tile(0)
            for n in range(12):
                m = n + 2
                load(m % 2, a["gla_in"][m] if m < 12 else a["gla_out"][m - 12])
                load_tile(2 * n + 1)
                load_tile(2 * n + 2)
            for m in (14, 15):
                load(m % 2, a["gla_out"][m - 12])
            load_tile(25)

            def ffn(w_in, w_out, tiles=()):
                both = {x[s]: 1 for x in (hi_done, lo_done) for s in range(2)}
                for n in range(3):
                    load(n % 2, w_in[n])
                    if tiles:
                        load_tile(tiles[n])
                for j in tiles[3:]:
                    load_tile(j)
                with cnt.loop(F // UC - 2, both) as i:
                    for n in (3, 4):
                        load(n % 2, w_in[bass.ds(i * 2 + n, 1)].rearrange("u p w -> p (u w)"))
                load(1, w_in[2 * F // UC - 1])
                with cnt.loop(D // UC, {x: 2 for x in both}) as i:
                    for j, (k0, k1) in enumerate(OUT_PARTS):
                        src = w_out[bass.ds(i, 1), :, k0 * UC:k1 * UC].rearrange("u p w -> p (u w)")
                        load(j % 2, src, (k1 - k0) * UC)

            ffn(a["ffn0_in"], a["ffn0_out"], range(26, 32))
            ffn(a["ffn1_in"], a["ffn1_out"])
            for n in range(10):
                load(n % 2, a["mix_in"][n])
                if n == 1:
                    sp.wait_ge(pair_out[1], 6)
                    for dst, name in ((trig, "trig"), (decay, "decay"), (pool_w, "pool_w"), (pool_n, "pool_n")):
                        sp.dma_start(dst[:], a[name]).then_inc(mix_loaded, 16)
            for n in range(4):
                load(n % 2, a["mix_out"][n])
            ffn(a["ffn2_in"], a["ffn2_out"])
            for m in range(KD):
                sp.wait_ge(out_done, m + 1)
                sp.dma_start(a["out"][:, m], y_ffn[:, m]).then_inc(stored, 16)
            sp.wait_ge(stored, 16 * KD)

        @block.gpsimd
        def _(pool):
            cnt = Counts(pool)
            pool.wait_ge(const_set, 3)

            def inverse_root(n):
                pool.wait_ge(var_done, cnt.next(var_done))
                nc.gpsimd.tensor_tensor(root4[:, 0:n], col4[:, 0:n], power[:, 0:n], ALU.pow).then_inc(root_done, 1)

            def add_squares(j, chunks):
                for c in range(CPU):
                    if c == 0:
                        pool.wait_ge(chunk_done, cnt.next(chunk_done))
                    else:
                        pool.wait_ge(pair_out[j], cnt.next(pair_out[j]))
                    pool.wait_ge(sum_step, cnt.now(sum_step))
                    at = xT[:, chunks[c]]
                    if len(at.shape) == 3:
                        at = at.rearrange("p o t -> p (o t)")
                    nc.gpsimd.tensor_tensor(sq_pool[:], at, at, ALU.mult).then_inc(pool_squared, 1)
                    pool.wait_ge(pool_squared, cnt.next(pool_squared))
                    nc.gpsimd.tensor_tensor(sq_sum[:], sq_sum[:], sq_pool[:], ALU.add).then_inc(sum_step, 1)
                    cnt.expect(sum_step)

            for n in (4, 2, 16, 4):
                inverse_root(n)
            for m in range(KD):
                pool.wait_ge(sq_streamed, 2 * KD + m + 1)
                if m == 0:
                    nc.gpsimd.tensor_copy(sq_sum[:], tmp[0][:]).then_inc(streamed_sum, 1)
                else:
                    pool.wait_ge(streamed_sum, 2 * KD + m)
                    nc.gpsimd.tensor_tensor(sq_sum[:], sq_sum[:], tmp[m % 2][:], ALU.add).then_inc(streamed_sum, 1)
            inverse_root(4)
            inverse_root(4)
            for m in range(KD):
                pool.wait_ge(y_scaled, KD + m + 1)
                nc.gpsimd.tensor_tensor(xT[:, m], xT[:, m], y_ffn[:, m], ALU.add).then_inc(x_added, 1)
            inverse_root(4)
            cnt.expect(chunk_done, KD // 2)
            cnt.expect(sum_step, 2 * KD)
            for j in range(2):
                cnt.expect(pair_out[j], 4)
            with cnt.loop(2, {chunk_done: 2, pair_out[0]: 1, pair_out[1]: 1, sum_step: 4, pool_squared: 4}) as i:
                for j in range(2):
                    add_squares(j, [bass.ds(i * 4 + (2 * j + c), 1) for c in range(CPU)])
            inverse_root(4)

            def pooling(g):
                w = WINDOWS[g]
                pool.wait_ge(u_copied, g + 1)
                u = cur = pool_u[g]
                s, turn = 1, 0
                while s < w:
                    nxt = tmp[2 + turn]
                    nc.gpsimd.tensor_copy(nxt[:, 0:s], cur[:, 0:s])
                    nc.gpsimd.tensor_tensor(nxt[:, s:T], cur[:, s:T], cur[:, 0:T - s], ALU.add).then_inc(pool_step, 1)
                    pool.wait_ge(pool_step, cnt.next(pool_step))
                    cur, s, turn = nxt, 2 * s, 1 - turn
                for x, y, op in ((cur[:, 0:16], pool_n[:, g, 0:16], ALU.mult), (cur[:], pool_n[:, g, 16:17].to_broadcast([P, T]), ALU.mult)):
                    nc.gpsimd.tensor_tensor(x, x, y, op).then_inc(pool_step, 1)
                    pool.wait_ge(pool_step, cnt.next(pool_step))
                nc.gpsimd.tensor_tensor(u[:], cur[:], u[:], ALU.subtract).then_inc(pooled, 1)
                pool.wait_ge(pooled, cnt.next(pooled))

            pool.wait_ge(mix_loaded, 64)
            for g in range(4):
                pooling(g)
            inverse_root(HR * RCH)
            for n in range(4):
                add_squares(n % 2, (CPU * n, CPU * n + 1))
            inverse_root(4)
            inverse_root(4)

        @block.tensor
        def _(pe):
            cnt = Counts(pe)
            filled = [False] * 8

            def take(b):
                if filled[b]:
                    pe.wait_ge(free[b], cnt.next(free[b]))
                filled[b] = True

            def mm(out, lhs, rhs, first, last):
                return pe.matmul(out, lhs, rhs, start=first, stop=last, skip_group_check=True)

            def mm3(out, lhs, rhs, first, last):
                mm(out, lhs[0], rhs[0], first, False)
                mm(out, lhs[0], rhs[1], False, False)
                return mm(out, lhs[1], rhs[0], False, last)

            def weights(s, k, c):
                return w_hi[s][:, k, c * P:(c + 1) * P], w_lo[s][:, k, c * P:(c + 1) * P]

            def mod_tile(j):
                pe.wait_ge(mod_loaded, cnt.next(mod_loaded, 16))
                for k in range(KD):
                    m = mm(bank[7][:, j:j + 1], mod_raw[:, k], sc[:, k, 0:1], k == 0, k == KD - 1)
                m.then_inc(mod_used, 1)

            def unit(s, banks, acts, by_chunk=None, says=None, tile=None, roots_to=None, streamed=False):
                pe.wait_ge(lo_done[s], cnt.next(lo_done[s]))
                for b in banks:
                    take(b)
                order = [(k, c) for k in range(KD) for c in range(CPU)] if by_chunk else \
                        [(k, c) for c in range(CPU) for k in range(KD)]
                for k, c in order:
                    if by_chunk is norm_lo and c == 0:
                        pe.wait_ge(norm_lo, cnt.next(norm_lo))
                    if by_chunk is mixed_lo and c == 0 and k == KD - HR:
                        for h in range(HR):
                            broadcast(4 + h, T, tmp[h])
                    if by_chunk is mixed_lo and c == 0 and k >= KD - HR:
                        pe.wait_ge(mixed_lo, cnt.upto(mixed_lo, k + 1))
                    m = mm3(bank[banks[c]][:], weights(s, k, c), (acts[0][:, k], acts[1][:, k]), k == 0, k == KD - 1)
                    if k == KD - 1:
                        m.then_inc(says or ready[banks[c]], 1)
                    if tile is not None and order.index((k, c)) == KD - 1:
                        mod_tile(tile)
                    if roots_to is not None and order.index((k, c)) == KD - 1:
                        broadcast(roots_to, T, tmp[3], roots_spread)
                    if streamed and c == CPU - 1:
                        pe.wait_ge(sq_streamed, cnt.next(sq_streamed))
                        m = token_sums(5, 0, tmp[k % 2], T, k == 0, k == KD - 1)
                        m.then_inc(sq_stream_used if k < KD - 1 else sums_ready, 1)

            def token_sums(b, col0, src, n, first, last):
                for j in range(n // P):
                    m = mm(bank[b][:, col0 + j:col0 + j + 1], src[:, j * P:(j + 1) * P], ones[:, 0:1], first and j == 0, last)
                return m

            def broadcast(b, n, diag, says=roots_ready):
                pe.wait_ge(diag_done, cnt.next(diag_done))
                mm(bank[b][:, 0:n], ones[:], diag[:, 0:n], True, True).then_inc(says, 1)

            def stats_summed(b):
                token_sums(b, 0, sq_sum, T, True, True).then_inc(sums_ready, 1)
                broadcast(b, T, tmp[3])

            pe.wait_ge(const_set, 3)
            pe.wait_ge(consts_loaded, 16)
            pe.wait_ge(silu_c_done, 1)

            def mod_columns(b):
                pe.wait_ge(rows_copied, b + 1)
                for j in range(4 * b, 4 * b + 4):
                    m = mm(bank[7][:, 2 * j:2 * j + 2], mod_rows[0:2, b, (j % 4) * P:(j % 4 + 1) * P], ident[0:2, 0:2],
                           True, True)
                if b == 3:
                    m.then_inc(cols_ready, 1)

            for n in range(8):
                pe.wait_ge(mod_w_loaded[n], 16)
                for k in range(KD):
                    m = mm(bank[n // 2][0:2, (n % 2) * UC:(n % 2 + 1) * UC], sc[:, k], mod_w[n][:, k], k == 0, k == KD - 1)
                if n % 2:
                    m.then_inc(rows_ready, 1)
                elif n:
                    mod_columns(n // 2 - 1)
                if n == 5:
                    pe.wait_ge(streamed_sum, KD)
                    token_sums(6, 0, sq_sum, T, True, True).then_inc(sums_ready, 1)
                if n == 6:
                    pe.wait_ge(streamed_sum, 2 * KD)
                    token_sums(5, 0, dec_k[0][1], TC, True, True).then_inc(sums_ready, 1)
            broadcast(6, T, tmp[3])
            broadcast(5, TC, dec_k[0][2])
            mod_columns(3)
            def low_rank():
                pe.wait_ge(rank_lo, 1)
                for b, n, parts in ((3, T, (a_hi, a_lo)), (4, TC, (hc_hi, hc_lo))):
                    for k in range(KD):
                        if b == 4:
                            pe.wait_ge(norm_lo, cnt.next(norm_lo))
                        m = mm3(bank[b][:, 0:n], (wr_hi[:, k], wr_lo[:, k]), (parts[0][:, k], parts[1][:, k]), k == 0, k == KD - 1)
                    m.then_inc(glr_ready, 1)
                filled[3] = filled[4] = True

            def gla_unit(n, banks, cx):
                s = n % 2
                unit(s, banks, (a_hi, a_lo), norm_lo if n == 0 else None, tile=2 * n)
                if n == 0:
                    low_rank()
                if cx is not None:
                    take(cx)
                    for c in range(CPU):
                        for k in range(KD):
                            m = mm3(bank[cx][:, c * TC:(c + 1) * TC], weights(s, k, c), (hc_hi[:, k], hc_lo[:, k]),
                                    k == 0, k == KD - 1)
                    m.then_inc(ready[cx], 1)
                mod_tile(2 * n + 1)

            gla_unit(0, (0, 1), 2)
            pe.wait_ge(free[3], cnt.next(free[3]))
            pe.wait_ge(free[4], cnt.next(free[4]))
            filled[3] = filled[4] = False
            gla_unit(1, (3, 4), 5)
            pe.wait_ge(rank_lo, 3)

            def gates(i):
                g = GATE_ORDER[i]
                for part, c0, n in ((0, 0, T), (1, T, TC)):
                    x = 3 + 2 * part + i % 2
                    take(x)
                    filled[x] = False
                    if i >= 2:
                        pe.wait_ge(log_gate, cnt.upto(log_gate, 2 * (i - 2) + part + 1))
                    if part and i % 2 == 0 and i >= 4:
                        pe.wait_ge(ctx_tok, cnt.upto(ctx_tok, (i - 2) // 2))
                    mm(bank[x][:, 0:n], wg[:, g * P:(g + 1) * P], glr[:, c0:c0 + n], True, True).then_inc(gates_ready, 1)

            gates(0)
            gates(1)
            gla_unit(2, (0, 1), None)
            gates(2)
            gates(3)
            gla_unit(3, (0, 1), None)

            def context_keys(h):
                pe.wait_ge(ctx_key, cnt.next(ctx_key))
                pe.wait_ge(log_gate, cnt.upto(log_gate, 2 * (2 * h + 3) if h < 2 else 16))
                for j in range(4):
                    m = pe.transpose(bank[5][:, j * P:(j + 1) * P], dec_k[0][0][:, j * P:(j + 1) * P], ident[:])
                m.then_inc(ctx_keys_ready, 1)

            def v_unit(h):
                s = h % 2
                context_keys(h)
                if h < 2:
                    gates(4 + 2 * h)
                    gates(5 + 2 * h)
                pe.wait_ge(lo_done[s], cnt.next(lo_done[s]))
                for b, tiles, parts in ((0, (0, 1), (a_hi, a_lo)), (1, (2, 3), (a_hi, a_lo)), (2, (0, 1), (hc_hi, hc_lo))):
                    if b == 1:
                        mod_tile(8 + 2 * h)
                    take(b)
                    for j, t in enumerate(tiles):
                        for k in range(KD):
                            m = mm3(bank[b][:, j * DV:(j + 1) * DV],
                                    (parts[0][:, k, t * P:(t + 1) * P], parts[1][:, k, t * P:(t + 1) * P]),
                                    (w_hi[s][:, k], w_lo[s][:, k]), k == 0, k == KD - 1)
                    m.then_inc(ready[b], 1)
                mod_tile(9 + 2 * h)
                pe.wait_ge(ctx_tok, cnt.upto(ctx_tok, h + 1))
                take(2)
                filled[2] = False
                pe.wait_ge(log_gate, cnt.upto(log_gate, 12 if h == 0 else 16))
                take(6)
                for d in range(2):
                    for t in range(2):
                        m = mm(bank[6][:, d * DV:(d + 1) * DV], dec_k[0][1][:, (2 * d + t) * P:(2 * d + t + 1) * P],
                               vc[h % 2][:, t], t == 0, t == 1)
                m.then_inc(ctx_state_ready, 1)

            for h in range(HG):
                v_unit(h)
            for n in range(4):
                unit(n % 2, ((0, 1), (3, 4))[n % 2], (a_hi, a_lo), tile=16 + 2 * n)
                mod_tile(17 + 2 * n)
            filled[7] = True
            filled[3] = filled[4] = False

            def scores(n):
                qd, kd, ke = dec_k[n % 2]
                pe.wait_ge(dec_done, cnt.next(dec_done, 3))
                if n == 0:
                    pe.wait_ge(r_copied, cnt.next(r_copied))
                    cnt.expect(free[3])
                for t in range(PAIRS):
                    m = pe.transpose(bank[5][:, t * P:(t + 1) * P], ke[:, t * P:(t + 1) * P], ident[:])
                m.then_inc(scan_keys, 1)
                for t in range(PAIRS):
                    m = mm(bank[4][:, t * P:(t + 1) * P], kd[:, t * P:(t + 1) * P], qd[:, t * P:(t + 1) * P], True, True)
                m.then_inc(scan_scores, 1)

            def scan(n):
                h, d, g = head_of(n)
                order = range(NCH) if d == 0 else range(NCH)[::-1]
                ob = (2 * (h % 2), 2 * (h % 2) + 1)
                qd = dec_k[n % 2][0]

                def kv(j):
                    t, r = order[j] // 2, (order[j] % 2) * CHUNK
                    b = 6 + j % 2
                    mm(bank[b][:, 0:DV], ke_tok[g][r:r + CHUNK, t], v[r:r + CHUNK, t, h * DV:(h + 1) * DV],
                       True, True).then_inc(kv_ready, 1)

                def inter(j):
                    c = order[j]
                    for e in range(2):
                        w = state[(7 * n + j - 1) % 4][:, e * P:(e + 1) * P] if j else cst[:, 2 * h + d, e * P:(e + 1) * P]
                        m = mm(bank[ob[e]][:, c * CHUNK:(c + 1) * CHUNK], w, qd[:, c * CHUNK:(c + 1) * CHUNK],
                               False, d == 1 and j == NCH - 1)
                        if j == NCH - 1 and d == 1:
                            m.then_inc(o_ready, 1)
                    if j == NCH - 1 and d == 0:
                        m.then_inc(forward_used, 1)
                    elif 0 < j < NCH - 1:
                        m.then_inc(state_used, 1)

                pe.wait_ge(ke_done, cnt.next(ke_done))
                if n == 0:
                    take(6)
                    take(7)
                    filled[6] = filled[7] = False
                kv(0)
                kv(1)
                if d == 0:
                    for b in ob:
                        take(b)
                pe.wait_ge(st_done, cnt.next(st_done))
                for e in range(2):
                    for t in range(PAIRS):
                        mm(bank[ob[e]][:, t * P:(t + 1) * P], v[:, t, h * DV + e * P:h * DV + (e + 1) * P],
                           st[d][:, t], d == 0 and t == 0, False)
                inter(0)
                for j in range(2, NCH - 1):
                    pe.wait_ge(state_done, cnt.next(state_done))
                    kv(j)
                    inter(j - 1)
                pe.wait_ge(state_done, cnt.next(state_done))
                inter(NCH - 2)
                if n + 1 < 2 * HG:
                    scores(n + 1)
                pe.wait_ge(state_done, cnt.next(state_done))
                inter(NCH - 1)

            scores(0)
            for n in range(2 * HG):
                scan(n)
            pe.wait_ge(o_summed, cnt.next(o_summed, HG))
            for h in range(HG):
                m = token_sums(4, PAIRS * h, tmp[h], T, True, True)
            m.then_inc(sums_ready, 1)
            take(3)
            filled[3] = False
            mod_tile(24)
            for h in range(HG):
                broadcast(ROOT_BANKS[h], T, tmp[h])
            for n in range(4):
                unit(n % 2, ((0, 1), (2, 3))[n % 2], (a_hi, a_lo), norm_lo if n == 0 else None,
                     tile=24 + n if n else None)

            def double_norm():
                token_sums(6, 0, sq_sum, T, True, True).then_inc(sums_ready, 1)
                broadcast(6, T, tmp[3])
                mod_tile(29)
                mod_tile(30)
                pe.wait_ge(streamed_sum, 3 * KD)
                token_sums(5, 0, sq_sum, T, True, True).then_inc(sums_ready, 1)
                broadcast(5, T, tmp[3])

            mod_tile(28)
            pe.wait_ge(sum_step, cnt.next(sum_step, KD))
            for b in range(4):
                take(b)
                filled[b] = False
            double_norm()

            def ffn(scaled=True, streamed=False, final=False):
                gate_free, up_free = (gate_scaled, up_scaled) if scaled else (silu_done, gated)

                def group(first=False):
                    if cnt.has(gate_free):
                        pe.wait_ge(gate_free, cnt.now(gate_free))
                    tiles = first and not scaled
                    unit(0, (0, 1), (a_hi, a_lo), norm_lo if first else None, silu_in, streamed=first and streamed)
                    cnt.expect(gate_free, CPU)
                    if first and scaled and not streamed:
                        pe.wait_ge(sum_step, cnt.next(sum_step, KD))
                        token_sums(5, 0, sq_sum, T, True, True).then_inc(sums_ready, 1)
                    if cnt.has(up_free):
                        pe.wait_ge(up_free, cnt.now(up_free))
                    unit(1, (2, 3), (a_hi, a_lo), None, up_ready, roots_to=5 if first and scaled else None,
                         tile=31 if tiles else None)
                    cnt.expect(up_free, CPU)
                    if scaled:
                        cnt.expect(gated, CPU)
                    filled[0] = filled[1] = filled[2] = filled[3] = False

                def out_body():
                    for j in range(2):
                        pe.wait_ge(pair_out[j], cnt.now(pair_out[j]))
                        for q, (k0, k1) in enumerate(OUT_PARTS):
                            s = q % 2
                            pe.wait_ge(lo_done[s], cnt.next(lo_done[s]))
                            if k1 == KF:
                                pe.wait_ge(gated, cnt.now(gated))
                            for c in range(CPU):
                                b = 4 + 2 * j + c
                                for k in range(k0, k1):
                                    m = mm3(bank[b][:], weights(s, k - k0, c), (g_hi[:, k], g_lo[:, k]), k == 0, k == KF - 1)
                                if k1 == KF:
                                    m.then_inc(out_ready, 1)
                            if k1 < KF:
                                m.then_inc(unit_used[s], 1)
                        cnt.expect(pair_out[j])

                group(True)
                with cnt.loop(F // UC - 1, {lo_done[0]: 1, lo_done[1]: 1, gated: CPU, gate_free: CPU, up_free: CPU}):
                    group()
                pe.wait_ge(gated, cnt.now(gated, CPU))
                for j in range(2):
                    cnt.expect(pair_out[j])
                if final:
                    out_body()
                    out_body()
                else:
                    with cnt.loop(2, {lo_done[0]: 4, lo_done[1]: 4, pair_out[0]: 1, pair_out[1]: 1}):
                        out_body()

            def x_summed():
                pe.wait_ge(sum_step, cnt.next(sum_step, KD))
                stats_summed(6)

            ffn(scaled=False)
            x_summed()
            cnt.expect(sq_streamed, 3 * KD)
            ffn(streamed=True)

            for n in range(6):
                banks = ((0, 1), (2, 3))[n % 2]
                if n >= 2:
                    if n < 4:
                        pe.wait_ge(u_copied, cnt.upto(u_copied, CPU * (n - 1)))
                    else:
                        pe.wait_ge(roped, cnt.upto(roped, CPU * (n - 3)))
                unit(n % 2, banks, (a_hi, a_lo), norm_lo if n == 0 else None, proj_ready,
                     roots_to=6 if n == 1 else None)
                if n == 0:
                    pe.wait_ge(sum_step, cnt.next(sum_step, KD))
                    token_sums(6, 0, sq_sum, T, True, True).then_inc(sums_ready, 1)
                for b in banks:
                    filled[b] = False
            for n in range(2):
                pe.wait_ge(lo_done[n], cnt.next(lo_done[n]))
                pe.wait_ge(roped, cnt.upto(roped, CPU * (n + 3)))
                for b in (2 * n, 2 * n + 1):
                    for j in range(2):
                        t = 2 * (b % 2) + j
                        for k in range(KD):
                            m = mm3(bank[b][:, j * UC:(j + 1) * UC],
                                    (a_hi[:, k, t * P:(t + 1) * P], a_lo[:, k, t * P:(t + 1) * P]),
                                    (w_hi[n][:, k], w_lo[n][:, k]), k == 0, k == KD - 1)
                    m.then_inc(ready[b], 1)
            pe.wait_ge(mix_loaded, 64)

            def pool_map(g):
                pe.wait_ge(pooled, cnt.next(pooled))
                if g:
                    pe.wait_ge(mixed_lo, cnt.upto(mixed_lo, g))
                mm(bank[6][:], pool_w[:, g], pool_u[g][:], True, True).then_inc(pool_mapped, 1)

            def ret_scores_of(h):
                pe.wait_ge(ret_in, cnt.next(ret_in, 2))
                if h:
                    pe.wait_ge(ret_scores, cnt.upto(ret_scores, h))
                for t in range(RCH):
                    s = slice(t * P, (t + 1) * P)
                    m = mm(bank[4][:, s], kr[:, h, s], qr[:, h, s], True, True)
                m.then_inc(ret_scored, 1)
                if h:
                    pe.wait_ge(ktok_done, cnt.upto(ktok_done, h))
                for t in range(RCH):
                    m = pe.transpose(bank[5][:, t * P:(t + 1) * P], ret_k[h % 2][:, t * P:(t + 1) * P], ident[:])
                m.then_inc(ret_keys, 1)

            def ret_states_of(h):
                pe.wait_ge(ktok_done, cnt.upto(ktok_done, h + 1))
                if h:
                    pe.wait_ge(r_state, cnt.upto(r_state, 3 * h))
                for t in range(RCH - 1):
                    m = mm(bank[7][:, t * P:(t + 1) * P], ret_kt[h % 2][:, t * P:(t + 1) * P], vr[:, t, h * P:(h + 1) * P], True, True)
                m.then_inc(ret_kv, 1)

            def ret_out_of(h):
                b = h % 2
                if h >= 2:
                    pe.wait_ge(ret_o, cnt.upto(ret_o, h - 1))
                pe.wait_ge(ret_scores, cnt.upto(ret_scores, h + 1))
                for t in range(RCH):
                    s = slice(t * P, (t + 1) * P)
                    mm(bank[b][:, s], vr[:, t, h * P:(h + 1) * P], ret_p[h % 2][:, s], t == 0, False)
                for t in range(1, RCH):
                    s = slice(t * P, (t + 1) * P)
                    pe.wait_ge(r_state, cnt.upto(r_state, 3 * h + t))
                    m = mm(bank[b][:, s], rstate[:, h % 2, t - 1], ret_q[h % 2][:, s], False, t == RCH - 1)
                m.then_inc(ret_o_ready, 1)

            def ret_sums_of(h):
                pe.wait_ge(ret_sq, cnt.next(ret_sq))
                return token_sums(6, RCH * h, ret_sq_t[h % 2], T, True, True)

            pe.wait_ge(v_copied, cnt.next(v_copied, 8))
            filled[2] = filled[3] = False
            ret_scores_of(0)
            unit(0, (2, 3), (a_hi, a_lo), says=proj_ready)
            ret_states_of(0)
            pool_map(0)
            ret_scores_of(1)
            ret_out_of(0)
            pool_map(1)
            pe.wait_ge(gate_silu, cnt.next(gate_silu, CPU))
            filled[2] = filled[3] = False
            unit(1, (2, 3), (a_hi, a_lo), says=proj_ready)
            ret_states_of(1)
            pool_map(2)
            ret_scores_of(2)
            ret_out_of(1)
            pool_map(3)
            ret_states_of(2)
            ret_scores_of(3)
            ret_out_of(2)
            ret_states_of(3)
            pe.wait_ge(mixed_lo, cnt.upto(mixed_lo, 4))
            ret_sums_of(0).then_inc(ret_sums_done, 1)
            ret_sums_of(1).then_inc(ret_sums_done, 1)
            ret_out_of(3)
            ret_sums_of(2)
            ret_sums_of(3).then_inc(sums_ready, 1)
            pe.wait_ge(ret_o, cnt.upto(ret_o, HR))
            pe.wait_ge(gate_silu, cnt.next(gate_silu, CPU))

            base = [cnt.n.get(pair_out[j], 0) for j in range(2)]
            for n in range(4):
                for b in range(4):
                    filled[b] = False
                if n >= 2:
                    pe.wait_ge(pair_out[n % 2], cnt.upto(pair_out[n % 2], base[n % 2] + 1))
                unit(n % 2, ((0, 1), (2, 3))[n % 2], (m_hi, m_lo), mixed_lo if n == 0 else None, mix_out)
            for j in range(2):
                pe.wait_ge(pair_out[j], cnt.upto(pair_out[j], base[j] + 2))
            for b in range(4):
                filled[b] = False
            ffn(final=True)
            x_summed()

        @block.scalar
        def _(act):
            cnt = Counts(act)

            def split_hi(s):
                act.wait_ge(raw_loaded[s], cnt.next(raw_loaded[s], 16))
                nc.scalar.activation(flat(w_hi[s]), flat(w_raw[s]), ACT.Copy).then_inc(hi_done[s], 1)

            def stream_squares(src, n, summed=False):
                for m in range(KD):
                    if summed:
                        act.wait_ge(x_added, cnt.next(x_added))
                    if m >= 2:
                        act.wait_ge(streamed_sum, cnt.next(streamed_sum))
                    nc.scalar.activation(tmp[m % 2][:, 0:n], src[:, m], ACT.Square).then_inc(sq_streamed, 1)
                cnt.expect(streamed_sum, 2)

            def norm_his(dst, n, shift=None):
                for m in range(KD):
                    act.wait_ge(scaled, cnt.next(scaled))
                    if shift is None:
                        ins = nc.scalar.activation(dst[:, m], tmp[m % 2][:, 0:n], ACT.Copy)
                    else:
                        ins = nc.scalar.activation(dst[:, m], tmp[m % 2][:, 0:n], ACT.Identity, bias=shift(m))
                    ins.then_inc(norm_hi, 1)

            def copy_out(b, dst, s=None):
                act.wait_ge(ready[b], cnt.next(ready[b]))
                nc.scalar.activation(dst, bank[b][:], ACT.Copy).then_inc(s or free[b], 1)

            act.wait_ge(cols_loaded, 16)
            nc.scalar.activation(flat(sc), col("c", 0, 2 * KD), ACT.Silu).then_inc(silu_c_done, 1)
            def copy_rows(b):
                act.wait_ge(rows_ready, b + 1)
                nc.scalar.activation(mod_rows[0:2, b], bank[b][0:2, :], ACT.Copy).then_inc(rows_copied, 1)

            copy_rows(0)
            act.wait_ge(x_loaded, 16)
            stream_squares(xT, T)
            copy_rows(1)
            act.wait_ge(c_loaded, 16)
            act.wait_ge(streamed_sum, cnt.now(streamed_sum))
            stream_squares(cT, TC)
            copy_rows(2)
            split_hi(0)
            copy_rows(3)
            act.wait_ge(mods_done, cnt.next(mods_done))
            norm_his(a_hi, T, lambda m: mod[:, m, 0:1])
            act.wait_ge(rank_loaded, 16)
            nc.scalar.activation(flat(wr_hi), small_raw[:, 0], ACT.Copy).then_inc(rank_hi, 1)
            nc.scalar.activation(wg_hi[:], small_raw[:, 1], ACT.Copy).then_inc(rank_hi, 1)
            norm_his(hc_hi, TC, lambda m: mod[:, m, 1:2])
            split_hi(1)
            for b, c0, n in ((3, 0, T), (4, T, TC)):
                act.wait_ge(glr_ready, cnt.next(glr_ready))
                nc.scalar.activation(glr[:, c0:c0 + n], bank[b][:, 0:n], ACT.Copy).then_inc(glr_hi, 1)

            def gate_logs(i):
                g = GATE_ORDER[i]
                parts = [(part, tmp[2 * part + i % 2][:, 0:n]) for part, n in ((0, T), (1, TC))]
                for part, t in parts:
                    b = 3 + 2 * part + i % 2
                    act.wait_ge(gates_ready, cnt.next(gates_ready))
                    if i >= 2:
                        act.wait_ge(log_gate, cnt.upto(log_gate, 2 * (i - 2) + part + 1))
                    nc.scalar.activation(t, bank[b][:, 0:t.shape[-1]], ACT.Abs, bias=col("b_gate", g)).then_inc(abs_done, 1)
                    cnt.expect(abs_done)
                for part, t in parts:
                    act.wait_ge(abs_done, cnt.now(abs_done, 1 - part))
                    nc.scalar.activation(t, t, ACT.Exp, scale=-1.0).then_inc(act_step, 1)
                    cnt.expect(act_step)
                for part, t in parts:
                    act.wait_ge(act_step, cnt.now(act_step, 1 - part))
                    nc.scalar.activation(t, t, ACT.Ln, bias=one[:, 0:1]).then_inc(ln_done, 1)

            def context_decays(h):
                act.wait_ge(ctx_end, cnt.upto(ctx_end, h + 1))
                act.wait_ge(scanned, cnt.upto(scanned, 2 * (2 * h + 2)))
                nc.scalar.activation(dec_k[0][0][:, 0:TC], Gc[:, h], ACT.Exp, scale=-1.0 / GATE_NORM,
                                     bias=end16[:, h:h + 1]).then_inc(ctx_exp, 1)
                nc.scalar.activation(dec_k[0][0][:, TC + 1:2 * TC], Gc[:, HG + h, 0:TC - 1], ACT.Exp,
                                     scale=1.0 / GATE_NORM).then_inc(ctx_exp, 1)

            copy_out(0, kT[:, 0])
            copy_out(1, kT[:, 1])
            act.wait_ge(ready[2], cnt.next(ready[2]))
            split_hi(0)
            copy_out(3, kT[:, 2])
            copy_out(4, kT[:, 3])
            act.wait_ge(ready[5], cnt.next(ready[5]))
            split_hi(1)
            gate_logs(0)
            gate_logs(1)
            copy_out(0, qT[:, 0])
            copy_out(1, qT[:, 1])
            split_hi(0)
            gate_logs(2)
            gate_logs(3)
            context_decays(0)
            copy_out(0, qT[:, 2])
            copy_out(1, qT[:, 3])
            split_hi(1)
            for h in range(HG):
                act.wait_ge(ctx_keys_ready, cnt.next(ctx_keys_ready))
                if h:
                    act.wait_ge(ctx_state_ready, cnt.upto(ctx_state_ready, h))
                nc.scalar.activation(dec_k[0][1][:], bank[5][:], ACT.Copy).then_inc(ctx_tok, 1)
                if h + 1 < HG:
                    context_decays(h + 1)
                if h < 2:
                    gate_logs(4 + 2 * h)
                    gate_logs(5 + 2 * h)
                for b in range(2):
                    act.wait_ge(ready[b], cnt.next(ready[b]))
                    nc.scalar.activation(v[:, 2 * b:2 * b + 2, h * DV:(h + 1) * DV],
                                         bank[b][:].rearrange("p (t e) -> p t e", t=2), ACT.Copy).then_inc(free[b], 1)
                act.wait_ge(ready[2], cnt.next(ready[2]))
                split_hi(h % 2)

            def decays(n):
                h, d, g = head_of(n)
                qd, kd, ke = dec_k[n % 2]
                if n >= 2 and n % 2 == 0:
                    act.wait_ge(forward_used, cnt.next(forward_used))
                gate = G[:, g]
                act.wait_ge(rest_done, cnt.next(rest_done))
                nc.scalar.activation(ke[:], ke[:], ACT.Exp, scale=1.0 / GATE_NORM).then_inc(exp_done, 1)
                nc.scalar.activation(qd[:], gate, ACT.Exp, scale=1.0 / GATE_NORM).then_inc(exp_done, 1)
                nc.scalar.activation(kd[:], gate, ACT.Exp, scale=-1.0 / GATE_NORM).then_inc(exp_done, 1)
                nc.scalar.activation(ends[n % 2][:], gate.rearrange("p (c t) -> p c t", t=CHUNK)[:, :, ends_at(d)], ACT.Exp,
                                     scale=1.0 / GATE_NORM).then_inc(exp_done, 1)

            decays(0)
            for n in range(4):
                b = ((0, 1), (3, 4))[n % 2]
                for c in range(CPU):
                    copy_out(b[c], sr[:, CPU * n + c], r_copied if (n, c) == (3, 1) else None)
                split_hi(n % 2)
            def turned_keys(n):
                act.wait_ge(scan_keys, cnt.next(scan_keys))
                nc.scalar.activation(flat(ke_tok[head_of(n)[2]]), bank[5][:], ACT.Copy).then_inc(ke_done, 1)

            def o_squares(h):
                for e in range(2):
                    b = 2 * (h % 2) + e
                    act.wait_ge(o_ready, cnt.next(o_ready))
                    nc.scalar.activation(o_sq[h + HG * e][:], bank[b][:], ACT.Square).then_inc(o_squared, 1)

            turned_keys(0)
            act.wait_ge(r_copied, cnt.next(r_copied))
            nc.scalar.activation(flat(sr), flat(sr), ACT.Silu).then_inc(silu_r, 1)
            decays(1)
            for n in range(1, 2 * HG):
                turned_keys(n)
                if n >= 2 and n % 2 == 0:
                    o_squares(n // 2 - 1)
                if n + 1 < 2 * HG:
                    decays(n + 1)
            o_squares(HG - 1)
            for m in range(KD):
                act.wait_ge(scaled, cnt.next(scaled))
                nc.scalar.activation(a_hi[:, m], sr[:, m], ACT.Copy).then_inc(norm_hi, 1)
            for n in range(4):
                for c in range(CPU):
                    m = CPU * n + c
                    b = (0, 1, 2, 3)[m % 4]
                    act.wait_ge(ready[b], cnt.next(ready[b]))
                    if m >= 2:
                        act.wait_ge(sum_step, cnt.next(sum_step))
                    nc.scalar.activation(tmp[m % 2][:], bank[b][:], ACT.Square).then_inc(y_squared, 1)
                    nc.scalar.activation(y_gla[:, m], bank[b][:], ACT.Copy).then_inc(free[b], 1)
                if n < 3:
                    split_hi(n % 2)
            cnt.expect(sum_step, 2)

            def x_upper(gains):
                for m in range(KD):
                    done = pair_out[m // 2 % 2] if m % 2 else chunk_done
                    act.wait_ge(done, cnt.next(done))
                    nc.scalar.activation(a_hi[:, m], xT[:, m], ACT.Copy, scale=gains(m)).then_inc(norm_hi, 1)

            def copy_roots(b):
                act.wait_ge(roots_spread, cnt.next(roots_spread))
                nc.scalar.activation(roots[:], bank[b][:], ACT.Copy).then_inc(roots_copied, 1)

            def ffn(scaled=True, final=False):
                def group(first=False):
                    split_hi(1)
                    if first and scaled:
                        act.wait_ge(silu_in, cnt.next(silu_in, CPU))
                        split_hi(0)
                        copy_roots(5)
                    if not scaled and cnt.has(gated):
                        act.wait_ge(gated, cnt.now(gated))
                    for c in range(CPU):
                        if scaled:
                            act.wait_ge(gate_scaled, cnt.next(gate_scaled))
                            nc.scalar.activation(tmp[c][:], tmp[c][:], ACT.Silu).then_inc(silu_done, 1)
                        else:
                            act.wait_ge(silu_in, cnt.next(silu_in))
                            nc.scalar.activation(tmp[c][:], bank[c][:], ACT.Silu).then_inc(silu_done, 1)
                    if not (first and scaled):
                        split_hi(0)
                    act.wait_ge(up_ready, cnt.next(up_ready, CPU))
                    if not scaled:
                        cnt.expect(gated, CPU)

                def out_body(final=False):
                    for j in range(2):
                        split_hi(1)
                        act.wait_ge(unit_used[0], cnt.next(unit_used[0]))
                        split_hi(0)
                        act.wait_ge(unit_used[1], cnt.next(unit_used[1]))
                        split_hi(1)
                        if not (final and j == 1):
                            act.wait_ge(unit_used[0], cnt.next(unit_used[0]))
                            split_hi(0)
                            act.wait_ge(out_ready, cnt.next(out_ready, CPU))

                group(True)
                with cnt.loop(F // UC - 1, {raw_loaded[0]: 16, raw_loaded[1]: 16, up_ready: CPU,
                                            **({gate_scaled: CPU} if scaled else {silu_in: CPU, gated: CPU})}):
                    group()
                if final:
                    out_body()
                    out_body(True)
                else:
                    with cnt.loop(2, {raw_loaded[0]: 64, raw_loaded[1]: 64, unit_used[0]: 4, unit_used[1]: 2,
                                      out_ready: 2 * CPU}):
                        out_body()
                if scaled:
                    cnt.expect(silu_in, F // P - CPU)

            stream_squares(xT, T, True)
            norm_his(a_hi, T, lambda m: mod[:, 3 * KD + m, 0:1])
            ffn(scaled=False)
            for m in range(KD):
                act.wait_ge(x_added, cnt.next(x_added))
                nc.scalar.activation(a_hi[:, m], xT[:, m], ACT.Copy, scale=col("ffn1_g", m)).then_inc(norm_hi, 1)
                if m >= 2:
                    act.wait_ge(sq_stream_used, cnt.next(sq_stream_used))
                nc.scalar.activation(tmp[m % 2][:], xT[:, m], ACT.Square).then_inc(sq_streamed, 1)
            cnt.expect(sq_stream_used)
            ffn()
            cnt.expect(chunk_done, KD // 2)
            for j in range(2):
                cnt.expect(pair_out[j], 4)
            x_upper(lambda m: col("mix_g", m))
            split_hi(1)
            act.wait_ge(proj_ready, cnt.next(proj_ready, CPU))
            split_hi(0)
            copy_roots(6)
            act.wait_ge(proj_ready, cnt.next(proj_ready, CPU))
            split_hi(1)
            for n in range(2, 6):
                act.wait_ge(proj_ready, cnt.next(proj_ready, CPU))
                split_hi(n % 2)
            for n in range(2):
                for b in (2 * n, 2 * n + 1):
                    act.wait_ge(ready[b], cnt.next(ready[b]))
                    for j in range(2):
                        t = 2 * (b % 2) + j
                        nc.scalar.activation(vr[:, t, n * UC:(n + 1) * UC], bank[b][:, j * UC:(j + 1) * UC], ACT.Copy,
                                             scale=root4[:, t:t + 1]).then_inc(v_copied, 1)
                split_hi(n)
            def pool_upper(g):
                act.wait_ge(pool_mapped, cnt.next(pool_mapped))
                nc.scalar.activation(m_hi[:, g], bank[6][:], ACT.Copy, scale=col("pool_scale", g)).then_inc(mixed_hi, 1)

            def turned(h):
                act.wait_ge(ret_keys, cnt.next(ret_keys))
                nc.scalar.activation(ret_kt[h % 2][:], bank[5][:], ACT.Copy).then_inc(ktok_done, 1)

            def gate_unit(n):
                for c in range(CPU):
                    act.wait_ge(gate_out, cnt.next(gate_out))
                    g = gr[:, CPU * n + c]
                    nc.scalar.activation(g, g, ACT.Silu).then_inc(gate_silu, 1)
                pool_upper(2 * n)
                split_hi(n)

            def ret_square(h):
                act.wait_ge(ret_o_ready, cnt.next(ret_o_ready))
                nc.scalar.activation(ret_sq_t[h % 2][:], bank[h % 2][:], ACT.Square).then_inc(ret_sq, 1)

            turned(0)
            gate_unit(0)
            turned(1)
            ret_square(0)
            pool_upper(1)
            gate_unit(1)
            turned(2)
            ret_square(1)
            pool_upper(3)
            turned(3)
            act.wait_ge(ret_sums_done, 1)
            ret_square(2)
            act.wait_ge(ret_sums_done, 2)
            ret_square(3)
            for h in range(HR):
                act.wait_ge(scaled, cnt.next(scaled))
                nc.scalar.activation(m_hi[:, 4 + h], gr[:, h], ACT.Copy).then_inc(mixed_hi, 1)
            for n in range(4):
                act.wait_ge(mix_out, cnt.next(mix_out, CPU))
                if n < 3:
                    split_hi(n % 2)
            x_upper(lambda m: col("ffn2_g", m))
            for j in range(2):
                cnt.expect(pair_out[j])
            ffn(final=True)

        @block.vector
        def _(dve):
            cnt = Counts(dve)
            V = nc.vector

            def split_lo(s):
                dve.wait_ge(hi_done[s], cnt.next(hi_done[s]))
                V.tensor_tensor(flat(w_lo[s]), flat(w_raw[s]), flat(w_hi[s]).bitcast(F32), ALU.subtract).then_inc(lo_done[s], 1)

            def mean_square(b, n, width):
                dve.wait_ge(sums_ready, cnt.next(sums_ready))
                V.tensor_scalar(col4[:, 0:n], bank[b][:, 0:n], 1.0 / width, EPS, ALU.mult, ALU.add).then_inc(var_done, 1)

            def diagonal(dst, n, c0=0):
                V.tensor_tensor(dst[:, 0:n * P].rearrange("p (t q) -> p t q", q=P), spread(ident[:], 1, [P, n, P]),
                                spread(root4[:, c0:c0 + n], 2, [P, n, P]), ALU.mult).then_inc(diag_done, 1)

            def stats(b, diag, n=PAIRS):
                mean_square(b, n, D)
                dve.wait_ge(root_done, cnt.next(root_done))
                diagonal(diag, n)
                dve.wait_ge(roots_ready, cnt.next(roots_ready))

            def norm_parts(src, b, gains, n, hi, lo, shift=None):
                def lower(m):
                    dve.wait_ge(norm_hi, cnt.next(norm_hi))
                    t = tmp[m % 2][:, 0:n]
                    up = hi[:, m].bitcast(F32)
                    if shift is None:
                        V.tensor_tensor(lo[:, m], t, up, ALU.subtract).then_inc(norm_lo, 1)
                        cnt.expect(norm_lo)
                    else:
                        V.scalar_tensor_tensor(lo[:, m], t, shift(m), up, ALU.add, ALU.subtract).then_inc(norm_lo, 1)
                        cnt.expect(norm_lo)

                for m in range(KD):
                    if m >= 2:
                        dve.wait_ge(norm_lo, cnt.now(norm_lo))
                    V.scalar_tensor_tensor(tmp[m % 2][:, 0:n], src[:, m], gains(m), bank[b][:, 0:n], ALU.mult, ALU.mult).then_inc(scaled, 1)
                    cnt.expect(scaled)
                    if m:
                        lower(m - 1)
                lower(KD - 1)

            V.memset(power[:], -0.5).then_inc(const_set, 1)
            V.memset(one[:], 1.0).then_inc(const_set, 1)
            V.memset(ones[:], 1.0).then_inc(const_set, 1)
            for dst, n in ((sq_sum, T), (dec_k[0][1], TC)):
                V.memset(dst[:, 0:n], 0.0).then_inc(dve_step, 1)
                dve.wait_ge(dve_step, cnt.next(dve_step))
                for m in range(KD):
                    dve.wait_ge(sq_streamed, cnt.next(sq_streamed))
                    if m:
                        dve.wait_ge(streamed_sum, cnt.now(streamed_sum))
                    V.tensor_tensor(dst[:, 0:n], dst[:, 0:n], tmp[m % 2][:, 0:n], ALU.add).then_inc(streamed_sum, 1)
                    cnt.expect(streamed_sum)
            dve.wait_ge(consts_loaded, 16)
            mean_square(6, PAIRS, D)
            dve.wait_ge(root_done, cnt.next(root_done))
            diagonal(tmp[3], PAIRS)
            split_lo(0)
            mean_square(5, 2, D)
            dve.wait_ge(root_done, cnt.next(root_done))
            diagonal(dec_k[0][2], 2)
            dve.wait_ge(roots_ready, cnt.next(roots_ready, 2))
            dve.wait_ge(cols_loaded, 16)
            dve.wait_ge(cols_ready, 1)
            V.tensor_tensor(mod[:, 0:2 * KD], bank[7][:, 0:4 * KD].rearrange("p (j v) -> p j v", v=2),
                            spread(col("mod_b", 0, 2 * KD), 2, [P, 2 * KD, 2]), ALU.add).then_inc(dve_step, 1)
            dve.wait_ge(dve_step, cnt.next(dve_step))
            for u in range(2):
                V.scalar_tensor_tensor(gain[:, u], mod[:, KD:2 * KD, u], 1.0, col("norm_g", 0, KD), ALU.add, ALU.mult).then_inc(mods_done, 1)
                cnt.expect(mods_done)
            dve.wait_ge(mods_done, cnt.now(mods_done))
            norm_parts(xT, 6, lambda m: gain[:, 0, m:m + 1], T, a_hi, a_lo, lambda m: mod[:, m, 0:1])
            dve.wait_ge(norm_lo, cnt.now(norm_lo))
            dve.wait_ge(rank_hi, cnt.next(rank_hi))
            V.tensor_tensor(flat(wr_lo), small_raw[:, 0], flat(wr_hi).bitcast(F32), ALU.subtract).then_inc(rank_lo, 1)
            dve.wait_ge(rank_hi, cnt.next(rank_hi))
            V.tensor_copy(wg[0:64, :], wg_hi[0:64, :].bitcast(F32)).then_inc(rank_lo, 1)
            V.tensor_tensor(wg[64:128, :], small_raw[64:128, 1], wg_hi[64:128, :].bitcast(F32), ALU.subtract).then_inc(rank_lo, 1)
            norm_parts(cT, 5, lambda m: gain[:, 1, m:m + 1], TC, hc_hi, hc_lo, lambda m: mod[:, m, 1:2])
            split_lo(1)
            for b, c0, n in ((3, 0, T), (4, T, TC)):
                dve.wait_ge(glr_hi, cnt.next(glr_hi))
                for r in (32, 96):
                    g = glr[r:r + 32, c0:c0 + n]
                    ins = V.tensor_tensor(g, bank[b][r:r + 32, 0:n], g.bitcast(F32), ALU.subtract)
                ins.then_inc(free[b], 1)
            dve.wait_ge(ready[2], cnt.next(ready[2]))
            V.tensor_copy(kcT[:, 0:2].rearrange("p a b -> p (a b)"), bank[2][:]).then_inc(free[2], 1)
            split_lo(0)
            dve.wait_ge(ready[5], cnt.next(ready[5]))
            V.tensor_copy(kcT[:, 2:4].rearrange("p a b -> p (a b)"), bank[5][:]).then_inc(free[5], 1)
            split_lo(1)
            dve.wait_ge(masks_loaded, 32)

            def log_gates(i):
                g = GATE_ORDER[i]
                parts = ((G, 0, T), (Gc, 1, TC))
                for dst, part, n in parts:
                    dve.wait_ge(abs_done, cnt.next(abs_done))
                    V.tensor_scalar(dst[:, g], bank[3 + 2 * part + i % 2][:, 0:n], col("b_gate", g), 0.0, ALU.add, ALU.min).then_inc(log_min, 1)
                    cnt.expect(log_min)
                for dst, part, n in parts:
                    dve.wait_ge(ln_done, cnt.next(ln_done))
                    dve.wait_ge(log_min, cnt.now(log_min, 1 - part))
                    V.tensor_tensor(dst[:, g], dst[:, g], tmp[2 * part + i % 2][:, 0:n], ALU.subtract).then_inc(log_gate, 1)
                    cnt.expect(log_gate)
                for dst, part, n in parts:
                    dve.wait_ge(log_gate, cnt.now(log_gate, 1 - part))
                    x = dst[:, g, ::-1] if part == 0 and g >= HG else dst[:, g]
                    keep = reset[:] if part == 0 else one[:, 0:1].to_broadcast([P, n])
                    V.tensor_tensor_scan(x, keep, x, 0.0, ALU.mult, ALU.add).then_inc(scanned, 1)
                    cnt.expect(scanned)
                if g < HG:
                    dve.wait_ge(scanned, cnt.now(scanned))
                    V.tensor_scalar(end16[:, g:g + 1], Gc[:, g, TC - 1:TC], 1.0 / GATE_NORM, None, ALU.mult).then_inc(ctx_end, 1)

            def context_key(h):
                dve.wait_ge(ctx_exp, cnt.next(ctx_exp, 2))
                V.memset(dec_k[0][0][:, TC:TC + 1], 1.0).then_inc(dve_step, 1)
                dve.wait_ge(dve_step, cnt.next(dve_step))
                e = dec_k[0][0][:].rearrange("p (d t) -> p d t", d=2)
                V.tensor_tensor(e, e, spread(kcT[:, h], 1, [P, 2, TC]), ALU.mult).then_inc(ctx_key, 1)

            log_gates(0)
            log_gates(1)
            split_lo(0)
            log_gates(2)
            log_gates(3)
            context_key(0)
            split_lo(1)
            for h in range(HG):
                if h + 1 < HG:
                    context_key(h + 1)
                if h < 2:
                    log_gates(4 + 2 * h)
                    log_gates(5 + 2 * h)
                dve.wait_ge(ready[2], cnt.next(ready[2]))
                V.tensor_copy(flat(vc[h % 2]), bank[2][:]).then_inc(free[2], 1)
                split_lo(h % 2)
                dve.wait_ge(ctx_state_ready, cnt.next(ctx_state_ready))
                V.tensor_copy(cst[:, 2 * h:2 * h + 2].rearrange("p a b -> p (a b)"), bank[6][:]).then_inc(free[6], 1)

            def rest(n):
                h, d, g = head_of(n)
                gate = G[:, g].rearrange("p (c t) -> p c t", t=CHUNK)
                j = ends_at(d)
                V.tensor_tensor(dec_k[n % 2][2][:].rearrange("p (c t) -> p c t", t=CHUNK),
                                gate[:, :, j:j + 1].to_broadcast([P, NCH, CHUNK]), gate, ALU.subtract).then_inc(rest_done, 1)

            def decayed(n, j):
                h = n // 2
                qd, kd, ke = dec_k[n % 2]
                dve.wait_ge(exp_done, cnt.next(exp_done))
                if j == 0:
                    V.tensor_tensor(ke[:], ke[:], kT[:, h], ALU.mult).then_inc(dec_done, 1)
                elif j == 1:
                    V.scalar_tensor_tensor(qd[:], qd[:], DK ** -0.5, qT[:, h], ALU.mult, ALU.mult).then_inc(dec_done, 1)
                else:
                    V.tensor_tensor(kd[:], kd[:], kT[:, h], ALU.mult).then_inc(dec_done, 1)
                    dve.wait_ge(exp_done, cnt.next(exp_done))

            def gate_o(h):
                dve.wait_ge(silu_r, 1)
                for e in range(2):
                    dve.wait_ge(o_squared, cnt.next(o_squared))
                    m = 2 * h + e
                    V.scalar_tensor_tensor(sr[:, m], bank[2 * (h % 2) + e][:], col("gla_g", e), sr[:, m],
                                           ALU.mult, ALU.mult).then_inc(free[2 * (h % 2) + e], 1)
                V.tensor_tensor(tmp[h][:], o_sq[h][:], o_sq[HG + h][:], ALU.add).then_inc(o_summed, 1)

            for d in range(2):
                V.memset(flat(st[d]), 0.0).then_inc(dve_step, 1)
                dve.wait_ge(dve_step, cnt.next(dve_step))
            rest(0)
            rest(1)
            for j in range(3):
                decayed(0, j)
            for n in range(4):
                split_lo(n % 2)
            dve.wait_ge(mod_used, cnt.next(mod_used, 3 * KD))
            V.tensor_tensor(mod[:, 2 * KD:5 * KD, 0], bank[7][:, 0:3 * KD], col("mod_b", 2 * KD, 3 * KD), ALU.add).then_inc(free[7], 1)
            cnt.expect(free[7])
            dve.wait_ge(free[7], cnt.now(free[7]))
            V.tensor_tensor(gain[:, 2], mod[:, 2 * KD:3 * KD, 0], col("norm_g", KD, KD), ALU.mult)
            V.scalar_tensor_tensor(gain[:, 3], mod[:, 4 * KD:5 * KD, 0], 1.0, col("norm_g", 2 * KD, KD), ALU.add, ALU.mult).then_inc(dve_step, 1)
            dve.wait_ge(dve_step, cnt.next(dve_step))
            def scan(n):
                h, d, g = head_of(n)
                order = range(NCH) if d == 0 else range(NCH)[::-1]
                dve.wait_ge(scan_scores, cnt.next(scan_scores))
                V.copy_predicated(st[d][:], spread(masks[:, d].bitcast(U32), 1, [P, PAIRS, P]),
                                  bank[4][:].rearrange("p (t q) -> p t q", q=P)).then_inc(st_done, 1)
                for j in range(NCH - 1):
                    w = 7 * n + j
                    dve.wait_ge(kv_ready, cnt.next(kv_ready))
                    if j:
                        dve.wait_ge(state_done, cnt.now(state_done))
                    if w >= 4:
                        q, r = divmod(w - 4, 7)
                        dve.wait_ge(state_used, cnt.upto(state_used, 6 * q + r + 1))
                    prev = state[(w - 1) % 4][:] if j else cst[:, n]
                    c = order[j]
                    V.scalar_tensor_tensor(state[w % 4][:], prev, ends[n % 2][:, c:c + 1], bank[6 + j % 2][:, 0:DV],
                                           ALU.mult, ALU.add).then_inc(state_done, 1)
                    cnt.expect(state_done)
                    if j == 0 and n >= 2 and n % 2 == 0:
                        gate_o(n // 2 - 1)
                    elif 2 <= j < 5 and n + 1 < 2 * HG:
                        decayed(n + 1, j - 2)
                    elif j == 5 and n + 2 < 2 * HG:
                        rest(n + 2)

            for n in range(2 * HG):
                scan(n)
            gate_o(HG - 1)
            mean_square(4, HG * PAIRS, DV)
            dve.wait_ge(root_done, cnt.next(root_done))
            for h in range(HG):
                diagonal(tmp[h], PAIRS, PAIRS * h)

            def lower_o(m):
                dve.wait_ge(norm_hi, cnt.next(norm_hi))
                V.tensor_tensor(a_lo[:, m], sr[:, m], a_hi[:, m].bitcast(F32), ALU.subtract).then_inc(norm_lo, 1)
                cnt.expect(norm_lo)

            for m in range(KD):
                if m % 2 == 0:
                    dve.wait_ge(roots_ready, cnt.next(roots_ready))
                V.tensor_tensor(sr[:, m], sr[:, m], bank[ROOT_BANKS[m // 2]][:], ALU.mult).then_inc(scaled, 1)
                cnt.expect(scaled)
                if m:
                    lower_o(m - 1)
            lower_o(KD - 1)
            V.memset(sq_sum[:], 0.0).then_inc(dve_step, 1)
            dve.wait_ge(dve_step, cnt.next(dve_step))
            for n in range(4):
                for c in range(CPU):
                    dve.wait_ge(y_squared, cnt.next(y_squared))
                    if cnt.has(sum_step):
                        dve.wait_ge(sum_step, cnt.now(sum_step))
                    V.tensor_tensor(sq_sum[:], sq_sum[:], tmp[c][:], ALU.add).then_inc(sum_step, 1)
                    cnt.expect(sum_step)
                if n < 3:
                    split_lo(n % 2)
            def double_norm(y, c, gains, shift=None):
                stats(6, tmp[3])
                for m in range(KD + 1):
                    if m < KD:
                        V.scalar_tensor_tensor(y[:, m], y[:, m], gain[:, c, m:m + 1], bank[6][:], ALU.mult, ALU.mult).then_inc(y_scaled, 1)
                        cnt.expect(y_scaled)
                    if m:
                        dve.wait_ge(y_scaled, cnt.now(y_scaled, 1 if m < KD else 0))
                        V.tensor_tensor(xT[:, m - 1], xT[:, m - 1], y[:, m - 1], ALU.add).then_inc(x_added, 1)
                stats(5, tmp[3])
                norm_parts(xT, 5, gains, T, a_hi, a_lo, shift)

            def x_lower(m, gains):
                dve.wait_ge(norm_hi, cnt.next(norm_hi))
                V.scalar_tensor_tensor(a_lo[:, m], xT[:, m], gains(m), a_hi[:, m].bitcast(F32),
                                       ALU.mult, ALU.subtract).then_inc(norm_lo, 1)
                cnt.expect(norm_lo)

            def x_roots(b):
                mean_square(b, PAIRS, D)
                dve.wait_ge(root_done, cnt.next(root_done))
                diagonal(tmp[3], PAIRS)
                split_lo(0)
                dve.wait_ge(roots_copied, cnt.next(roots_copied))

            def sum_pair(banks, chunks, half, to_x, j, squares):
                dst = xT if to_x else y_ffn
                at = [dst[:, chunks[c]] for c in range(CPU)]
                if len(at[0].shape) == 3:
                    at = [x.rearrange("p o t -> p (o t)") for x in at]
                for c in range(CPU):
                    out = pair_out[j] if c else chunk_done
                    if half:
                        dve.wait_ge(out_ready, cnt.next(out_ready))
                    else:
                        dve.wait_ge(mix_out, cnt.next(mix_out))
                    b = bank[banks[c]][:]
                    if not to_x:
                        V.tensor_scalar(at[c], b, 1.0, None, ALU.mult).then_inc(out, 1)
                    else:
                        V.scalar_tensor_tensor(at[c], b, 0.5 if half else 1.0, at[c], ALU.mult, ALU.add).then_inc(out, 1)
                    cnt.expect(out)
                    if squares:
                        dve.wait_ge(out, cnt.now(out))
                        dve.wait_ge(sum_step, cnt.now(sum_step))
                        V.tensor_tensor(tmp[c][:], at[c], at[c], ALU.mult).then_inc(sq_done, 1)
                        dve.wait_ge(sq_done, cnt.next(sq_done))
                        V.tensor_tensor(sq_sum[:], sq_sum[:], tmp[c][:], ALU.add).then_inc(sum_step, 1)
                    cnt.expect(sum_step)

            def ffn(to_x, scaled=True, last_ffn=False):
                def group(m0, first=False):
                    split_lo(1)
                    if first and scaled:
                        x_roots(5)
                    if scaled:
                        for c in range(CPU):
                            dve.wait_ge(silu_in, cnt.next(silu_in))
                            if cnt.has(gated):
                                dve.wait_ge(gated, cnt.now(gated))
                            V.tensor_tensor(tmp[c][:], bank[c][:], roots[:], ALU.mult).then_inc(gate_scaled, 1)
                    if not (first and scaled):
                        split_lo(0)
                    for c in range(CPU):
                        dve.wait_ge(up_ready, cnt.next(up_ready))
                        if scaled:
                            V.tensor_tensor(tmp[2 + c][:], bank[2 + c][:], roots[:], ALU.mult).then_inc(up_scaled, 1)
                            cnt.expect(up_scaled)
                        else:
                            cnt.expect(silu_in)
                            dve.wait_ge(silu_done, cnt.next(silu_done))
                            if cnt.has(gated):
                                dve.wait_ge(gated, cnt.now(gated, 1 - c))
                            V.tensor_tensor(tmp[2 + c][:], tmp[c][:], bank[2 + c][:], ALU.mult).then_inc(prod_done, 1)
                            cnt.expect(prod_done)
                            V.tensor_tensor(hidden(g_hi, m0, c), tmp[c][:], bank[2 + c][:], ALU.mult).then_inc(gate_hi, 1)
                            cnt.expect(gate_hi)
                    if scaled:
                        for c in range(CPU):
                            dve.wait_ge(silu_done, cnt.next(silu_done))
                            dve.wait_ge(up_scaled, cnt.now(up_scaled, 1 - c))
                            V.tensor_tensor(tmp[2 + c][:], tmp[2 + c][:], tmp[c][:], ALU.mult).then_inc(prod_done, 1)
                            cnt.expect(prod_done)
                        for c in range(CPU):
                            dve.wait_ge(prod_done, cnt.now(prod_done, 1 - c))
                            V.tensor_scalar(hidden(g_hi, m0, c), tmp[2 + c][:], 1.0, None, ALU.mult).then_inc(gate_hi, 1)
                            cnt.expect(gate_hi)
                    for c in range(CPU):
                        dve.wait_ge(prod_done, cnt.now(prod_done, 1 - c))
                        dve.wait_ge(gate_hi, cnt.now(gate_hi, 1 - c))
                        V.tensor_tensor(hidden(g_lo, m0, c), tmp[2 + c][:], hidden(g_hi, m0, c).bitcast(F32), ALU.subtract).then_inc(gated, 1)
                        cnt.expect(gated)

                def out_body(i, final=False):
                    for j in range(2):
                        split_lo(1)
                        split_lo(0)
                        split_lo(1)
                        if not (final and j == 1):
                            split_lo(0)
                        chunks = [bass.ds(i * 4 + (2 * j + c), 1) if not isinstance(i, int) else 4 * i + 2 * j + c for c in range(CPU)]
                        sum_pair((4 + 2 * j, 5 + 2 * j), chunks, True, to_x, j, last_ffn or not to_x)

                def hidden(t, m0, c):
                    if isinstance(m0, int):
                        return t[:, m0 + c]
                    return t[:, bass.ds(m0 * CPU + (CPU + c), 1)].rearrange("p o t -> p (o t)")

                group(0, True)
                if not scaled:
                    dve.wait_ge(mod_used, cnt.next(mod_used, KD))
                    V.tensor_tensor(mod[:, 5 * KD:, 0], bank[7][:, 3 * KD:4 * KD], col("mod_b", 5 * KD, KD), ALU.add).then_inc(dve_step, 1)
                    dve.wait_ge(dve_step, cnt.next(dve_step))
                    V.tensor_tensor(gain[:, 4], mod[:, 5 * KD:, 0], col("norm_g", 3 * KD, KD), ALU.mult).then_inc(dve_step, 1)
                    dve.wait_ge(dve_step, cnt.next(dve_step))
                for j in range(2):
                    V.memset(sq_sum[:, j * (T // 2):(j + 1) * (T // 2)], 0.0).then_inc(pair_out[j], 1)
                    cnt.expect(pair_out[j])
                with cnt.loop(F // UC - 1, {hi_done[0]: 1, hi_done[1]: 1, up_ready: CPU, silu_done: CPU,
                                            prod_done: CPU, gate_hi: CPU, gated: CPU, silu_in: CPU,
                                            **({up_scaled: CPU} if scaled else {})}) as i:
                    group(i)
                dve.wait_ge(gated, cnt.now(gated))
                if last_ffn:
                    out_body(0)
                    out_body(1, True)
                else:
                    with cnt.loop(2, {hi_done[0]: 4, hi_done[1]: 4, out_ready: 2 * CPU, chunk_done: 2,
                                      sum_step: 2 * CPU, pair_out[0]: 1, pair_out[1]: 1,
                                      **({} if to_x else {sq_done: 2 * CPU})}) as i:
                        out_body(i)

            double_norm(y_gla, 2, lambda m: gain[:, 3, m:m + 1], lambda m: mod[:, 3 * KD + m, 0:1])
            ffn(False, scaled=False)
            stats(6, tmp[3])
            for m in range(KD + LAG):
                if m < KD:
                    V.scalar_tensor_tensor(y_ffn[:, m], y_ffn[:, m], gain[:, 4, m:m + 1], bank[6][:],
                                           ALU.mult, ALU.mult).then_inc(y_scaled, 1)
                if m >= LAG:
                    x_lower(m - LAG, lambda m: col("ffn1_g", m))
            ffn(True)
            for m in range(KD):
                x_lower(m, lambda m: col("mix_g", m))
            split_lo(1)
            x_roots(6)

            def pool_input(n):
                for c in range(CPU):
                    b = CPU * n + c
                    dve.wait_ge(proj_ready, cnt.next(proj_ready))
                    V.tensor_tensor(pool_u[b][:], bank[b][:], roots[:], ALU.mult).then_inc(u_copied, 1)

            def rotate(n):
                dst = kr if n < 4 else qr
                for c in range(CPU):
                    b = bank[2 * (n % 2) + c]
                    t = tmp[c]
                    h = CPU * (n % 2) + c
                    dve.wait_ge(proj_ready, cnt.next(proj_ready))
                    if cnt.has(roped):
                        dve.wait_ge(roped, cnt.now(roped, 1 if c == 0 else 0))
                    V.tensor_tensor(t[0:64, :], b[64:128, :], trig[64:128, 1], ALU.mult)
                    V.tensor_tensor(t[64:128, :], b[0:64, :], trig[0:64, 1], ALU.mult)
                    V.tensor_tensor(dst[:, h], b[:], trig[:, 0], ALU.mult).then_inc(dve_step, 1)
                    dve.wait_ge(dve_step, cnt.next(dve_step))
                    V.tensor_tensor(dst[:, h], dst[:, h], t[:], ALU.add).then_inc(roped, 1)
                    cnt.expect(roped)

            pool_input(0)
            pool_input(1)
            split_lo(1)
            dve.wait_ge(mix_loaded, 64)
            V.tensor_tensor(trig[:], trig[:], spread(roots[:], 1, [P, 2, T]), ALU.mult).then_inc(dve_step, 1)
            dve.wait_ge(dve_step, cnt.next(dve_step))
            split_lo(0)
            rotate(2)
            split_lo(1)
            rotate(3)
            split_lo(0)
            rotate(4)
            split_lo(1)
            rotate(5)
            split_lo(0)
            dve.wait_ge(roped, cnt.now(roped))

            def ret_inputs(h):
                for out, x, r in ((ret_q[h % 2], qr, 0), (ret_k[h % 2], kr, 1)):
                    V.tensor_tensor(out[:].rearrange("p (t q) -> p t q", q=P), x[:, h].rearrange("p (t q) -> p t q", q=P),
                                    spread(decay[:, r, h], 1, [P, RCH, P]), ALU.mult).then_inc(ret_in, 1)

            def ret_decayed_scores(h):
                dve.wait_ge(ret_scored, cnt.next(ret_scored))
                V.tensor_tensor(ret_p[h % 2][:].rearrange("p (t q) -> p t q", q=P), bank[4][:].rearrange("p (t q) -> p t q", q=P),
                                spread(decay[:, 2, h], 1, [P, RCH, P]), ALU.mult).then_inc(ret_scores, 1)

            def ret_state(h):
                whole = float((1.0 - 2.0 ** (-5.0 - h)) ** P)
                dve.wait_ge(ret_kv, cnt.next(ret_kv))
                r = rstate[:, h % 2]
                V.tensor_scalar(r[:, 0], bank[7][:, 0:P], 1.0, None, ALU.mult).then_inc(r_state, 1)
                cnt.expect(r_state)
                for t in (1, 2):
                    dve.wait_ge(r_state, cnt.now(r_state))
                    V.scalar_tensor_tensor(r[:, t], r[:, t - 1], whole, bank[7][:, t * P:(t + 1) * P], ALU.mult, ALU.add).then_inc(r_state, 1)
                    cnt.expect(r_state)

            def ret_gated(h):
                dve.wait_ge(ret_sq, cnt.next(ret_sq))
                if h == 0:
                    dve.wait_ge(gate_silu, cnt.upto(gate_silu, 1))
                dve.wait_ge(gate_silu, cnt.upto(gate_silu, h + 1))
                V.scalar_tensor_tensor(gr[:, h], bank[h % 2][:], col("ret_g", h), gr[:, h], ALU.mult, ALU.mult).then_inc(ret_o, 1)
                cnt.expect(ret_o)

            def pool_lower(g):
                dve.wait_ge(mixed_hi, cnt.next(mixed_hi))
                V.scalar_tensor_tensor(m_lo[:, g], bank[6][:], col("pool_scale", g), m_hi[:, g].bitcast(F32),
                                       ALU.mult, ALU.subtract).then_inc(mixed_lo, 1)

            def gate_input(n):
                for c in range(CPU):
                    dve.wait_ge(proj_ready, cnt.next(proj_ready))
                    V.tensor_tensor(gr[:, CPU * n + c], bank[2 + c][:], roots[:], ALU.mult).then_inc(gate_out, 1)

            ret_inputs(0)
            ret_inputs(1)
            split_lo(1)
            dve.wait_ge(pooled, 4)
            ret_decayed_scores(0)
            gate_input(0)
            ret_state(0)
            pool_lower(0)
            split_lo(0)
            ret_decayed_scores(1)
            ret_gated(0)
            pool_lower(1)
            ret_inputs(2)
            gate_input(1)
            ret_state(1)
            pool_lower(2)
            split_lo(1)
            ret_decayed_scores(2)
            ret_gated(1)
            pool_lower(3)
            ret_inputs(3)
            ret_state(2)
            ret_decayed_scores(3)
            ret_gated(2)
            ret_state(3)
            ret_gated(3)
            mean_square(6, HR * RCH, P)
            dve.wait_ge(root_done, cnt.next(root_done))
            for h in range(HR):
                diagonal(tmp[h], RCH, RCH * h)

            def head_lower(h):
                dve.wait_ge(mixed_hi, cnt.next(mixed_hi))
                V.tensor_tensor(m_lo[:, 4 + h], gr[:, h], m_hi[:, 4 + h].bitcast(F32), ALU.subtract).then_inc(mixed_lo, 1)

            dve.wait_ge(ret_o, cnt.now(ret_o))
            for h in range(HR):
                dve.wait_ge(roots_ready, cnt.next(roots_ready))
                V.tensor_tensor(gr[:, h], gr[:, h], bank[4 + h][:], ALU.mult).then_inc(scaled, 1)
                if h:
                    head_lower(h - 1)
            head_lower(HR - 1)
            V.memset(sq_sum[:], 0.0).then_inc(dve_step, 1)
            dve.wait_ge(dve_step, cnt.next(dve_step))
            for n in range(4):
                sum_pair((2 * (n % 2), 2 * (n % 2) + 1), (CPU * n, CPU * n + 1), False, True, n % 2, False)
                if n < 3:
                    split_lo(n % 2)
            for m in range(KD):
                x_lower(m, lambda m: col("ffn2_g", m))
            ffn(True, last_ffn=True)
            stats(6, tmp[3])
            for m in range(KD):
                V.scalar_tensor_tensor(y_ffn[:, m], xT[:, m], col("final_g", m), bank[6][:], ALU.mult, ALU.mult).then_inc(out_done, 1)


def _units(w):
    n = w.shape[1] // UC
    return w.reshape(KD, P, n, UC).transpose(2, 1, 0, 3).reshape(n, P, UNIT)


def _tiles(w):
    n = w.shape[1] // P
    return w.reshape(KD, P, n, P).transpose(2, 1, 0, 3).reshape(n, P, KD * P)


def _out_units(w):
    return w.reshape(KF, P, D // UC, UC).transpose(2, 1, 0, 3).reshape(D // UC, P, KF * UC)


def _fm(x):
    return x.T.reshape(KD, P, x.shape[0]).transpose(1, 0, 2)


def _cols(v):
    return v.reshape(-1, P).T


def _constants():
    f = np.float32
    j, i = np.arange(P)[:, None], np.arange(P)[None, :]
    same = j // CHUNK == i // CHUNK
    masks = np.stack([same & (j <= i), same & (j >= i)], 1).astype(f)
    reset = np.ones((P, T), f)
    reset[:, ::CHUNK] = 0
    inv_freq = (f(1) / (f(10000.0) ** (np.arange(0, P, 2, dtype=f) / f(P)))).astype(f)
    ang = (np.arange(T, dtype=f)[:, None] * inv_freq[None, :]).astype(f).T
    cos, sin = np.cos(ang), np.sin(ang)
    trig = np.stack([np.concatenate([cos, cos]), np.concatenate([sin, -sin])], 1).astype(f)
    lg = np.log1p(-np.exp2(-5.0 - np.arange(HR)))
    pos = np.arange(P)
    decay = np.zeros((P, 3, HR, P))
    for h in range(HR):
        decay[:, 0, h] = np.exp(lg[h] * (pos + 1))[None]
        decay[:, 1, h] = np.exp(lg[h] * (P - 1 - pos))[None] * P ** -0.5
        rel = pos[None, :] - pos[:, None]
        decay[:, 2, h] = np.where(rel >= 0, np.exp(lg[h] * np.maximum(rel, 0)), 0) * P ** -0.5
    pool_n = np.zeros((P, 4, 17))
    for g, w in enumerate(WINDOWS):
        pool_n[:, g, :16] = w / np.minimum(np.arange(1, 17), w)
        pool_n[:, g, 16] = 1 / w
    return {"masks": masks, "reset": reset, "trig": trig, "decay": decay.astype(f), "pool_n": pool_n.astype(f),
            "ident": np.eye(P, dtype=f)}


def kernel(x, c, ctx, c_ctx, mod_w, mod_b, norm_g, ffn_w_in, ffn_w_out, gla_w_in, gla_w_gate, gla_b_gate,
           gla_norm_g, gla_w_out, ffn1_norm_2, ffn1_w1_2, ffn1_w3_2, ffn1_w2_2, mix_norm_2, w_in_2, pool_w_2,
           pool_scale_2, ret_norm_2, w_out_2, ffn2_norm_2, ffn2_w1_2, ffn2_w3_2, ffn2_w2_2, final_norm_2, **_unused):
    import concourse.bacc as bacc
    from concourse.bass_utils import run_bass_kernel_spmd

    f = np.float32
    w = np.asarray(gla_w_in)[0]
    q, k, v, r, lr = np.split(w, [512, 1024, 2048, 3072], axis=1)
    gate = np.zeros((2 * RANK, 2, HG * DK), f)
    for z in range(2):
        gate[z * RANK:(z + 1) * RANK, z] = np.asarray(gla_w_gate)[0, z]
    gate = np.tile(gate.reshape(2 * RANK, D), (4, 1))
    rank = np.tile(lr, (1, 4)).reshape(KD, P, P).transpose(1, 0, 2).reshape(P, D)
    mod = np.asarray(mod_w)[0]
    c2 = np.stack([_cols(np.asarray(c)[0]), _cols(np.asarray(c_ctx))], 2).reshape(P, 2 * KD)

    def pairs(w1, w3):
        u = np.stack([_units(w1), _units(w3)], 1)
        return u.reshape(-1, P, UNIT)

    ffn_in = np.asarray(ffn_w_in)[0]
    wi = np.asarray(w_in_2)[0]
    u2, q2, k2, v2, g2 = np.split(wi, 5, axis=1)
    arrays = {
        "cols": np.concatenate([c2, _cols(np.asarray(mod_b)[0]), _cols(np.asarray(norm_g)[0]),
                                _cols(np.asarray(gla_b_gate)[0]), _cols(np.asarray(gla_norm_g)[0]),
                                _cols(np.asarray(ffn1_norm_2)[0]), _cols(np.asarray(mix_norm_2)[0]),
                                _cols(np.asarray(pool_scale_2)[0]), _cols(np.asarray(ret_norm_2)[0]),
                                _cols(np.asarray(ffn2_norm_2)[0]), _cols(np.asarray(final_norm_2))], 1),
        "x_fm": _fm(np.asarray(x)[0]), "ctx_fm": _fm(np.asarray(ctx)[0]),
        "mod01": _units(mod[:, :2 * D]), "mod25": _tiles(mod[:, 2 * D:]),
        "gla_in": np.concatenate([_units(k), _units(q), _units(v), _units(r)]),
        "rank_w": np.stack([rank, gate], 1),
        "gla_out": _units(np.asarray(gla_w_out)[0]),
        "ffn0_in": pairs(ffn_in[:, :F], ffn_in[:, F:]), "ffn0_out": _out_units(np.asarray(ffn_w_out)[0]),
        "ffn1_in": pairs(np.asarray(ffn1_w1_2)[0], np.asarray(ffn1_w3_2)[0]),
        "ffn1_out": _out_units(np.asarray(ffn1_w2_2)[0]),
        "mix_in": np.concatenate([_units(u2), _units(k2), _units(q2), _units(v2), _units(g2)]),
        "pool_w": np.asarray(pool_w_2)[0].transpose(1, 0, 2),
        "mix_out": _units(np.asarray(w_out_2)[0]),
        "ffn2_in": pairs(np.asarray(ffn2_w1_2)[0], np.asarray(ffn2_w3_2)[0]),
        "ffn2_out": _out_units(np.asarray(ffn2_w2_2)[0]),
        **_constants(),
    }
    nc = bacc.Bacc("TRN2", target_bir_lowering=False, num_devices=1)
    aps, inputs = {}, {}
    for name, value in arrays.items():
        value = np.ascontiguousarray(value)
        inputs[f"in_{name}"] = value
        aps[name] = nc.dram_tensor(f"in_{name}", value.shape, mybir.dt.from_np(value.dtype), kind="ExternalInput").ap()
    aps["out"] = nc.dram_tensor("out_fm", (P, KD, T), F32, kind="ExternalOutput").ap()
    build(nc, aps)
    got = run_bass_kernel_spmd(nc, [inputs], core_ids=[0]).results[0]["out_fm"]
    return np.ascontiguousarray(got.transpose(2, 1, 0).reshape(1, T, D))
```
